# Optimizing a Trainium2 kernel written in Bass

```python
import math
import jax, jax.numpy as jnp
from jax import lax
import numpy as np

D_MODEL = 1024
BATCH = 1
SEQ = 1024
DEPTH = 2

GRID_W = 64
CTX_LEN = 256
CONV_WIDTH = 3
D_CONV = 512
N_DIFF_HEADS = 4
DIFF_QK_DIM = 64
DIFF_V_DIM = 128
D_ATTN = N_DIFF_HEADS * DIFF_V_DIM
N_FOURIER_GROUPS = 8
FOURIER_GROUP = D_MODEL // N_FOURIER_GROUPS
D_FF = 4 * D_MODEL
Q_BLOCK = 128
ROPE_BASE = 10000.0
LN_EPS = 1e-6
SUBLN_EPS = 1e-5
DEEPNORM_ALPHA = (2.0 * DEPTH) ** 0.25
DEEPNORM_BETA = (8.0 * DEPTH) ** -0.25
N_EVEN = (DEPTH + 1) // 2
N_ODD = DEPTH // 2
COL_CONV = 3 * D_CONV
COL_Q = N_DIFF_HEADS * 2 * DIFF_QK_DIM
COL_K = N_DIFF_HEADS * 2 * DIFF_QK_DIM
COL_V = D_ATTN
Q0 = COL_CONV
K0 = Q0 + COL_Q
V0 = K0 + COL_K
D_IN = V0 + COL_V


def layer_norm(x):
    xf = x.astype(jnp.float32)
    mu = jnp.mean(xf, axis=-1, keepdims=True)
    var = jnp.mean(jnp.square(xf - mu), axis=-1, keepdims=True)
    return ((xf - mu) * lax.rsqrt(var + LN_EPS)).astype(x.dtype)

def layer_norm_affine(x, g, b):
    xf = x.astype(jnp.float32)
    mu = jnp.mean(xf, axis=-1, keepdims=True)
    var = jnp.mean(jnp.square(xf - mu), axis=-1, keepdims=True)
    y = (xf - mu) * lax.rsqrt(var + LN_EPS) * g.astype(jnp.float32) + b.astype(jnp.float32)
    return y.astype(x.dtype)

def modulation(cond, w, b):
    return jnp.split(jax.nn.silu(cond) @ w + b, 6, axis=-1)

def modulate(h, shift, scale):
    return layer_norm(h) * (1.0 + scale) + shift

def post_norm_residual(h, y, gate, g, b):
    return layer_norm_affine(DEEPNORM_ALPHA * h + gate * y, g, b)

def rope_1d(x, pos):
    half = x.shape[-1] // 2
    inv = ROPE_BASE ** (-jnp.arange(half, dtype=jnp.float32) / half)
    ang = pos.astype(jnp.float32)[:, None] * inv[None, :]
    cos = jnp.cos(ang)[:, None, None, :].astype(x.dtype)
    sin = jnp.sin(ang)[:, None, None, :].astype(x.dtype)
    x1, x2 = x[..., :half], x[..., half:]
    return jnp.concatenate([x1 * cos - x2 * sin, x1 * sin + x2 * cos], axis=-1)

def rope_2d(x, row, col):
    d = x.shape[-1] // 2
    return jnp.concatenate([rope_1d(x[..., :d], row), rope_1d(x[..., d:], col)], axis=-1)

def short_conv(u, w):
    n = u.shape[1]
    pad = CONV_WIDTH // 2
    up = jnp.pad(u, ((0, 0), (pad, pad), (0, 0)))
    return sum(up[:, t:t + n] * w[t] for t in range(CONV_WIDTH))

def conv_mixer(p, w):
    gb, gc, v = jnp.split(p, 3, axis=-1)
    return gb * short_conv(gc * v, w)

def heads_qk(p):
    return p.reshape(p.shape[0], p.shape[1], N_DIFF_HEADS, 2, DIFF_QK_DIM)

def heads_v(p):
    return p.reshape(p.shape[0], p.shape[1], N_DIFF_HEADS, DIFF_V_DIM)

def diff_attend(q, k, v, lam):
    s = jnp.einsum('bqhcd,bkhcd->bhcqk', q, k).astype(jnp.float32) * (DIFF_QK_DIM ** -0.5)
    p = jax.nn.softmax(s, axis=-1)
    pd = (p[:, :, 0] - lam * p[:, :, 1]).astype(v.dtype)
    return jnp.einsum('bhqk,bkhd->bqhd', pd, v)

def diff_attention_blocks(q, k, v, lam):
    b, n = q.shape[0], q.shape[1]
    nb = n // Q_BLOCK
    qb = q.reshape(b, nb, Q_BLOCK, N_DIFF_HEADS, 2, DIFF_QK_DIM).transpose(1, 0, 2, 3, 4, 5)
    out = lax.map(lambda blk: diff_attend(blk, k, v, lam), qb)
    return out.transpose(1, 0, 2, 3, 4).reshape(b, n, N_DIFF_HEADS, DIFF_V_DIM)

def sub_ln(o, g, lam_init):
    of = o.astype(jnp.float32)
    y = of * lax.rsqrt(jnp.mean(of * of, axis=-1, keepdims=True) + SUBLN_EPS)
    y = y * g.astype(jnp.float32) * (1.0 - lam_init)
    return y.reshape(o.shape[0], o.shape[1], D_ATTN).astype(o.dtype)

def fourier_mix(u):
    b, n, _ = u.shape
    ug = u.astype(jnp.float32).reshape(b, n, N_FOURIER_GROUPS, FOURIER_GROUP)
    f = jnp.fft.fft2(ug, axes=(1, 3), norm='ortho').real
    return f.reshape(b, n, D_MODEL).astype(u.dtype)

def sq_relu_mlp(u, w1, w2):
    return jnp.square(jax.nn.relu(u @ w1)) @ w2

def first_inputs(seed: int = 0) -> dict:
    key = jax.random.key(seed)
    ks = jax.random.split(key, 16)
    f32 = jnp.float32

    def nrm(k, shape, s):
        return s * jax.random.normal(k, shape, f32)

    return {
        'x': nrm(ks[0], (BATCH, SEQ, D_MODEL), 1.0),
        'c': nrm(ks[1], (BATCH, D_MODEL), 1.0),
        'ctx': nrm(ks[2], (BATCH, CTX_LEN, D_MODEL), 1.0),
        'c_ctx': nrm(ks[3], (D_MODEL,), 1.0),
        'ada_w': nrm(ks[4], (DEPTH, D_MODEL, 6 * D_MODEL), 0.5 * D_MODEL ** -0.5),
        'ada_b': nrm(ks[5], (DEPTH, 6 * D_MODEL), 0.01),
        'ln_g': 1.0 + nrm(ks[6], (DEPTH, 2, D_MODEL), 0.05),
        'ln_b': nrm(ks[7], (DEPTH, 2, D_MODEL), 0.02),
        'mlp_w1': nrm(ks[8], (DEPTH, D_MODEL, D_FF), D_MODEL ** -0.5),
        'mlp_w2': nrm(ks[9], (DEPTH, D_FF, D_MODEL), DEEPNORM_BETA * D_FF ** -0.5),
        'w_in': nrm(ks[10], (N_EVEN, D_MODEL, D_IN), D_MODEL ** -0.5),
        'conv_w': nrm(ks[11], (N_EVEN, CONV_WIDTH, D_CONV), CONV_WIDTH ** -0.5),
        'lambda_qk': nrm(ks[12], (N_EVEN, 4, DIFF_QK_DIM), 0.1),
        'subln_g': 1.0 + nrm(ks[13], (N_EVEN, DIFF_V_DIM), 0.05),
        'w_out_mix': nrm(ks[14], (N_EVEN, D_CONV + D_ATTN, D_MODEL), DEEPNORM_BETA * (D_CONV + D_ATTN) ** -0.5),
        'w_out_fourier': nrm(ks[15], (N_ODD, D_MODEL, D_MODEL), DEEPNORM_BETA * D_MODEL ** -0.5),
    }

def first_block(x, c, ctx, c_ctx, ada_w, ada_b, ln_g, ln_b, mlp_w1, mlp_w2, w_in, conv_w, lambda_qk, subln_g, w_out_mix, w_out_fourier):
    n = x.shape[1]
    rows = n // GRID_W
    row = jnp.repeat(jnp.arange(rows, dtype=jnp.int32), GRID_W)
    col = jnp.tile(jnp.arange(GRID_W, dtype=jnp.int32), rows)
    last_attn = 2 * ((DEPTH - 1) // 2)
    cond_lat = c[:, None, :]
    cond_ctx = c_ctx[None, None, :]
    h, hc = x, ctx
    for i in range(DEPTH):
        j = i // 2
        update_ctx = i < last_attn
        sh1, sc1, g1, sh2, sc2, g2 = modulation(cond_lat, ada_w[i], ada_b[i])
        u = modulate(h, sh1, sc1)
        if update_ctx or i == last_attn:
            mc = modulation(cond_ctx, ada_w[i], ada_b[i])
            uc = modulate(hc, mc[0], mc[1])
        if i % 2 == 0:
            lam_init = 0.8 - 0.6 * math.exp(-0.3 * i)
            lq = lambda_qk[j].astype(jnp.float32)
            lam = jnp.exp(jnp.sum(lq[0] * lq[1])) - jnp.exp(jnp.sum(lq[2] * lq[3])) + lam_init
            p = u @ w_in[j]
            q = rope_2d(heads_qk(p[..., Q0:K0]), row, col)
            k = rope_2d(heads_qk(p[..., K0:V0]), row, col)
            v = heads_v(p[..., V0:])
            if update_ctx:
                pc = uc @ w_in[j]
                kvc = pc[..., K0:]
            else:
                kvc = uc @ w_in[j][:, K0:]
            kc = heads_qk(kvc[..., :COL_K])
            vc = heads_v(kvc[..., COL_K:])
            k_all = jnp.concatenate([k, kc], axis=1)
            v_all = jnp.concatenate([v, vc], axis=1)
            o = diff_attention_blocks(q, k_all, v_all, lam)
            y = jnp.concatenate([conv_mixer(p[..., :COL_CONV], conv_w[j]), sub_ln(o, subln_g[j], lam_init)], axis=-1) @ w_out_mix[j]
            if update_ctx:
                oc = diff_attend(heads_qk(pc[..., Q0:K0]), kc, vc, lam)
                yc = jnp.concatenate([conv_mixer(pc[..., :COL_CONV], conv_w[j]), sub_ln(oc, subln_g[j], lam_init)], axis=-1) @ w_out_mix[j]
        else:
            y = fourier_mix(u) @ w_out_fourier[j]
            if update_ctx:
                yc = fourier_mix(uc) @ w_out_fourier[j]
        h = post_norm_residual(h, y, g1, ln_g[i, 0], ln_b[i, 0])
        h = post_norm_residual(h, sq_relu_mlp(modulate(h, sh2, sc2), mlp_w1[i], mlp_w2[i]), g2, ln_g[i, 1], ln_b[i, 1])
        if update_ctx:
            hc = post_norm_residual(hc, yc, mc[2], ln_g[i, 0], ln_b[i, 0])
            hc = post_norm_residual(hc, sq_relu_mlp(modulate(hc, mc[3], mc[4]), mlp_w1[i], mlp_w2[i]), mc[5], ln_g[i, 1], ln_b[i, 1])
    return h


DEPTH_2 = 1

N_META = 16
D_MIX = D_MODEL
D_POOL = D_MIX // 4
POOL_WINDOWS = (2, 4, 8, 16)
POOL_GROUPS = len(POOL_WINDOWS)
POOL_GW = D_POOL // POOL_GROUPS
D_CONV_2 = D_MIX // 4
CONV_K = 31
D_RNN = D_MIX - D_POOL - D_CONV_2
RG_HEADS = 8
RG_HD = D_RNN // RG_HEADS
RG_CONV_K = 4
RG_C = 8.0
D_IN_2 = D_POOL + 2 * D_CONV_2 + 2 * D_RNN
D_FF_2 = 4 * D_MODEL
EPS = 1e-6


def _rmsnorm(x, g):
    xf = x.astype(jnp.float32)
    y = xf * lax.rsqrt(jnp.mean(xf * xf, axis=-1, keepdims=True) + EPS)
    return y.astype(x.dtype) * g

def _layernorm(x, g, b):
    xf = x.astype(jnp.float32)
    mu = jnp.mean(xf, axis=-1, keepdims=True)
    var = jnp.mean(jnp.square(xf - mu), axis=-1, keepdims=True)
    return ((xf - mu) * lax.rsqrt(var + EPS)).astype(x.dtype) * g + b

def _causal_depthwise_conv(x, w, b):
    K, C = w.shape
    y = lax.conv_general_dilated(
        x, w[:, None, :], window_strides=(1,), padding=[(K - 1, 0)],
        dimension_numbers=('NWC', 'WIO', 'NWC'), feature_group_count=C)
    return y + b

def _pool_mixer(u, w_grp, scale):
    B_, T, _ = u.shape
    uf = u.astype(jnp.float32)
    cs = jnp.cumsum(uf, axis=1)
    pos = jnp.arange(1, T + 1, dtype=jnp.int32)
    outs = []
    for g, w in enumerate(POOL_WINDOWS):
        sl = slice(g * POOL_GW, (g + 1) * POOL_GW)
        c = cs[..., sl]
        prev = jnp.pad(c, ((0, 0), (w, 0), (0, 0)))[:, :T]
        cnt = jnp.minimum(pos, w).astype(jnp.float32)[None, :, None]
        outs.append((c - prev) / cnt - uf[..., sl])
    pooled = jnp.stack(outs, axis=2).astype(u.dtype)
    mixed = jnp.einsum('btgc,gcd->btgd', pooled, w_grp).reshape(B_, T, D_POOL)
    return mixed * scale

def _conformer_conv(v, gt, w_dw, b_dw, ln_g, ln_b, w_pw):
    u = v * jax.nn.sigmoid(gt)
    u = _causal_depthwise_conv(u, w_dw, b_dw)
    u = jax.nn.silu(_layernorm(u, ln_g, ln_b))
    return u @ w_pw

def _linear_scan(a, b):
    def comb(l, r):
        return (l[0] * r[0], r[0] * l[1] + r[1])
    _, h = lax.associative_scan(comb, (a, b), axis=1)
    return h

def _rglru_branch(gate_in, x_in, conv_w, conv_b, w_a, b_a, w_x, b_x, lam):
    B_, T, _ = x_in.shape
    f32 = jnp.float32
    xc = _causal_depthwise_conv(x_in, conv_w, conv_b)
    xh = xc.reshape(B_, T, RG_HEADS, RG_HD)
    r = jax.nn.sigmoid((jnp.einsum('bthc,hcd->bthd', xh, w_a).reshape(B_, T, D_RNN) + b_a).astype(f32))
    i = jax.nn.sigmoid((jnp.einsum('bthc,hcd->bthd', xh, w_x).reshape(B_, T, D_RNN) + b_x).astype(f32))
    log_a = -RG_C * r * jax.nn.softplus(-lam.astype(f32))
    a = jnp.exp(log_a)
    mult = jnp.sqrt(-jnp.expm1(2.0 * log_a))
    h = _linear_scan(a, mult * (i * xc.astype(f32)))
    return (jax.nn.gelu(gate_in.astype(f32)) * h).astype(x_in.dtype)

def second_inputs(seed: int = 0) -> dict:
    key = jax.random.key(seed)
    ks = jax.random.split(key, 24)
    f32 = jnp.float32
    L = DEPTH_2

    def nrm(k, shape, scale):
        return jax.random.normal(k, shape, f32) * scale

    u = jax.random.uniform(ks[15], (L, D_RNN), f32, 0.9, 0.999)
    a0 = u ** (1.0 / RG_C)
    rg_lambda = jnp.log(a0) - jnp.log1p(-a0)
    return {
        "x": nrm(ks[0], (BATCH, SEQ, D_MODEL), 1.0),
        "meta_tokens": nrm(ks[1], (N_META, D_MODEL), 1.0),
        "mix_norm_g": 1.0 + nrm(ks[2], (L, D_MODEL), 0.05),
        "w_in": nrm(ks[3], (L, D_MODEL, D_IN_2), D_MODEL ** -0.5),
        "pool_w": nrm(ks[4], (L, POOL_GROUPS, POOL_GW, POOL_GW), POOL_GW ** -0.5),
        "pool_scale": 1.0 + nrm(ks[5], (L, D_POOL), 0.1),
        "convb_dw_w": nrm(ks[6], (L, CONV_K, D_CONV_2), CONV_K ** -0.5),
        "convb_dw_b": nrm(ks[7], (L, D_CONV_2), 0.02),
        "convb_ln_g": 1.0 + nrm(ks[8], (L, D_CONV_2), 0.05),
        "convb_ln_b": nrm(ks[9], (L, D_CONV_2), 0.02),
        "convb_pw_w": nrm(ks[10], (L, D_CONV_2, D_CONV_2), D_CONV_2 ** -0.5),
        "rg_conv_w": nrm(ks[11], (L, RG_CONV_K, D_RNN), RG_CONV_K ** -0.5),
        "rg_conv_b": nrm(ks[12], (L, D_RNN), 0.02),
        "rg_w_a": nrm(ks[13], (L, RG_HEADS, RG_HD, RG_HD), RG_HD ** -0.5),
        "rg_b_a": nrm(ks[14], (L, D_RNN), 0.02),
        "rg_w_x": nrm(ks[16], (L, RG_HEADS, RG_HD, RG_HD), RG_HD ** -0.5),
        "rg_b_x": nrm(ks[17], (L, D_RNN), 0.02),
        "rg_lambda": rg_lambda,
        "w_out": nrm(ks[18], (L, D_MIX, D_MODEL), D_MIX ** -0.5),
        "mlp_norm_g": 1.0 + nrm(ks[19], (L, D_MODEL), 0.05),
        "w_up": nrm(ks[20], (L, D_MODEL, D_FF_2), D_MODEL ** -0.5),
        "w_down": nrm(ks[21], (L, D_FF_2, D_MODEL), D_FF_2 ** -0.5),
        "final_norm_g": 1.0 + nrm(ks[22], (D_MODEL,), 0.05),
    }

def second_block(x, meta_tokens, mix_norm_g, w_in, pool_w, pool_scale, convb_dw_w, convb_dw_b,
              convb_ln_g, convb_ln_b, convb_pw_w, rg_conv_w, rg_conv_b, rg_w_a, rg_b_a,
              rg_w_x, rg_b_x, rg_lambda, w_out, mlp_norm_g, w_up, w_down, final_norm_g):
    B_ = x.shape[0]
    meta = jnp.broadcast_to(meta_tokens[None].astype(x.dtype), (B_, N_META, D_MODEL))
    h = jnp.concatenate([meta, x], axis=1)
    splits = [D_POOL, D_POOL + D_CONV_2, D_POOL + 2 * D_CONV_2, D_POOL + 2 * D_CONV_2 + D_RNN]
    for l in range(DEPTH_2):
        u = _rmsnorm(h, mix_norm_g[l])
        p = u @ w_in[l]
        p_pool, p_bval, p_bgate, p_cgate, p_cx = jnp.split(p, splits, axis=-1)
        y_a = _pool_mixer(p_pool, pool_w[l], pool_scale[l])
        y_b = _conformer_conv(p_bval, p_bgate, convb_dw_w[l], convb_dw_b[l],
                              convb_ln_g[l], convb_ln_b[l], convb_pw_w[l])
        y_c = _rglru_branch(p_cgate, p_cx, rg_conv_w[l], rg_conv_b[l], rg_w_a[l], rg_b_a[l],
                            rg_w_x[l], rg_b_x[l], rg_lambda[l])
        y = jnp.concatenate([y_a, y_b, y_c], axis=-1)
        h = h + y @ w_out[l]
        u = _rmsnorm(h, mlp_norm_g[l])
        h = h + jnp.square(jax.nn.relu(u @ w_up[l])) @ w_down[l]
    h = _rmsnorm(h, final_norm_g)
    return h[:, N_META:]


def setup_inputs(seed=0):
    out = dict(first_inputs(seed))
    for name, value in second_inputs(seed + 1).items():
        if name != "x":
            out[name + "_2"] = value
    return out


def reference(
    x, c, ctx, c_ctx, ada_w, ada_b, ln_g, ln_b, mlp_w1, mlp_w2, w_in, conv_w, lambda_qk,
    subln_g, w_out_mix, w_out_fourier, meta_tokens_2, mix_norm_g_2, w_in_2, pool_w_2,
    pool_scale_2, convb_dw_w_2, convb_dw_b_2, convb_ln_g_2, convb_ln_b_2, convb_pw_w_2,
    rg_conv_w_2, rg_conv_b_2, rg_w_a_2, rg_b_a_2, rg_w_x_2, rg_b_x_2, rg_lambda_2, w_out_2,
    mlp_norm_g_2, w_up_2, w_down_2, final_norm_g_2,
):
    x = first_block(
        x, c, ctx, c_ctx, ada_w, ada_b, ln_g, ln_b, mlp_w1, mlp_w2, w_in, conv_w, lambda_qk,
        subln_g, w_out_mix, w_out_fourier,
    )
    return second_block(
        x, meta_tokens_2, mix_norm_g_2, w_in_2, pool_w_2, pool_scale_2, convb_dw_w_2,
        convb_dw_b_2, convb_ln_g_2, convb_ln_b_2, convb_pw_w_2, rg_conv_w_2, rg_conv_b_2,
        rg_w_a_2, rg_b_a_2, rg_w_x_2, rg_b_x_2, rg_lambda_2, w_out_2, mlp_norm_g_2, w_up_2,
        w_down_2, final_norm_g_2,
    )


_drawn_inputs = setup_inputs


def setup_inputs(seed=0):
    import zlib

    import numpy as np

    out = dict(_drawn_inputs(seed))
    spreads = {}
    factors = {'ctx': 4.651,
     'ada_b': 4.2,
     'lambda_qk': 8.0,
     'subln_g': 8.0,
     'convb_dw_b_2': 6.079,
     'convb_ln_g_2': 3.813,
     'convb_ln_b_2': 8.0,
     'rg_b_a_2': 31.682,
     'rg_b_x_2': 8.0,
     'pool_scale_2': 3.05}
    for name, (base, spread) in spreads.items():
        noise = np.random.default_rng([zlib.crc32(name.encode()), seed]).standard_normal(out[name].shape)
        drawn = base * np.exp(spread * noise) if base else spread * noise
        out[name] = __import__('jax').numpy.asarray(drawn.astype(out[name].dtype))
    for name, factor in factors.items():
        out[name] = (out[name] * factor).astype(out[name].dtype)
    return out
```

```python
import math
from contextlib import ExitStack

import numpy as np

import concourse.bass as bass
from concourse import mybir

P = 128
F32 = mybir.dt.float32
F32R = mybir.dt.float32r
ALU = mybir.AluOpType
ACT = mybir.ActivationFunctionType
AX_X = mybir.AxisListType.X

T = 1024
D = 1024
TT = T // P
KT = D // P
CH = 512
NCH = T // CH
TPC = CH // P
CTX = 256
CTT = CTX // P
D_FF = 4096
FB = 4
D_CONV = 512
Q0, K0, V0 = 3 * D_CONV, 3 * D_CONV + 512, 3 * D_CONV + 1024
HEADS = 4
QK = 64
KEYS = T + CTX
DEPTH = 2
ALPHA = (2.0 * DEPTH) ** 0.25
LAM_INIT = 0.2
META = 16
TM = T + META
CONV_K = 31
RG_K = 4
RG_C = 8.0
UNIT = 1024
N_RAW = 3
N_SPLIT = 5
N_TEMP = 5

VECTORS = [("c", 8), ("c_ctx", 8), ("conv_w", 12), ("subln_g", 1), ("mix_norm_g_2", 8), ("mlp_norm_g_2", 8),
           ("pool_scale_2", 2), ("convb_dw_b_2", 2), ("convb_ln_g_2", 2), ("convb_ln_b_2", 2),
           ("rg_conv_w_2", 16), ("rg_conv_b_2", 4), ("rg_b_a_2", 4), ("rg_b_x_2", 4), ("rg_lambda_2", 4),
           ("ada_b", 96), ("convb_dw_w_2", 62)]


def vector_columns():
    start, at, groups = {}, 0, []
    group, used = [], 0
    for name, rows in VECTORS:
        if used + rows > P:
            groups.append((group, used))
            at, group, used = at + used, [], 0
        start[name] = at + used
        group.append((name, rows, used))
        used += rows
    groups.append((group, used))
    return start, groups, at + used


class Later:

    def matmul(self, *operands, **options):
        self.step = lambda e: e.matmul(*operands, **options)

    def transpose(self, *operands, **options):
        self.step = lambda e: e.transpose(*operands, **options)

    def memset(self, *operands, **options):
        self.step = lambda e: e.memset(*operands, **options)

    def affine_select(self, *operands, **options):
        self.step = lambda e: e.affine_select(*operands, **options)

    def copy(self, *operands, **options):
        self.step = lambda e: e.copy(*operands, **options)

    def activation(self, *operands, **options):
        self.step = lambda e: e.activation(*operands, **options)

    def tensor_tensor(self, *operands, **options):
        self.step = lambda e: e.tensor_tensor(*operands, **options)

    def tensor_scalar(self, *operands, **options):
        self.step = lambda e: e.tensor_scalar(*operands, **options)

    def scalar_tensor_tensor(self, *operands, **options):
        self.step = lambda e: e.scalar_tensor_tensor(*operands, **options)

    def tensor_tensor_scan(self, *operands, **options):
        self.step = lambda e: e.tensor_tensor_scan(*operands, **options)

    def tensor_reduce(self, *operands, **options):
        self.step = lambda e: e.tensor_reduce(*operands, **options)

    def tensor_copy(self, *operands, **options):
        self.step = lambda e: e.tensor_copy(*operands, **options)

    def bn_stats(self, *operands, **options):
        self.step = lambda e: e.bn_stats(*operands, **options)

    def bn_aggr(self, *operands, **options):
        self.step = lambda e: e.bn_aggr(*operands, **options)

    def reciprocal(self, *operands, **options):
        self.step = lambda e: e.reciprocal(*operands, **options)

    def stream_shuffle(self, *operands, **options):
        self.step = lambda e: e.stream_shuffle(*operands, **options)


def later(emit):
    kept = Later()
    emit(kept)
    return kept.step


class Queue:

    def __init__(self, program, name):
        self.program, self.name = program, name
        self.steps, self.seen = [], {}
        self.stage, self.count = None, 0

    def begin(self, stage):
        self.stage, self.count = self.program.semaphore(f"{self.name}_{stage}"), 0

    def wait(self, *marks):
        for mark in marks:
            if mark is None:
                continue
            if isinstance(mark, list):
                self.wait(*mark)
                continue
            sem, value = mark
            if self.seen.get(id(sem), 0) < value:
                self.seen[id(sem)] = value
                self.steps.append(lambda e, s=sem, v=value: e.wait_ge(s, v))

    def do(self, emit):
        self.count += 1
        step = later(emit)
        self.steps.append(lambda e, s=self.stage: step(e).then_inc(s, 1))
        return (self.stage, self.count)

    def quiet(self, emit):
        self.steps.append(later(emit))

    def run(self, engine):
        for step in self.steps:
            step(engine)


class Unit:

    def __init__(self, pieces, after=None, gate=None, whole=False, zero=False, into=None, size=UNIT):
        self.pieces, self.after, self.gate, self.whole = pieces, after, gate, whole
        self.zero, self.into, self.size = zero, into, size
        self.hi = self.lo = self.raw = self.ready = None


class Program:
    def __init__(self, nc, a, out):
        self.nc, self.a, self.out = nc, a, out
        self.stack = ExitStack()
        self.pe, self.act, self.dve = Queue(self, "pe"), Queue(self, "act"), Queue(self, "dve")
        self.pool, self.sp = Queue(self, "pool"), Queue(self, "sp")

    def semaphore(self, name):
        return self.stack.enter_context(self.nc.semaphore(name))

    def sbuf(self, name, shape, dtype=F32, stack=None):
        return (stack or self.stack).enter_context(self.nc.sbuf_tensor(name, shape, dtype))

    def scratch(self, name, shape):
        return self.nc.dram_tensor(name, shape, F32, kind="Internal").ap()

    def allocate(self):
        sb = self.sbuf
        self.col_at, self.col_groups, n_cols = vector_columns()
        self.ident = sb("ident", [P, P])
        self.ones = sb("ones", [P, P])
        self.cols = sb("cols", [P, n_cols])
        self.cc = sb("cc", [P, KT, 2])
        self.mod = sb("mod", [P, DEPTH, 48])
        self.mod_ctx = sb("mod_ctx", [P, 16])
        self.eps = sb("eps", [P, 3])
        self.small = sb("small", [P, 16, 16])
        self.lam = sb("lam", [P, 8])
        self.softplus = sb("softplus", [P, 8, 4])
        self.sumsq = sb("sumsq", [P, TT, HEADS])
        self.U_meta_hi = sb("U_meta_hi", [P, KT, META], F32R)
        self.U_meta_lo = sb("U_meta_lo", [P, KT, META], F32R)
        self.temp = [sb(f"temp{i}", [P, CH]) for i in range(N_TEMP)]
        self.temp_free = [[] for _ in range(N_TEMP)]
        self.temp_next = 0
        self.raw = [sb(f"raw{i}", [P, UNIT]) for i in range(N_RAW)]
        self.split_hi = [sb(f"split_hi{i}", [P, UNIT], F32R) for i in range(N_SPLIT)]
        self.split_lo = [sb(f"split_lo{i}", [P, UNIT], F32R) for i in range(N_SPLIT)]

        with ExitStack() as s:
            sb("U_lo_first", [P, KT, CH], stack=s)
            self.XH = [None, None]
            self.XH[0] = sb("XH0", [P, TPC, D], stack=s)
            sb("U_hi_first", [P, KT, CH], stack=s)
            self.XH[1] = sb("XH1", [P, TPC, D], stack=s)
        self.U_lo = sb("U_lo", [P, NCH, KT, CH], F32R)
        self.U_hi = sb("U_hi", [P, NCH, KT, CH], F32R)

        with ExitStack() as s:
            self.prob = [[sb(f"prob{i}{c}", [P, KEYS], stack=s) for c in range(2)] for i in range(2)]
            self.PT_hi = sb("PT_hi", [P, KEYS // P, P], F32R, stack=s)
            self.PT_lo = sb("PT_lo", [P, KEYS // P, P], F32R, stack=s)
        with ExitStack() as s:
            self.conv_gc = sb("conv_gc", [P, T], stack=s)
            self.gv = sb("conv_gv", [P, T + 2], stack=s)
            self.cv = sb("conv_cv", [P, T], stack=s)
            self.cv2 = sb("conv_cv2", [P, T], stack=s)
        self.H = sb("H", [P, TT, D])

        with ExitStack() as s:
            self.Uc_hi = sb("Uc_hi", [P, KT, CTX], F32R, stack=s)
            self.Uc_lo = sb("Uc_lo", [P, KT, CTX], F32R, stack=s)
            self.rope_cos = sb("rope_cos", [P, T], stack=s)
            self.rope_sin = sb("rope_sin", [P, T], stack=s)
            self.stage_buf = [sb(f"stage{i}", [P, CH], stack=s) for i in range(4)]
        with ExitStack() as s:
            self.XHc = sb("XHc", [P, CTT, D], stack=s)
            self.ctx_raw = sb("ctx_raw", [P, CTT, D], stack=s)
        with ExitStack() as s:
            self.O = sb("O", [P, TT, HEADS * P], stack=s)
            self.conv_in = sb("conv_in", [P, 4, T], stack=s)
        with ExitStack() as s:
            self.XHall = sb("XHall", [P, TT, D], stack=s)
        with ExitStack() as s:
            self.table_hi = sb("table_hi", [P, UNIT], F32R, stack=s)
            self.table_lo = sb("table_lo", [P, UNIT], F32R, stack=s)
            self.PQ_hi = sb("PQ_hi", [P, 8, 2 * P], F32R, stack=s)
            self.PQ_lo = sb("PQ_lo", [P, 8, 2 * P], F32R, stack=s)
            self.chan_raw = sb("chan_raw", [P, 2 * P], stack=s)
            self.chan_hi = sb("chan_hi", [P, 2 * P], F32R, stack=s)
            self.chan_lo = sb("chan_lo", [P, 2 * P], F32R, stack=s)
        with ExitStack() as s:
            self.gated = [sb(f"gated{i}", [P, TM + 14], stack=s) for i in range(2)]
            self.dw = [sb(f"dw{i}", [P, T], stack=s) for i in range(2)]
            self.xc = [sb(f"xc{i}", [P, TM], stack=s) for i in range(4)]
            self.cx = sb("cx", [P, TM + 3], stack=s)
            self.work = sb("work", [P, TM], stack=s)
        with ExitStack() as s:
            self.meta_raw = sb("meta_raw", [META, D], stack=s)
            self.meta_hat = sb("meta_hat", [META, D], stack=s)
        self.A_hi = sb("A_hi", [P, FB, T], F32R)
        self.A_lo = sb("A_lo", [P, FB, T], F32R)
        self.row_gate = sb("row_gate", [P, D])
        self.row_g = sb("row_g", [P, D])
        self.row_b = sb("row_b", [P, D])

        self.psum = self.stack.enter_context(self.nc.psum_tensor("psum", [P, 8, CH], F32))
        self.bank_free = [[] for _ in range(8)]
        self.bank_next = 0
        self.small_next = 0
        self.d_q = self.scratch("d_q", (HEADS, P, T))
        self.d_k = self.scratch("d_k", (HEADS, P, T))
        self.d_kc = self.scratch("d_kc", (HEADS, P, CTX))
        self.d_v = self.scratch("d_v", (KEYS, HEADS * P))
        self.d_conv = self.scratch("d_conv", (4, P, T))
        self.d_pool = self.scratch("d_pool", (2, P, TM))
        self.d_gelu = self.scratch("d_gelu", (4, P, TM))
        self.s_raw = [[self.semaphore(f"s_raw{i}"), 0] for i in range(N_RAW)]
        self.s_store = [[self.semaphore(f"s_store{i}"), 0] for i in range(4)]

    def take_bank(self, n=None):
        if n is None:
            n = self.bank_next
            self.bank_next = (n + 1) % 8
        self.pe.wait(*self.bank_free[n])
        self.bank_free[n] = []
        return n

    def take_temp(self, *queues):
        n = self.temp_next
        self.temp_next = (n + 1) % N_TEMP
        for q in queues:
            q.wait(*self.temp_free[n])
        self.temp_free[n] = []
        return n

    def take_small(self):
        n = self.small_next
        self.small_next = (n + 1) % 16
        return self.small[:, n, :]

    def columns(self, name, i=0, n=1):
        at = self.col_at[name] + i
        return self.cols[:, at:at + n]

    def dma(self, queue, sem, dst, src):
        sem[1] += 16
        queue.steps.append(lambda e, s=sem[0]: e.dma_start(dst, src).then_inc(s, 16))
        return (sem[0], sem[1])

    def load(self, name, dst, src, *after):
        self.pool.wait(*after)
        return self.dma(self.pool, [self.semaphore("s_" + name), 0], dst, src)

    def weights_begin(self, units):
        self.units = units
        self.raw_free = [[] for _ in range(N_RAW)]
        self.split_free = [[] for _ in range(N_SPLIT)]
        self.raw_marks = {}
        self.n_rows = 0
        self.n_load = self.n_split = self.n_take = self.n_slot = 0

    def pump(self):
        moved = True
        while moved:
            moved = False
            if self.n_load < len(self.units):
                u, slot = self.units[self.n_load], self.n_load % N_RAW
                after = u.after() if u.after else []
                if self.raw_free[slot] is not None and after is not None:
                    self.sp.wait(*self.raw_free[slot], *after)
                    self.raw_free[slot] = None
                    u.raw = self.raw[slot]
                    if u.zero:
                        self.dve.wait(*self.zero_after(slot))
                        self.sp.wait(self.dve.do(lambda e, r=u.raw: e.memset(r[:], 0.0)))
                    for dst, src in u.pieces:
                        u.ready = self.dma(self.sp, self.s_raw[slot], dst(u.raw), src)
                    u.loaded_slot = slot
                    self.n_load += 1
                    moved = True
            if self.n_split < self.n_load:
                u = self.units[self.n_split]
                if u.whole:
                    self.n_split += 1
                    moved = True
                    continue
                gate = u.gate() if u.gate else ()
                if gate is None:
                    continue
                if u.into:
                    got = u.into()
                    if got is None:
                        continue
                    hi, lo, free = got
                else:
                    slot = self.n_slot % N_SPLIT
                    if self.split_free[slot] is None:
                        continue
                    free = self.split_free[slot]
                    hi, lo = self.split_hi[slot], self.split_lo[slot]
                    self.split_free[slot] = None
                    u.slot = slot
                    self.n_slot += 1
                n, raw = u.size, u.raw
                source = [u.ready]
                if gate:
                    row, made = gate
                    self.dve.wait(u.ready, made)
                    source = [self.dve.do(lambda e, r=raw, g=row: e.tensor_tensor(r[:], r[:], g[:], ALU.mult))]
                self.act.wait(*source, *free)
                m_hi = self.act.do(lambda e, h=hi, r=raw, n=n: e.copy(h[:, 0:n], r[:, 0:n]))
                self.dve.wait(*source, *free, m_hi)
                m_lo = self.dve.do(lambda e, h=hi, l=lo, r=raw, n=n: e.tensor_tensor(
                    l[:, 0:n], r[:, 0:n], h[:, 0:n].bitcast(F32), ALU.subtract))
                u.hi, u.lo, u.ready = hi, lo, [m_hi, m_lo]
                self.raw_marks[u.loaded_slot] = [m_hi, m_lo]
                self.raw_free[u.loaded_slot] = [m_hi, m_lo]
                self.n_split += 1
                moved = True

    def zero_after(self, slot):
        return self.raw_marks.get(slot, [])

    def take_unit(self):
        self.pump()
        u = self.units[self.n_take]
        assert u.raw is not None and (u.whole or u.hi is not None), self.n_take
        self.n_take += 1
        self.pe.wait(*(u.ready if isinstance(u.ready, list) else [u.ready]))
        return u

    def release(self, u, mark):
        if u.whole:
            self.raw_free[u.loaded_slot] = [mark]
            self.raw_marks[u.loaded_slot] = [mark]
        elif not u.into:
            self.split_free[u.slot] = [mark]
        self.pump()

    def passes(self, out, l_hi, l_lo, r_hi, r_lo, start, stop):
        pe = self.pe
        pe.quiet(lambda e: e.matmul(out, l_hi, r_hi, start=start, stop=False))
        pe.quiet(lambda e: e.matmul(out, l_hi, r_lo, start=False, stop=False))
        last = lambda e: e.matmul(out, l_lo, r_hi, start=False, stop=stop)
        if stop:
            return pe.do(last)
        pe.quiet(last)
        return None

    def split(self, src, hi, lo, ready, free=()):
        self.act.wait(*ready, *free)
        m_hi = self.act.do(lambda e: e.copy(hi, src))
        self.dve.wait(*ready, *free, m_hi)
        m_lo = self.dve.do(lambda e: e.tensor_tensor(lo, src, hi.bitcast(F32), ALU.subtract))
        return [m_hi, m_lo]

    def statistics(self, src, rows, width, ready, rms=False, eps=0):
        dve, act = self.dve, self.act
        s = self.take_small()
        dve.wait(*ready)
        n = (width + CH - 1) // CH
        for i in range(n):
            m = dve.do(lambda e, i=i: e.bn_stats(s[0:rows, 6 * i:6 * i + 6], src[:, i * CH:min(width, (i + 1) * CH)]))
        dve.wait(m)
        mean, var, std, scale = (s[0:rows, 12 + i:13 + i] for i in range(4))
        m = dve.do(lambda e: e.bn_aggr(s[0:rows, 12:14], s[0:rows, 0:6 * n]))
        if rms:
            dve.wait(m)
            m = dve.do(lambda e: e.scalar_tensor_tensor(var, mean, mean, var, ALU.mult, ALU.add))
        act.wait(m)
        m = act.do(lambda e: e.activation(std, var, ACT.Sqrt, bias=self.eps[0:rows, eps:eps + 1]))
        dve.wait(m)
        m = dve.do(lambda e: e.reciprocal(scale, std))
        if rms:
            return scale, self.eps[0:rows, 2:3], [m]
        dve.wait(m)
        m = dve.do(lambda e: e.scalar_tensor_tensor(std, mean, -1.0, scale, ALU.mult, ALU.mult))
        return scale, std, [m]

    def normalize(self, src, dst, rows, ready, free=(), rms=False):
        scale, bias, got = self.statistics(src, rows, D, ready, rms)
        self.act.wait(*got, *free)
        return self.act.do(lambda e: e.activation(dst, src, ACT.Identity, bias=bias, scale=scale))

    def transpose_chunk(self, c, XH, ready, scale, shift, u_free, fold=None):
        pe, act, dve = self.pe, self.act, self.dve
        pe.wait(*ready)
        banks, marks = [], []
        for k in range(KT):
            b = self.take_bank()
            for i in range(TPC):
                emit = lambda e, b=b, i=i, k=k: e.transpose(self.psum[:, b, i * P:(i + 1) * P],
                                                            XH[:, i, k * P:(k + 1) * P], self.ident[:])
                if i < TPC - 1:
                    pe.quiet(emit)
            marks.append(pe.do(emit))
            banks.append(b)
        out = []
        for k, b in enumerate(banks):
            done = marks[-1] if c == 1 else marks[k]
            t = self.take_temp(act)
            v = self.temp[t]
            hi, lo = self.U_hi[:, c, k, :], self.U_lo[:, c, k, :]
            act.wait(done, *u_free)
            m_v = act.do(lambda e, v=v, b=b, k=k: e.activation(v[:], self.psum[:, b, :], ACT.Identity,
                                                               bias=shift(k), scale=scale(k)))
            self.bank_free[b] = [m_v]
            m = self.split(v[:], hi, lo, [m_v], u_free)
            self.temp_free[t] = m
            out += m
        return out

    def ada(self, layer, first, n, with_ctx=False):
        pe, dve = self.pe, self.dve
        pe.wait(self.cc_ready)
        b = self.take_bank()
        w = 2 if with_ctx else 1
        for i in range(n):
            u = self.take_unit()
            W = u.raw[:].rearrange("p (k m) -> p k m", k=KT)
            for k in range(KT):
                emit = lambda e, W=W, k=k, i=i: e.matmul(self.psum[:, b, w * i:w * i + w], W[:, k, :],
                                                         self.cc[:, k, 0:w], start=(k == 0), stop=(k == KT - 1))
                if k < KT - 1:
                    pe.quiet(emit)
            mark = pe.do(emit)
            self.release(u, mark)
        bias = self.columns("ada_b", 48 * layer + first, n)
        got = self.psum[:, b, 0:w * n].rearrange("p (n w) -> p n w", w=w)
        dve.wait(mark, self.cols_ready)
        m = dve.do(lambda e: e.tensor_tensor(self.mod[:, layer, first:first + n], got[:, :, 0], bias, ALU.add))
        if with_ctx:
            m = dve.do(lambda e: e.tensor_tensor(self.mod_ctx[:, first:first + n], got[:, :, 1], bias, ALU.add))
        self.bank_free[b] = [m]
        for which in range(2):
            lo, hi = max(first, 24 * which + 8), min(first + n, 24 * which + 16)
            if lo < hi:
                dve.wait(m)
                s = self.mod[:, layer, lo:hi]
                m = dve.do(lambda e: e.tensor_scalar(s, s, 1.0, None, ALU.add))
                if with_ctx:
                    s2 = self.mod_ctx[:, lo:hi]
                    m = dve.do(lambda e: e.tensor_scalar(s2, s2, 1.0, None, ALU.add))
        for part in range(first // 8, (first + n + 7) // 8):
            self.mod_ready[(layer, part)] = m
        return m

    def gate_row(self, layer, which):
        pe, act, dve = self.pe, self.act, self.dve
        col = 24 * which + 16
        ready = self.mod_ready[(layer, col // 8)]
        banks = [self.take_bank(), self.take_bank()]
        for k in range(KT):
            t = self.take_temp(dve)
            v = self.temp[t]
            dve.wait(ready)
            m = dve.do(lambda e, v=v, k=k: e.tensor_scalar(v[:, 0:P], self.ones[:],
                                                           self.mod[:, layer, col + k:col + k + 1], None, ALU.mult))
            pe.wait(m)
            m = pe.do(lambda e, v=v, k=k: e.matmul(self.psum[:, banks[k // 4], (k % 4) * P:(k % 4 + 1) * P],
                                                   v[:, 0:P], self.ident[:], start=True, stop=True))
            self.temp_free[t] = [m]
        act.wait(m, *self.gate_used)
        for i in range(2):
            m = act.do(lambda e, i=i: e.copy(self.row_gate[:, i * CH:(i + 1) * CH], self.psum[:, banks[i], :]))
            self.bank_free[banks[i]] = [m]
        self.gate_ready[(layer, which)] = m

    def up_group(self, n, chunk_ready, evacuate, before_chunk=None, chunk_major=False, extra=None):
        units = []
        order = [(i, c) for c in range(NCH) for i in range(n)] if chunk_major else \
                [(i, c) for i in range(n) for c in range(NCH)]
        for i, c in order:
            if before_chunk and chunk_major and i == 0:
                before_chunk(c)
            if i == len(units):
                units.append(self.take_unit())
            u = units[i]
            W_hi = u.hi[:].rearrange("p (k m) -> p k m", k=KT)
            W_lo = u.lo[:].rearrange("p (k m) -> p k m", k=KT)
            self.pe.wait(*chunk_ready(c))
            b = self.take_bank()
            for k in range(KT):
                mark = self.passes(self.psum[:, b, :], W_hi[:, k, :], W_lo[:, k, :], self.U_hi[:, c, k, :],
                                   self.U_lo[:, c, k, :], k == 0, k == KT - 1)
            self.u_read = mark
            evacuate(i, c, b, mark)
            if c == NCH - 1:
                if extra:
                    mark = extra(i, W_hi, W_lo)
                self.release(u, mark)

    def down_block(self, lhs, lhs_ready, alpha=1.0, after_tile=None, between=None):
        pe, dve = self.pe, self.dve
        units = [self.take_unit() for _ in range(FB)]
        for tt in range(TT):
            banks = [self.take_bank(), self.take_bank()]
            for j in range(FB):
                pe.wait(*lhs_ready(j, tt))
                l_hi, l_lo = lhs(j, tt)
                for half in range(2):
                    s = slice(half * CH, (half + 1) * CH)
                    mark = self.passes(self.psum[:, banks[half], :], l_hi, l_lo, units[j].hi[:, s], units[j].lo[:, s],
                                       j == 0, j == FB - 1)
                    if j == FB - 1:
                        dve.wait(mark, *self.h_ready[tt])
                        h = self.H[:, tt, s]
                        acc = self.psum[:, banks[half], :]
                        if alpha == 1.0:
                            m = dve.do(lambda e, h=h, acc=acc: e.tensor_tensor(h, h, acc, ALU.add))
                        else:
                            m = dve.do(lambda e, h=h, acc=acc: e.scalar_tensor_tensor(h, h, alpha, acc, ALU.mult, ALU.add))
                        self.bank_free[banks[half]] = [m]
            self.h_ready[tt] = [m]
            if tt == TT - 1:
                for u in units:
                    self.release(u, mark)
            if after_tile:
                after_tile(tt)
            if between:
                between(tt)
        return mark

    def mlp(self, name, chunk_ready, before_chunk, fill=None, after_tile=None, between=None, alpha=1.0):
        for q in (self.pe, self.act, self.dve):
            q.begin(name)
        ready = {}

        def evacuate(j, c, b, mark):
            act, dve = self.act, self.dve
            t1, t2 = self.take_temp(act), self.take_temp(dve)
            r, a = self.temp[t1], self.temp[t2]
            act.wait(mark)
            m_r = act.do(lambda e: e.activation(r[:], self.psum[:, b, :], ACT.Relu))
            self.bank_free[b] = [m_r]
            dve.wait(m_r)
            m_a = dve.do(lambda e: e.tensor_tensor(a[:], r[:], r[:], ALU.mult))
            self.temp_free[t1] = [m_a]
            s = slice(c * CH, (c + 1) * CH)
            m = self.split(a[:], self.A_hi[:, j, s], self.A_lo[:, j, s], [m_a], self.a_read)
            self.temp_free[t2] = m
            ready[(j, c)] = m

        blocks = D_FF // (P * FB)
        for blk in range(blocks):
            self.up_group(FB, chunk_ready, evacuate, before_chunk if blk == 0 else None, chunk_major=(blk == 0))
            if fill:
                fill(blk)
            last = blk == blocks - 1
            mark = self.down_block(
                lambda j, tt: (self.A_hi[:, j, tt * P:(tt + 1) * P], self.A_lo[:, j, tt * P:(tt + 1) * P]),
                lambda j, tt: ready[(j, tt // TPC)], alpha if blk == 0 else 1.0,
                after_tile if last else None, between if last else None)
            self.a_read = [mark]

    def u_lhs(self, first):
        return lambda j, tt: (self.U_hi[:, tt // TPC, first + j, (tt % TPC) * P:(tt % TPC + 1) * P],
                              self.U_lo[:, tt // TPC, first + j, (tt % TPC) * P:(tt % TPC + 1) * P])

    def boundary(self, post, rms, scale, shift, all_tiles=False):
        state = {"xh": [None] * TT, "chunk": [[], []], "done": [False, False]}
        if post:
            rows_ready = self.load_rows(*post)
        u_free = [self.u_read]

        def after_tile(tt):
            h = self.H[:, tt, :]
            ready = self.h_ready[tt]
            if post:
                m = self.normalize(h, h, P, ready)
                self.dve.wait(m, *rows_ready)
                m = self.dve.do(lambda e: e.tensor_tensor(h, h, self.row_g[:], ALU.mult))
                self.dve.wait(m)
                m = self.dve.do(lambda e: e.tensor_tensor(h, h, self.row_b[:], ALU.add))
                self.rows_used = [m]
                ready = self.h_ready[tt] = [m]
            if all_tiles:
                return
            state["xh"][tt] = self.normalize(h, self.XH[tt // TPC][:, tt % TPC, :], P, ready, u_free, rms)
            self.h_ready[tt] = ready + [state["xh"][tt]]

        def make(c):
            if not state["done"][c]:
                state["done"][c] = True
                state["chunk"][c] = self.transpose_chunk(c, self.XH[c], state["xh"][c * TPC:(c + 1) * TPC],
                                                         scale, shift, u_free)

        def between(tt):
            if tt == TT - 1 and not all_tiles:
                make(0)

        return after_tile, between, make, lambda c: state["chunk"][c]

    def load_rows(self, g, b):
        n = self.n_rows = self.n_rows + 1
        return [self.load(f"row_g{n}", self.row_g[:], g.partition_broadcast(P), *self.rows_used),
                self.load(f"row_b{n}", self.row_b[:], b.partition_broadcast(P), *self.rows_used)]

    def plan_units(self):
        a = self.a
        units = []

        def up(w, col):
            v = w[:, col:col + P].rearrange("(k p) m -> p k m", p=P)
            return Unit([(lambda r: r[:].rearrange("p (k m) -> p k m", k=KT), v)])

        def down(w, row, gate=None):
            return Unit([(lambda r: r[:], w[row:row + P, :])], gate=gate)

        def ada(layer, first, n):
            for i in range(first, first + n):
                u = up(a["ada_w"][layer], i * P)
                u.whole = True
                units.append(u)

        def gate(layer, which):
            def ask():
                m = self.gate_ready.get((layer, which))
                return None if m is None else (self.row_gate, m)
            return ask

        def mlp(w1, w2, g=None, fill=None):
            for blk in range(D_FF // (P * FB)):
                for j in range(FB):
                    units.append(up(w1, (blk * FB + j) * P))
                if fill:
                    fill(blk)
                for j in range(FB):
                    units.append(down(w2, (blk * FB + j) * P, g))

        ada(0, 8, 8)
        ada(0, 0, 8)
        w_in = a["w_in"][0]
        n = [0]

        def ada_fill():
            if n[0] < 8:
                ada(0, 16 + 4 * n[0], 4)
                n[0] += 1
        for i in range(4):
            units.append(up(w_in, Q0 + i * P))
        for i in range(4):
            units.append(up(w_in, K0 + i * P))
            ada_fill()
        for i in range(4):
            v = w_in[2 * i * P:(2 * i + 2) * P, V0:V0 + 512].rearrange("(k p) n -> p k n", p=P)
            units.append(Unit([(lambda r: r[:].rearrange("p (k n) -> p k n", k=2), v)]))
        for i in range(4):
            for part in (1, 2, 0):
                units.append(up(w_in, part * D_CONV + i * P))
            ada_fill()
        for h in range(HEADS):
            stored = lambda key: (lambda: self.stored.get(key))
            units.append(Unit([(lambda r: r[:], self.d_q[h])], after=stored(("q", h))))
            units.append(Unit([(lambda r: r[:], self.d_k[h])], after=stored(("k", h))))
            v = self.d_v[:, h * P:(h + 1) * P].rearrange("(k p) n -> p k n", p=P)
            units.append(Unit([(lambda r: r[:, 0:256], self.d_kc[h]),
                               (lambda r: r[:, 256:512].rearrange("p (k n) -> p k n", k=2), v[:, TT:TT + CTT, :])],
                              after=stored("ctx"), size=512))
            units.append(Unit([(lambda r: r[:].rearrange("p (k n) -> p k n", k=TT), v[:, 0:TT, :])],
                              after=stored("v")))
        for k in range(KT):
            units.append(down(a["w_out_mix"][0], k * P, gate(0, 0)))
        mlp(a["mlp_w1"][0], a["mlp_w2"][0], gate(0, 1), lambda blk: ada(1, 6 * blk, 6))
        for i in range(6):
            into = (lambda: None if self.table_free is None else (self.table_hi, self.table_lo, self.table_free)) \
                if i == 5 else None
            units.append(Unit([(lambda r: r[:], a["dft"][i])], into=into))
        for k in range(KT):
            units.append(down(a["w_out_fourier"][0], k * P, gate(1, 0)))
        mlp(a["mlp_w1"][1], a["mlp_w2"][1], gate(1, 1))
        w = a["w_in_2"][0]
        for m in (4, 5, 2, 3, 10, 11, 12, 13, 0, 1, 6, 7, 8, 9):
            units.append(up(w, m * P))
        pieces = []
        for e in range(2):
            s = slice(64 * e, 64 * e + 64)
            pieces.append((lambda r, s=s: r[s, 0:256].rearrange("p (j n) -> p j n", j=2)[:, :, s],
                           a["pool_w_2"][0].rearrange("(j e) c d -> e c j d", e=2)[e]))
        pieces.append((lambda r: r[:, 256:768].rearrange("p (k n) -> p k n", k=2),
                       a["convb_pw_w_2"][0].rearrange("(k p) n -> p k n", p=P)))
        units.append(Unit(pieces, zero=True, size=768))
        pieces = []
        for i, name in enumerate(("rg_w_a_2", "rg_w_x_2")):
            for e in range(2):
                s = slice(64 * e, 64 * e + 64)
                pieces.append((lambda r, s=s, i=i: r[s, 512 * i:512 * i + 512].rearrange("p (j n) -> p j n", j=4)[:, :, s],
                               a[name][0].rearrange("(j e) c d -> e c j d", e=2)[e]))
        units.append(Unit(pieces, zero=True))
        for k in range(KT):
            units.append(down(a["w_out_2"][0], k * P))
        mlp(a["w_up_2"][0], a["w_down_2"][0])
        return units

    def start(self):
        pe, act, dve, pool, a = self.pe, self.act, self.dve, self.pool, self.a
        for q in (pe, act, dve, pool):
            q.begin("start")
        self.gate_ready, self.mod_ready, self.stored = {}, {}, {}
        self.gate_used, self.rows_used, self.a_read = [], [], []
        self.table_free = None
        self.u_read = None
        s_vec = [self.semaphore("s_vectors"), 0]
        for g, (names, used) in enumerate(self.col_groups):
            for name, rows, at in names:
                v = self.a["v_" + name]
                vec_loaded = self.dma(pool, s_vec, self.conv_gather(g)[at:at + rows, :], v)
        m = pool.do(lambda e: e.memset(self.ident[:], 0.0))
        pool.wait(m)
        self.ident_ready = pool.do(lambda e: e.affine_select(
            out=self.ident[:], in_=self.ident[:], compare_op=ALU.not_equal, fill=1.0, base=0,
            pattern=[[-1, P]], channel_multiplier=1))
        m = dve.do(lambda e: e.memset(self.ones[:], 1.0))
        for i, v in enumerate((1e-6, 1e-5, 0.0)):
            m_eps = dve.do(lambda e, i=i, v=v: e.memset(self.eps[:, i:i + 1], v))
        self.ones_ready = m_eps
        act.wait(m_eps)
        x = a["x"][0].rearrange("(t p) d -> p t d", p=P)
        self.h_ready = []
        for t in range(TT):
            self.h_ready.append([self.load(f"x{t}", self.H[:, t, :], x[:, t, :])])
        ctx = a["ctx"][0].rearrange("(t p) d -> p t d", p=P)
        ctx_loaded = self.load("ctx", self.ctx_raw[:], ctx)
        lq_loaded = self.load("lambda", self.temp[4][:, 0:256],
                              a["lambda_qk"][0].rearrange("a d -> (a d)").partition_broadcast(P))
        pe.wait(self.ident_ready, vec_loaded)
        at = 0
        for g, (names, used) in enumerate(self.col_groups):
            b = self.take_bank()
            m = pe.do(lambda e, g=g, b=b, used=used: e.transpose(self.psum[:, b, 0:used], self.conv_gather(g)[0:used, :],
                                                                 self.ident[0:used, 0:used]))
            dve.wait(m)
            m = dve.do(lambda e, b=b, used=used, at=at: e.tensor_copy(self.cols[:, at:at + used], self.psum[:, b, 0:used]))
            self.bank_free[b] = [m]
            at += used
        self.cols_ready = m
        act.wait(m)
        act.do(lambda e: e.activation(self.cc[:, :, 0], self.columns("c", 0, 8), ACT.Silu))
        self.cc_ready = act.do(lambda e: e.activation(self.cc[:, :, 1], self.columns("c_ctx", 0, 8), ACT.Silu))
        lq = self.temp[4]
        dve.wait(lq_loaded)
        v = lq[:, 0:256].rearrange("p (a b d) -> p a b d", a=2, b=2)
        m = dve.do(lambda e: e.tensor_tensor(lq[:, 256:384].rearrange("p (a d) -> p a d", a=2), v[:, :, 0, :], v[:, :, 1, :], ALU.mult))
        dve.wait(m)
        m = dve.do(lambda e: e.tensor_reduce(self.lam[:, 0:2], lq[:, 256:384].rearrange("p (a d) -> p a d", a=2), AX_X, ALU.add))
        self.temp_free[4] = [m]
        act.wait(m)
        m = act.do(lambda e: e.activation(self.lam[:, 2:4], self.lam[:, 0:2], ACT.Exp))
        dve.wait(m)
        m = dve.do(lambda e: e.tensor_tensor(self.lam[:, 4:5], self.lam[:, 3:4], self.lam[:, 2:3], ALU.subtract))
        dve.wait(m)
        self.lam_ready = dve.do(lambda e: e.tensor_scalar(self.lam[:, 4:5], self.lam[:, 4:5], -LAM_INIT, None, ALU.add))
        xh = [None] * TT
        xhc = [self.normalize(self.ctx_raw[:, t, :], self.XHc[:, t, :], P, [ctx_loaded]) for t in range(CTT)]
        for t in range(TT):
            xh[t] = self.normalize(self.H[:, t, :], self.XH[t // TPC][:, t % TPC, :], P, self.h_ready[t])
            self.h_ready[t] = self.h_ready[t] + [xh[t]]
        self.ada(0, 8, 8, with_ctx=True)
        self.ada(0, 0, 8, with_ctx=True)
        return xh, xhc

    def conv_gather(self, g):
        return self.temp[g][:, 0:P]

    def project_attention(self, xh, xhc):
        pe, act, dve, pool, a = self.pe, self.act, self.dve, self.pool, self.a
        for q in (pe, act, dve, pool):
            q.begin("project")
        mod_done = [self.mod_ready[(0, 0)], self.mod_ready[(0, 1)]]
        act.wait(*mod_done)
        scale = lambda k: self.mod[:, 0, 8 + k:9 + k]
        shift = lambda k: self.mod[:, 0, k:k + 1]
        pe.wait(*xhc)
        uc_ready = []
        banks = []
        for k in range(KT):
            if k % 2 == 0:
                b = self.take_bank()
            for t in range(CTT):
                m = pe.do(lambda e, b=b, k=k, t=t: e.transpose(
                    self.psum[:, b, (k % 2) * CTX + t * P:(k % 2) * CTX + (t + 1) * P],
                    self.XHc[:, t, k * P:(k + 1) * P], self.ident[:]))
            banks.append(b)
        all_read = m
        for k in range(KT):
            t = self.take_temp(act)
            v, b = self.temp[t], banks[k]
            act.wait(all_read)
            m_v = act.do(lambda e, v=v, b=b, k=k: e.activation(
                v[:, 0:CTX], self.psum[:, b, (k % 2) * CTX:(k % 2 + 1) * CTX], ACT.Identity,
                bias=self.mod_ctx[:, k:k + 1], scale=self.mod_ctx[:, 8 + k:9 + k]))
            self.bank_free[b] = [m_v]
            m = self.split(v[:, 0:CTX], self.Uc_hi[:, k, :], self.Uc_lo[:, k, :], [m_v], [all_read])
            self.temp_free[t] = m
            uc_ready += m
        rope_loaded = [self.load("rope_cos", self.rope_cos[:], a["rope_cos"], all_read),
                       self.load("rope_sin", self.rope_sin[:], a["rope_sin"], all_read)]
        chunk = [[], []]

        def before_chunk(c):
            chunk[c] = self.transpose_chunk(c, self.XH[c], xh[c * TPC:(c + 1) * TPC], scale, shift, [])

        stage_next, stage_free = [0], [[all_read], [all_read], [all_read], [all_read]]

        def take_stage(*queues):
            n = stage_next[0]
            stage_next[0] = (n + 1) % 4
            for q in queues:
                q.wait(*stage_free[n])
            return n

        def store(n, dst, src, ready):
            pool.wait(*ready)
            m = self.dma(pool, self.s_store[n], dst, src)
            stage_free[n] = [m]
            return m

        swap = [(i + 16) % 32 for i in range(32)]

        def rope(dram):
            marks = {}

            def evacuate(i, c, b, mark):
                s = slice(c * CH, (c + 1) * CH)
                t1, t2 = self.take_temp(dve), self.take_temp(dve)
                sw, xcos = self.temp[t1], self.temp[t2]
                x = self.psum[:, b, :]
                act_copy = act
                act_copy.wait(mark, *self.temp_free[t2])
                n = take_stage(act, dve)
                st = self.stage_buf[n]
                m_x = act.do(lambda e: e.copy(st[:], x))
                self.bank_free[b] = [m_x]
                dve.wait(m_x, *rope_loaded)
                m = dve.do(lambda e: e.stream_shuffle(sw[:], st[:], swap))
                m2 = dve.do(lambda e: e.tensor_tensor(xcos[:], st[:], self.rope_cos[:, s], ALU.mult))
                dve.wait(m)
                m = dve.do(lambda e: e.tensor_tensor(sw[:], sw[:], self.rope_sin[:, s], ALU.mult))
                dve.wait(m, m2)
                m = dve.do(lambda e: e.tensor_tensor(st[:], sw[:], xcos[:], ALU.add))
                self.temp_free[t1] = self.temp_free[t2] = [m]
                marks.setdefault(i, []).append(store(n, dram(i)[:, s], st[:], [m]))
            return evacuate, marks

        evac_q, q_marks = rope(lambda i: self.d_q[i])
        self.up_group(4, lambda c: chunk[c], evac_q, before_chunk, chunk_major=True)
        for h in range(HEADS):
            self.stored[("q", h)] = q_marks[h]

        kc_marks = []

        def keys_of_context(i, W_hi, W_lo):
            pe.wait(*uc_ready)
            b = self.take_bank()
            for k in range(KT):
                mark = self.passes(self.psum[:, b, 0:CTX], W_hi[:, k, :], W_lo[:, k, :], self.Uc_hi[:, k, :],
                                   self.Uc_lo[:, k, :], k == 0, k == KT - 1)
            n = take_stage(act)
            act.wait(mark)
            m = act.do(lambda e: e.copy(self.stage_buf[n][:, 0:CTX], self.psum[:, b, 0:CTX]))
            self.bank_free[b] = [m]
            kc_marks.append(store(n, self.d_kc[self.head], self.stage_buf[n][:, 0:CTX], [m]))
            return mark

        fills = [0]

        def fill():
            if fills[0] < 8:
                self.ada(0, 16 + 4 * fills[0], 4)
                fills[0] += 1

        for h in range(HEADS):
            self.head = h
            evac_k, k_marks = rope(lambda i, h=h: self.d_k[h])
            self.up_group(1, lambda c: chunk[c], evac_k, extra=keys_of_context)
            self.stored[("k", h)] = k_marks[0]
            fill()
        units = [self.take_unit() for _ in range(4)]
        v_marks = []
        for t in range(TT + CTT):
            b = self.take_bank()
            for k in range(KT):
                u = units[k // 2]
                s = slice((k % 2) * CH, (k % 2 + 1) * CH)
                if t < TT:
                    l = [U[:, t // TPC, k, (t % TPC) * P:(t % TPC + 1) * P] for U in (self.U_hi, self.U_lo)]
                else:
                    l = [U[:, k, (t - TT) * P:(t - TT + 1) * P] for U in (self.Uc_hi, self.Uc_lo)]
                mark = self.passes(self.psum[:, b, :], l[0], l[1], u.hi[:, s], u.lo[:, s], k == 0, k == KT - 1)
            n = take_stage(act)
            act.wait(mark)
            m = act.do(lambda e, n=n, b=b: e.copy(self.stage_buf[n][:], self.psum[:, b, :]))
            self.bank_free[b] = [m]
            v_marks.append(store(n, self.d_v[t * P:(t + 1) * P, :], self.stage_buf[n][:], [m]))
        for u in units:
            self.release(u, mark)
        self.stored["v"] = v_marks[-4:] 
        self.stored["ctx"] = kc_marks[-1:] + v_marks[-4:]
        h_read = [m for r in self.h_ready for m in r]
        dve.wait(*h_read)
        zero = dve.do(lambda e: e.memset(self.gv[:, 0:1], 0.0))
        zero = dve.do(lambda e: e.memset(self.gv[:, T + 1:T + 2], 0.0))
        state = {"gc": [], "gv": [], "free_gc": h_read, "free_gv": [], "free_cv": [[], []], "cv": None}
        conv_marks = []
        self.stored["conv"] = conv_marks
        for i in range(4):
            cv = (self.cv, self.cv2)[i % 2]

            def evac(part, c, b, mark, i=i, cv=cv):
                s = slice(c * CH, (c + 1) * CH)
                x = self.psum[:, b, :]
                if part == 0:
                    act.wait(mark, *state["free_gc"])
                    m = act.do(lambda e: e.copy(self.conv_gc[:, s], x))
                    state["gc"] = [m]
                elif part == 1:
                    dve.wait(mark, *state["gc"], *state["free_gv"])
                    m = dve.do(lambda e: e.tensor_tensor(self.gv[:, 1 + c * CH:1 + (c + 1) * CH], x, self.conv_gc[:, s], ALU.mult))
                    state["free_gc"] = [m]
                    if c == 1:
                        w = [self.columns("conv_w", 4 * tap + i) for tap in range(3)]
                        dve.wait(m, zero, *state["free_cv"][i % 2])
                        mm = dve.do(lambda e: e.tensor_scalar(cv[:], self.gv[:, 0:T], w[0], None, ALU.mult))
                        for tap in (1, 2):
                            dve.wait(mm)
                            mm = dve.do(lambda e, tap=tap: e.scalar_tensor_tensor(
                                cv[:], self.gv[:, tap:tap + T], w[tap], cv[:], ALU.mult, ALU.add))
                        state["free_gv"] = state["cv"] = [mm]
                else:
                    n = take_stage(dve)
                    st = self.stage_buf[n]
                    dve.wait(mark, *state["cv"])
                    m = dve.do(lambda e: e.tensor_tensor(st[:], x, cv[:, s], ALU.mult))
                    state["free_cv"][i % 2] = [m]
                    conv_marks.append(store(n, self.d_conv[i, :, s], st[:], [m]))
                self.bank_free[b] = [m]

            self.up_group(3, lambda c: chunk[c], evac)
            fill()
        while fills[0] < 8:
            fill()
        self.h_region_free = list(state["free_cv"][0]) + list(state["free_cv"][1]) + state["free_gc"]
        self.stage_all = [m for s in stage_free for m in s]
        self.uc_read = mark
        self.project_done = self.u_read

    def attention(self):
        pe, act, dve, pool = self.pe, self.act, self.dve, self.pool
        for q in (pe, act, dve, pool):
            q.begin("attention")
        A_BANKS = ((0, 1, 2), (3, 4, 5))
        scale = QK ** -0.5
        conv_loaded = self.load("conv_in", self.conv_in[:], self.d_conv.rearrange("k p t -> p k t"),
                                self.project_done, self.uc_read, *self.stage_all, *self.stored["conv"])
        act.wait(self.project_done, self.uc_read, *self.stage_all, *self.h_region_free)
        dve.wait(self.project_done, self.uc_read, *self.stage_all, *self.h_region_free)
        S = [self.psum[:, 3 * c:3 * c + 3, :].rearrange("p b n -> p (b n)")[:, 0:KEYS] for c in range(2)]
        units = {}
        o_read = []
        prev = None
        prob_free = [[[], []], [[], []]]
        pt_free = []
        conv_done = []
        o_marks = [[] for _ in range(TT)]

        def scores(h, qt, par):
            if qt == 0:
                units[h] = [self.take_unit() for _ in range(3)]
            uq, uk, uc = units[h][:3]
            info = []
            for c in range(2):
                s = slice(64 * c, 64 * c + 64)
                for b, (src, lo_, hi_) in zip(A_BANKS[c], ((uk, 0, 512), (uk, 512, 1024), (uc, 0, 256))):
                    self.take_bank(b)
                    mark = self.passes(self.psum[:, b, 0:hi_ - lo_], uq.hi[s, qt * P:(qt + 1) * P],
                                       uq.lo[s, qt * P:(qt + 1) * P], src.hi[s, lo_:hi_], src.lo[s, lo_:hi_], True, True)
                sm = self.take_small()
                dve.wait(mark)
                m = dve.do(lambda e, c=c, sm=sm: e.tensor_reduce(sm[:, 0:1], S[c], AX_X, ALU.max))
                dve.wait(m)
                m = dve.do(lambda e, sm=sm: e.tensor_scalar(sm[:, 1:2], sm[:, 0:1], -scale, None, ALU.mult))
                act.wait(m, *prob_free[par][c])
                m = act.do(lambda e, c=c, sm=sm: e.activation(self.prob[par][c][:], S[c], ACT.Exp, bias=sm[:, 1:2],
                                                              scale=scale, accum_out=sm[:, 2:3]))
                for b in A_BANKS[c]:
                    self.bank_free[b] = [m]
                info.append((sm, m))
            (sm0, m0), (sm1, m1) = info
            if qt == TT - 1:
                self.release(uq, mark)
                self.release(uk, mark)
            dve.wait(m0, m1, self.lam_ready)
            m = dve.do(lambda e: e.reciprocal(sm1[:, 3:4], sm1[:, 2:3]))
            m_r0 = dve.do(lambda e: e.reciprocal(sm0[:, 3:4], sm0[:, 2:3]))
            dve.wait(m)
            m = dve.do(lambda e: e.scalar_tensor_tensor(sm1[:, 4:5], sm1[:, 3:4], sm0[:, 2:3], self.lam[:, 4:5],
                                                        ALU.mult, ALU.mult))
            dve.wait(m)
            p0, p1 = self.prob[par]
            m = dve.do(lambda e: e.scalar_tensor_tensor(p0[:], p1[:], sm1[:, 4:5], p0[:], ALU.mult, ALU.add))
            prob_free[par][1] = [m]
            return h, qt, par, m, sm0[:, 3:4], m_r0

        def values(h, qt, par, mixed, r0, m_r0):
            nonlocal pt_free
            if qt == 0:
                units[h].append(self.take_unit())
            uc, uv = units[h][2], units[h][3]
            p0 = self.prob[par][0]
            pe.wait(mixed)
            ready = []
            for first, n, b in ((0, 4, 6), (4, 4, 7), (8, 2, 6)):
                self.take_bank(b)
                for i in range(n):
                    m = pe.do(lambda e, i=i, b=b, first=first: e.transpose(
                        self.psum[:, b, i * P:(i + 1) * P], p0[:, (first + i) * P:(first + i + 1) * P], self.ident[:]))
                src = self.psum[:, b, 0:n * P]
                s = slice(first, first + n)
                got = self.split(src, self.PT_hi[:, s, :].rearrange("p k n -> p (k n)"),
                                 self.PT_lo[:, s, :].rearrange("p k n -> p (k n)"), [m], pt_free)
                self.bank_free[b] = got
                ready.append(got)
            prob_free[par][0] = [m]
            self.take_bank(7)
            for k in range(KEYS // P):
                pe.wait(*ready[k // 4])
                if k < TT:
                    v_hi, v_lo = uv.hi[:, k * P:(k + 1) * P], uv.lo[:, k * P:(k + 1) * P]
                else:
                    s = slice(256 + (k - TT) * P, 256 + (k - TT + 1) * P)
                    v_hi, v_lo = uc.hi[:, s], uc.lo[:, s]
                mark = self.passes(self.psum[:, 7, 0:P], self.PT_hi[:, k, :], self.PT_lo[:, k, :], v_hi, v_lo,
                                   k == 0, k == KEYS // P - 1)
            pt_free = [mark]
            act.wait(mark, m_r0)
            m = act.do(lambda e: e.activation(self.O[:, qt, h * P:(h + 1) * P], self.psum[:, 7, 0:P], ACT.Copy, scale=r0))
            self.bank_free[7] = [m]
            o_marks[qt] = [m]
            if qt == TT - 1:
                self.release(uc, mark)
                self.release(uv, mark)
            if h == HEADS - 1:
                t = self.take_temp(dve)
                sq = self.temp[t]
                o = self.O[:, qt, :]
                dve.wait(m)
                m = dve.do(lambda e: e.tensor_tensor(sq[:], o, o, ALU.mult))
                dve.wait(m)
                m = dve.do(lambda e: e.tensor_reduce(self.sumsq[:, qt, :], sq[:].rearrange("p (h d) -> p h d", h=HEADS),
                                                     AX_X, ALU.add))
                self.temp_free[t] = [m]
                o_marks[qt] = [m]

        step = 0
        for h in range(HEADS):
            for qt in range(TT):
                now = scores(h, qt, step % 2)
                if prev:
                    values(*prev)
                prev = now
                if qt < 2 * NCH and h > 0 and step % 2 == 0 and len(conv_done) < 16:
                    pass
                if step >= 4 and step < 12:
                    i, c = (step - 4) // 2, (step - 4) % 2
                    conv_done += self.split(self.conv_in[:, i, c * CH:(c + 1) * CH], self.U_hi[:, c, i, :],
                                            self.U_lo[:, c, i, :], [conv_loaded, self.project_done])
                step += 1
        values(*prev)
        self.bank_next = 0
        last_values = pt_free
        x = self.a["x"][0].rearrange("(t p) d -> p t d", p=P)
        free = [prob_free[0][0], prob_free[0][1], prob_free[1][0], prob_free[1][1], pt_free]
        for t in range(TT):
            self.h_ready[t] = [self.load(f"xx{t}", self.H[:, t, :], x[:, t, :], *free)]
        self.gate_row(0, 0)
        return conv_done, o_marks

    def attention_out(self, conv_done, o_marks):
        pe, act, dve = self.pe, self.act, self.dve
        ss = self.sumsq[:].rearrange("p t h -> p (t h)")
        act.wait(*[m for ms in o_marks for m in ms])
        m = act.do(lambda e: e.activation(ss, ss, ACT.Sqrt, bias=self.eps[:, 1:2], scale=1.0 / P))
        dve.wait(m)
        m_r = dve.do(lambda e: e.reciprocal(ss, ss))
        g = self.softplus[:, 7, 0:1]
        m_g = dve.do(lambda e: e.tensor_scalar(g, self.columns("subln_g"), 1.0 - LAM_INIT, None, ALU.mult))
        act.wait(m_g)
        normed = []
        dve.wait(m_r)
        for t in range(TT):
            o = self.O[:, t, :].rearrange("p (h d) -> p h d", h=HEADS)
            normed.append(dve.do(lambda e, o=o, t=t: e.tensor_tensor(
                o, o, self.sumsq[:, t, :].unsqueeze(2).to_broadcast([P, HEADS, P]), ALU.mult)))
        self.down_block(self.u_lhs(0), lambda j, tt: conv_done, ALPHA)
        ready = []
        for c in range(NCH):
            for h in range(HEADS):
                b = self.take_bank()
                pe.wait(*normed[c * TPC:(c + 1) * TPC])
                for i in range(TPC):
                    m = pe.do(lambda e, b=b, i=i, h=h, c=c: e.transpose(
                        self.psum[:, b, i * P:(i + 1) * P], self.O[:, c * TPC + i, h * P:(h + 1) * P], self.ident[:]))
                t = self.take_temp(act)
                v = self.temp[t]
                act.wait(m)
                m = act.do(lambda e, v=v, b=b: e.activation(v[:], self.psum[:, b, :], ACT.Copy, scale=g))
                self.bank_free[b] = [m]
                m = self.split(v[:], self.U_hi[:, c, 4 + h, :], self.U_lo[:, c, 4 + h, :], [m])
                self.temp_free[t] = m
                ready.append(m)
        return ready

    def fourier(self, xh, chunk_unused=None):
        pe, act, dve = self.pe, self.act, self.dve
        for q in (pe, act, dve):
            q.begin("fourier")
        scale = lambda k: self.mod[:, 1, 8 + k:9 + k]
        shift = lambda k: self.mod[:, 1, k:k + 1]
        act.wait(self.mod_ready[(1, 0)], self.mod_ready[(1, 1)])
        u_ready = {}
        for k in range(KT):
            vs = []
            for c in range(2):
                b = self.take_bank()
                pe.wait(*xh[c * TPC:(c + 1) * TPC])
                for i in range(TPC):
                    m = pe.do(lambda e, b=b, i=i, c=c, k=k: e.transpose(
                        self.psum[:, b, i * P:(i + 1) * P], self.XHall[:, c * TPC + i, k * P:(k + 1) * P], self.ident[:]))
                self.xh_read = m
                t = self.take_temp(act)
                act.wait(m)
                m = act.do(lambda e, t=t, b=b, k=k: e.activation(self.temp[t][:], self.psum[:, b, :], ACT.Identity,
                                                                 bias=shift(k), scale=scale(k)))
                self.bank_free[b] = [m]
                vs.append((t, m))
            (t0, m0), (t1, m1) = vs
            v0, v1 = self.temp[t0], self.temp[t1]
            t2 = self.take_temp(dve)
            odd = self.temp[t2]
            dve.wait(m0, m1)
            m = dve.do(lambda e, odd=odd, v0=v0, v1=v1: e.tensor_tensor(odd[:], v0[:], v1[:], ALU.subtract))
            m_e = dve.do(lambda e, v0=v0, v1=v1: e.tensor_tensor(v0[:], v0[:], v1[:], ALU.add))
            ready = self.split(odd[:], self.U_hi[:, 0, k, :], self.U_lo[:, 0, k, :], [m, self.u_read])
            self.temp_free[t2] = ready
            q = CH // 2
            dve.wait(m_e)
            m = dve.do(lambda e, v0=v0, v1=v1: e.tensor_tensor(v1[:, 0:q], v0[:, 0:q], v0[:, q:CH], ALU.subtract))
            m2 = dve.do(lambda e, v0=v0, v1=v1: e.tensor_tensor(v1[:, q:CH], v0[:, 0:q], v0[:, q:CH], ALU.add))
            self.temp_free[t0] = [m2]
            got = self.split(v1[:], self.U_hi[:, 1, k, :], self.U_lo[:, 1, k, :], [m, m2, self.u_read])
            self.temp_free[t1] = got
            u_ready[k] = ready + got
        chan = self.load("chan", self.chan_raw[:], self.a["dft_chan"], self.xh_read)
        chan_ready = self.split(self.chan_raw[:], self.chan_hi[:], self.chan_lo[:], [chan, self.xh_read])
        self.table_free = [self.xh_read]
        tables = [self.take_unit() for _ in range(6)]
        pq_free, y_ready = [], []
        act.wait(self.xh_read)
        for g in range(KT):
            pe.wait(*chan_ready, *u_ready[g])
            pq_ready = []
            for half in range(2):
                for pair in range(2):
                    b = self.take_bank()
                    for i in range(2):
                        s = slice((2 * pair + i) * P, (2 * pair + i + 1) * P)
                        mark = self.passes(self.psum[:, b, i * 2 * P:(i + 1) * 2 * P], self.U_hi[:, half, g, s],
                                           self.U_lo[:, half, g, s], self.chan_hi[:], self.chan_lo[:], True, True)
                    at = 4 * half + 2 * pair
                    m = self.split(self.psum[:, b, :], self.PQ_hi[:, at:at + 2, :].rearrange("p a n -> p (a n)"),
                                   self.PQ_lo[:, at:at + 2, :].rearrange("p a n -> p (a n)"), [mark], pq_free)
                    self.bank_free[b] = m
                    pq_ready.append(m)
            u_taken = mark
            b_odd, b_even = self.take_bank(), self.take_bank()
            for cls, (tiles, first, n, b, col) in enumerate(((4, 0, CH, b_odd, 0), (2, 4, CH // 2, b_even, 0),
                                                             (2, 6, CH // 2, b_even, CH // 2))):
                for t in range(tiles):
                    pe.wait(*pq_ready[(first + t) // 2])
                    for cs in range(2):
                        if cls == 0:
                            r = [x[:, cs * CH:(cs + 1) * CH] for x in (tables[t].hi, tables[t].lo)]
                        else:
                            u = tables[3 + cls]
                            at = (2 * t + cs) * n
                            r = [x[:, at:at + n] for x in (u.hi, u.lo)]
                        l = [x[:, first + t, cs * P:(cs + 1) * P] for x in (self.PQ_hi, self.PQ_lo)]
                        mark = self.passes(self.psum[:, b, col:col + n], l[0], l[1], r[0], r[1],
                                           t == 0 and cs == 0, t == tiles - 1 and cs == 1)
                if cls == 0:
                    odd_done = mark
            pq_free = [mark]
            dst = lambda off, step: [x[:, :, g, off::step] for x in (self.U_hi, self.U_lo)]
            hi, lo = dst(1, 2)
            got = [self.split(self.psum[:, b_odd, :].rearrange("p (c n) -> p c n", c=2), hi, lo, [odd_done, u_taken])]
            evens = [(self.psum[:, b_even, i * 256:(i + 1) * 256].rearrange("p (c n) -> p c n", c=2), *dst(off, 4))
                     for i, off in ((0, 2), (1, 0))]
            act.wait(mark, u_taken)
            m_hi = [act.do(lambda e, src=src, hi=hi: e.copy(hi, src)) for src, hi, lo in evens]
            dve.wait(mark, u_taken, *m_hi)
            m_lo = [dve.do(lambda e, src=src, hi=hi, lo=lo: e.tensor_tensor(lo, src, hi.bitcast(F32), ALU.subtract))
                    for src, hi, lo in evens]
            got.append(m_hi + m_lo)
            self.bank_free[b_odd], self.bank_free[b_even] = got
            y_ready.append(got[0] + got[1])
        for u in tables:
            self.release(u, mark)
        self.a_read = [mark]
        self.gate_used = self.gate_used_now()
        return y_ready

    def gate_used_now(self):
        return [(self.dve.stage, self.dve.count)] if self.dve.count else []

    def mixers(self, chunk_ready, before_chunk):
        pe, act, dve, pool, a = self.pe, self.act, self.dve, self.pool, self.a
        for q in (pe, act, dve, pool):
            q.begin("mixers")
        region = [self.a_read, *[m for r in self.h_ready for m in r], self.rows_used]
        meta = self.load("meta", self.meta_raw[:], a["meta_tokens_2"], *region)
        act.wait(*region)
        dve.wait(*region)
        m = self.normalize(self.meta_raw[:], self.meta_hat[:], META, [meta], rms=True)
        pe.wait(m)
        b = self.take_bank()
        for k in range(KT):
            m = pe.do(lambda e, k=k: e.transpose(self.psum[:, b, k * META:(k + 1) * META],
                                                 self.meta_hat[:, k * P:(k + 1) * P], self.ident[0:META, 0:META]))
        t = self.take_temp(dve)
        v = self.temp[t]
        dve.wait(m)
        g = self.columns("mix_norm_g_2", 0, KT).unsqueeze(2).to_broadcast([P, KT, META])
        vv = v[:, 0:KT * META].rearrange("p (k m) -> p k m", k=KT)
        meta_read = m
        m = dve.do(lambda e: e.tensor_tensor(vv, self.psum[:, b, 0:KT * META].rearrange("p (k m) -> p k m", k=KT), g, ALU.mult))
        self.bank_free[b] = [m]
        meta_ready = self.split(vv, self.U_meta_hi[:], self.U_meta_lo[:], [m])
        self.temp_free[t] = meta_ready
        act.wait(meta_read)
        dve.wait(meta_read)
        for buf in self.gated:
            pad = dve.do(lambda e, buf=buf: e.memset(buf[:, 0:14], 0.0))
        pad = dve.do(lambda e: e.memset(self.cx[:, 0:3], 0.0))
        dve.wait(pad)

        background = []
        s_stage = [[self.semaphore(f"s_mix{i}"), 0] for i in range(2)]
        stage_free = [[], []]
        gated_m = [[], []]
        cx_m, cx_free, xc_m = [], [], {}
        work_free, dw_m, pool_m, gelu_m = [], [], [], []
        self.work_free = []

        def place(dst, off):
            return lambda c: dst[:, off:off + META] if c < 0 else dst[:, off + META + c * CH:off + META + (c + 1) * CH]

        def evac(unit, c, b, mark):
            n = META if c < 0 else CH
            x = self.psum[:, b, 0:n]
            if unit < 2:
                act.wait(mark)
                m = act.do(lambda e: e.activation(place(self.gated[unit], 14)(c), x, ACT.Sigmoid))
                gated_m[unit].append(m)
            elif unit < 4:
                dst = place(self.gated[unit - 2], 14)(c)
                dve.wait(mark, *gated_m[unit - 2])
                m = dve.do(lambda e: e.tensor_tensor(dst, x, dst, ALU.mult))
                gated_m[unit - 2].append(m)
            elif unit < 8:
                act.wait(mark, *cx_free)
                m = act.do(lambda e: e.copy(place(self.cx, 3)(c), x))
                cx_m.append(m)
            else:
                act.wait(mark, *self.work_free)
                f = ACT.Copy if unit < 10 else ACT.Gelu_apprx_tanh
                m = act.do(lambda e: e.activation(place(self.work, 0)(c), x, f))
                work_m.append(m)
            self.bank_free[b] = [m]

        work_m = []

        def taps(i):
            src, dst = self.gated[i], self.dw[i]

            def first():
                dve.wait(*gated_m[i])
                dw_m[:] = [dve.do(lambda e: e.tensor_scalar(dst[:], src[:, 0:T], self.columns("convb_dw_w_2", i),
                                                            self.columns("convb_dw_b_2", i), ALU.mult, ALU.add))]
            background.append(first)
            for tap in range(1, CONV_K):
                def one(tap=tap):
                    dve.wait(*dw_m)
                    dw_m[:] = [dve.do(lambda e: e.scalar_tensor_tensor(
                        dst[:], src[:, tap:tap + T], self.columns("convb_dw_w_2", 2 * tap + i), dst[:], ALU.mult, ALU.add))]
                background.append(one)

        def after_unit(unit):
            if unit == 3:
                taps(0)
                taps(1)
            if 4 <= unit < 8:
                j = unit - 4
                dst = self.xc[j]
                dve.wait(*cx_m)
                m = dve.do(lambda e: e.tensor_scalar(dst[:], self.cx[:, 0:TM], self.columns("rg_conv_w_2", j),
                                                     self.columns("rg_conv_b_2", j), ALU.mult, ALU.add))
                for tap in range(1, RG_K):
                    dve.wait(m)
                    m = dve.do(lambda e, tap=tap: e.scalar_tensor_tensor(
                        dst[:], self.cx[:, tap:tap + TM], self.columns("rg_conv_w_2", 4 * tap + j), dst[:], ALU.mult, ALU.add))
                cx_free[:] = [m]
                cx_m.clear()
                xc_m[j] = [m]
            if unit >= 8:
                i = unit - 8 if unit < 10 else unit - 10
                dram = self.d_pool[i] if unit < 10 else self.d_gelu[i]
                pool.wait(*work_m)
                m = self.dma(pool, s_stage[0], dram, self.work[:])
                (pool_m if unit < 10 else gelu_m).append(m)
                self.work_free = [m]
                work_m.clear()
            for _ in range(6):
                if background:
                    background.pop(0)()

        count = [0]

        def extra_at(first):
            def extra(i, W_hi, W_lo):
                pe.wait(*meta_ready)
                b = self.take_bank()
                for k in range(KT):
                    mark = self.passes(self.psum[:, b, 0:META], W_hi[:, k, :], W_lo[:, k, :], self.U_meta_hi[:, k, :],
                                       self.U_meta_lo[:, k, :], k == 0, k == KT - 1)
                evac(first + i, -1, b, mark)
                after_unit(first + i)
                return mark
            return extra

        self.up_group(4, chunk_ready, evac, before_chunk, chunk_major=True, extra=extra_at(0))
        for unit in range(4, 14):
            self.up_group(1, chunk_ready, lambda i, c, b, mark, unit=unit: evac(unit, c, b, mark), extra=extra_at(unit))
        u_done = self.u_read_all = (pe.stage, pe.count)
        while background:
            background.pop(0)()
        Yslot = lambda k, c: (self.U_hi[:, c, k, :], self.U_lo[:, c, k, :])
        unit_small = self.take_unit()
        unit_rg = self.take_unit()

        y_ready = {}
        gated_free = list(dw_m)
        L = TM
        for i in range(2):
            x_t = self.work
            pool.wait(*self.work_free, *pool_m)
            loaded = self.dma(pool, s_stage[0], self.work[:], self.d_pool[i])
            s_a, s_b = self.gated[0], self.gated[1]
            dve.wait(loaded, *gated_free)
            m = dve.do(lambda e: e.tensor_tensor(s_a[:, 1:L], x_t[:, 1:L], x_t[:, 0:L - 1], ALU.add))
            dve.wait(m)
            if i == 0:
                m = dve.do(lambda e: e.tensor_tensor(s_b[64:P, 3:L], s_a[64:P, 3:L], s_a[64:P, 1:L - 2], ALU.add))
                parts = ((0, s_a, 2), (64, s_b, 4))
            else:
                m = dve.do(lambda e: e.tensor_tensor(s_b[:, 3:L], s_a[:, 3:L], s_a[:, 1:L - 2], ALU.add))
                dve.wait(m)
                m = dve.do(lambda e: e.tensor_tensor(s_a[:, 7:L], s_b[:, 7:L], s_b[:, 3:L - 4], ALU.add))
                dve.wait(m)
                m = dve.do(lambda e: e.tensor_tensor(s_b[64:P, 15:L], s_a[64:P, 15:L], s_a[64:P, 7:L - 8], ALU.add))
                parts = ((0, s_a, 8), (64, s_b, 16))
            dve.wait(m)
            for p0, src, w in parts:
                m = dve.do(lambda e, p0=p0, src=src, w=w: e.scalar_tensor_tensor(
                    src[p0:p0 + 64, META:TM], src[p0:p0 + 64, META:TM], 1.0 / w, x_t[p0:p0 + 64, META:TM],
                    ALU.mult, ALU.subtract))
            dve.wait(m)
            m = dve.do(lambda e: e.tensor_copy(s_a[64:P, META:TM], s_b[64:P, META:TM]))
            self.work_free = [m]
            for c in range(NCH):
                hi, lo = Yslot(i, c)
                got = self.split(s_a[:, META + c * CH:META + (c + 1) * CH], hi, lo, [m], [u_done])
                gated_free = got
                b = self.take_bank()
                pe.wait(*got)
                mark = self.passes(self.psum[:, b, :], unit_small.hi[:, i * P:(i + 1) * P],
                                   unit_small.lo[:, i * P:(i + 1) * P], hi, lo, True, True)
                t = self.take_temp(act)
                act.wait(mark)
                mv = act.do(lambda e, t=t, b=b, i=i: e.activation(self.temp[t][:], self.psum[:, b, :], ACT.Copy,
                                                                  scale=self.columns("pool_scale_2", i)))
                self.bank_free[b] = [mv]
                got2 = self.split(self.temp[t][:], hi, lo, [mv, mark])
                self.temp_free[t] = got2
                y_ready[(i, c)] = got2
        for c in range(NCH):
            back = [self.take_bank(), self.take_bank()]
            for half in range(2):
                b = self.take_bank()
                pe.wait(*dw_m)
                for i in range(2):
                    for k in range(2):
                        s = slice(c * CH + (2 * half + i) * P, c * CH + (2 * half + i + 1) * P)
                        m = pe.do(lambda e, i=i, k=k, s=s, b=b: e.transpose(
                            self.psum[:, b, (2 * i + k) * P:(2 * i + k + 1) * P], self.dw[k][:, s], self.ident[:]))
                t = self.take_temp(act)
                v = self.temp[t]
                stats = [(self.psum[:, b, 2 * i * P:(2 * i + 2) * P], self.statistics(
                    self.psum[:, b, 2 * i * P:(2 * i + 2) * P], P, 2 * P, [m])) for i in range(2)]
                for i, (src, (sc, bi, _)) in enumerate(stats):
                    act.wait(*stats[1][1][2])
                    mn = act.do(lambda e, i=i, v=v, src=src, sc=sc, bi=bi: e.activation(
                        v[:, 2 * i * P:(2 * i + 2) * P], src, ACT.Identity, bias=bi, scale=sc))
                self.bank_free[b] = [mn]
                pe.wait(mn)
                for i in range(2):
                    for k in range(2):
                        m = pe.do(lambda e, i=i, k=k, v=v, half=half: e.transpose(
                            self.psum[:, back[k], (2 * half + i) * P:(2 * half + i + 1) * P],
                            v[:, (2 * i + k) * P:(2 * i + k + 1) * P], self.ident[:]))
                self.temp_free[t] = [m]
            z = []
            for k in range(2):
                t = self.take_temp(act)
                act.wait(m)
                mv = act.do(lambda e, t=t, k=k: e.activation(self.temp[t][:], self.psum[:, back[k], :], ACT.Silu,
                                                             bias=self.columns("convb_ln_b_2", k),
                                                             scale=self.columns("convb_ln_g_2", k)))
                self.bank_free[back[k]] = [mv]
                hi, lo = Yslot(2 + k, c)
                got = self.split(self.temp[t][:], hi, lo, [mv], [u_done])
                self.temp_free[t] = got
                z += got
            pe.wait(*z)
            outs = []
            for j in range(2):
                b = self.take_bank()
                for k in range(2):
                    s = slice(256 + k * 256 + j * P, 256 + k * 256 + (j + 1) * P)
                    hi, lo = Yslot(2 + k, c)
                    mark = self.passes(self.psum[:, b, :], unit_small.hi[:, s], unit_small.lo[:, s], hi, lo, k == 0, k == 1)
                outs.append(b)
            for j, b in enumerate(outs):
                hi, lo = Yslot(2 + j, c)
                got = self.split(self.psum[:, b, :], hi, lo, [mark])
                self.bank_free[b] = got
                y_ready[(2 + j, c)] = got
        self.release(unit_small, mark)
        sp = [self.softplus[:, i, :] for i in range(8)]
        lam = self.columns("rg_lambda_2", 0, 4)
        m = act.do(lambda e: e.activation(sp[0], lam, ACT.Abs))
        act.wait(m)
        m = act.do(lambda e: e.activation(sp[1], sp[0], ACT.Exp, scale=-1.0))
        dve.wait(m)

        def chain(emit):
            mm = dve.do(emit)
            dve.wait(mm)
            return mm
        chain(lambda e: e.tensor_scalar(sp[2], sp[1], 2.0, None, ALU.add))
        chain(lambda e: e.reciprocal(sp[2], sp[2]))
        chain(lambda e: e.tensor_tensor(sp[2], sp[2], sp[1], ALU.mult))
        chain(lambda e: e.tensor_tensor(sp[3], sp[2], sp[2], ALU.mult))
        chain(lambda e: e.memset(sp[4], 1.0 / 19))
        for n in (17, 15, 13, 11, 9, 7, 5, 3, 1):
            chain(lambda e: e.tensor_tensor(sp[4], sp[4], sp[3], ALU.mult))
            chain(lambda e, n=n: e.tensor_scalar(sp[4], sp[4], 1.0 / n, None, ALU.add))
        chain(lambda e: e.tensor_tensor(sp[4], sp[4], sp[2], ALU.mult))
        chain(lambda e: e.tensor_scalar(sp[5], lam, -1.0, 0.0, ALU.mult, ALU.max))
        chain(lambda e: e.scalar_tensor_tensor(sp[4], sp[4], 2.0, sp[5], ALU.mult, ALU.add))
        chain(lambda e: e.tensor_scalar(sp[5], sp[4], -RG_C, None, ALU.mult))
        c8 = chain(lambda e: e.tensor_scalar(sp[6], sp[4], RG_C, None, ALU.mult))
        act.wait(c8)
        w0, w1, w2, w3 = self.gated[0][:, 0:TM], self.gated[1][:, 0:TM], self.cx[:, 0:TM], self.work[:]
        parts = ((-1, 0, META), (0, META, CH), (1, META + CH, CH))
        free = [gated_free, cx_free, self.work_free]
        for j in range(4):
            xc = self.xc[j]
            ready = []
            for c, at, n in parts:
                hi, lo = Yslot(4 + j, c) if c >= 0 else (self.U_meta_hi[:, 4 + j, :], self.U_meta_lo[:, 4 + j, :])
                ready.append(self.split(xc[:, at:at + n], hi, lo, xc_m[j], [u_done]))
            sig = []
            for which, dst, bias in ((0, w0, "rg_b_a_2"), (1, w1, "rg_b_x_2")):
                for (c, at, n), got in zip(parts, ready):
                    hi, lo = Yslot(4 + j, c) if c >= 0 else (self.U_meta_hi[:, 4 + j, :], self.U_meta_lo[:, 4 + j, :])
                    pe.wait(*got)
                    b = self.take_bank()
                    s = slice(which * 512 + j * P, which * 512 + (j + 1) * P)
                    mark = self.passes(self.psum[:, b, 0:n], unit_rg.hi[:, s], unit_rg.lo[:, s], hi, lo, True, True)
                    act.wait(mark, *free)
                    m = act.do(lambda e, dst=dst, at=at, n=n, b=b, bias=bias, j=j: e.activation(
                        dst[:, at:at + n], self.psum[:, b, 0:n], ACT.Sigmoid, bias=self.columns(bias, j)))
                    self.bank_free[b] = [m]
                    sig.append(m)
            read = mark
            dve.wait(*sig)
            m_ix = dve.do(lambda e, xc=xc: e.tensor_tensor(w1, w1, xc[:], ALU.mult))
            m_a = None
            act.wait(*sig, *free)
            m_a = act.do(lambda e, j=j: e.activation(w2, w0, ACT.Exp, scale=sp[5][:, j:j + 1]))
            m_t = act.do(lambda e, j=j: e.activation(w3, w0, ACT.Tanh, scale=sp[6][:, j:j + 1]))
            dve.wait(m_a, m_t)
            m = chain(lambda e: e.tensor_tensor(w0, w2, w2, ALU.mult))
            m = chain(lambda e: e.scalar_tensor_tensor(w0, w0, 1.0, w3, ALU.add, ALU.mult))
            pool.wait(m, *gelu_m)
            gl = self.dma(pool, s_stage[1], w3, self.d_gelu[j])
            act.wait(m)
            m = act.do(lambda e: e.activation(w0, w0, ACT.Sqrt))
            dve.wait(m, m_ix)
            m = chain(lambda e: e.tensor_tensor(w1, w1, w0, ALU.mult))
            m = chain(lambda e: e.tensor_tensor_scan(w0, w2, w1, 0.0, ALU.mult, ALU.add))
            dve.wait(gl)
            m = chain(lambda e: e.tensor_tensor(w1, w0, w3, ALU.mult))
            for c in range(NCH):
                hi, lo = Yslot(4 + j, c)
                at = META + c * CH
                got = self.split(w1[:, at:at + CH], hi, lo, [m, read])
                y_ready[(4 + j, c)] = got
            free = [got]
        self.release(unit_rg, mark)
        self.a_read = [m, y_ready[(7, 1)], mark]
        return y_ready

    def finish(self):
        rows = [self.load("final_g", self.row_g[:], self.a["final_norm_g_2"].partition_broadcast(P), *self.rows_used,
                          self.a_read)]
        out = self.out[0].rearrange("(t p) d -> p t d", p=P)
        stores = []

        def after_tile(tt):
            h = self.H[:, tt, :]
            m = self.normalize(h, h, P, self.h_ready[tt], rms=True)
            self.dve.wait(m, *rows)
            m = self.dve.do(lambda e: e.tensor_tensor(h, h, self.row_g[:], ALU.mult))
            self.pool.wait(m)
            stores.append(self.dma(self.pool, [self.semaphore(f"s_out{tt}"), 0], out[:, tt, :], h))
            self.pool_last = stores
        return after_tile, stores

    def build(self):
        self.allocate()
        self.weights_begin(self.plan_units())
        xh, xhc = self.start()
        self.project_attention(xh, xhc)
        conv_done, o_marks = self.attention()
        o_ready = self.attention_out(conv_done, o_marks)
        for q in (self.pe, self.act, self.dve):
            q.begin("mix_out")
        self.u_in_use = True
        mark = self.down_block(self.u_lhs(4), lambda j, tt: o_ready[(tt // TPC) * HEADS + j], 1.0)
        self.u_read = mark
        self.a_read = [mark]
        self.gate_used = self.gate_used_now()
        after, between, make, ready = self.boundary(
            (self.a["ln_g"][0, 0], self.a["ln_b"][0, 0]), False,
            lambda k: self.mod[:, 0, 32 + k:33 + k], lambda k: self.mod[:, 0, 24 + k:25 + k])
        for tt in range(TT):
            after(tt)
        make(0)
        self.gate_row(0, 1)
        post = (self.a["ln_g"][0, 1], self.a["ln_b"][0, 1])
        after2 = {}

        def lazy_after(tt):
            if tt == 0:
                after2["b"] = self.boundary(post, False, None, None, all_tiles=True)
            after2["b"][0](tt)
        self.mlp("mlp0", ready, lambda c: make(c), lambda blk: self.ada(1, 6 * blk, 6), lazy_after, None, ALPHA)
        self.mod_done(1)
        self.gate_used = self.gate_used_now()
        xh = []
        for tt in range(TT):
            m = self.normalize(self.H[:, tt, :], self.XHall[:, tt, :], P, self.h_ready[tt], self.a_read)
            self.h_ready[tt] = self.h_ready[tt] + [m]
            xh.append(m)
        y_ready = self.fourier(xh)
        self.gate_row(1, 0)
        self.down_block(self.u_lhs(0), lambda j, tt: y_ready[j], ALPHA)
        mark = self.down_block(self.u_lhs(4), lambda j, tt: y_ready[4 + j], 1.0)
        self.u_read = mark
        self.gate_used = self.gate_used_now()
        after, between, make, ready = self.boundary(
            (self.a["ln_g"][1, 0], self.a["ln_b"][1, 0]), False,
            lambda k: self.mod[:, 1, 32 + k:33 + k], lambda k: self.mod[:, 1, 24 + k:25 + k])
        for tt in range(TT):
            after(tt)
        make(0)
        self.gate_row(1, 1)
        hold = {}

        def post_then_rms(tt):
            if tt == 0:
                hold["b"] = self.boundary((self.a["ln_g"][1, 1], self.a["ln_b"][1, 1]), True,
                                          lambda k: self.columns("mix_norm_g_2", k), lambda k: self.eps[:, 2:3])
            hold["b"][0](tt)
        self.mlp("mlp1", ready, lambda c: make(c), None, post_then_rms, lambda tt: hold["b"][1](tt), ALPHA)
        _, _, make2, ready2 = hold["b"]
        y_ready = self.mixers(ready2, make2)
        self.down_block(self.u_lhs(0), lambda j, tt: y_ready[(j, tt // TPC)], 1.0)
        mark = self.down_block(self.u_lhs(4), lambda j, tt: y_ready[(4 + j, tt // TPC)], 1.0)
        self.u_read = mark
        after, between, make, ready = self.boundary(None, True, lambda k: self.columns("mlp_norm_g_2", k),
                                                    lambda k: self.eps[:, 2:3])
        for tt in range(TT):
            after(tt)
        make(0)
        after_last, stores = self.finish()
        self.mlp("mlp2", ready, lambda c: make(c), None, after_last)
        self.pool.wait(*stores)
        self.sp.wait(*stores)

    def mod_done(self, layer):
        pass

    def run(self):
        nc = self.nc
        block = self.stack.enter_context(nc.Block())

        @block.sync
        def _(e):
            self.sp.run(e)

        @block.scalar
        def _(e):
            self.act.run(e)

        @block.vector
        def _(e):
            self.dve.run(e)

        @block.gpsimd
        def _(e):
            self.pool.run(e)

        @block.tensor
        def _(e):
            self.pe.run(e)


def build_program(nc, arrays, out):
    program = Program(nc, arrays, out)
    with program.stack:
        program.build()
        program.run()


def rope_tables():
    d = np.arange(P) % QK
    inv = (np.float32(10000.0) ** (-np.arange(16, dtype=np.float32) / np.float32(16))).astype(np.float32)
    tok = np.arange(T)
    pos = np.where((d < 32)[:, None], tok[None, :] // 64, tok[None, :] % 64).astype(np.float32)
    ang = (pos * inv[d % 16][:, None]).astype(np.float32).astype(np.float64)
    sign = np.where(d % 32 < 16, -1.0, 1.0)[:, None]
    return np.cos(ang).astype(np.float32), (np.sin(ang) * sign).astype(np.float32)


def dft_tables():
    out = np.zeros((6, P, UNIT), np.float32)
    n = np.arange(P)[:, None]
    for t in range(4):
        ang = 2 * np.pi * (((n + P * t) * (2 * np.arange(CH) + 1)[None, :]) % T) / T
        out[t] = np.concatenate([np.cos(ang), -np.sin(ang)], 1)
    for c, off in ((4, 2), (5, 0)):
        parts = []
        for t in range(2):
            ang = 2 * np.pi * (((n + P * t) * (4 * np.arange(CH // 2) + off)[None, :]) % T) / T
            parts += [np.cos(ang), -np.sin(ang)]
        out[c] = np.concatenate(parts, 1)
    ang = 2 * np.pi * ((n * np.arange(P)[None, :]) % P) / P
    chan = np.concatenate([np.cos(ang), np.sin(ang)], 1) / math.sqrt(T * P)
    return out, chan.astype(np.float32)


_WHOLE = ["x", "ctx", "ada_w", "ln_g", "ln_b", "mlp_w1", "mlp_w2", "w_in", "lambda_qk", "w_out_mix", "w_out_fourier",
          "meta_tokens_2", "w_in_2", "pool_w_2", "convb_pw_w_2", "rg_w_a_2", "rg_w_x_2", "w_out_2", "w_up_2",
          "w_down_2", "final_norm_g_2"]


def kernel(**inputs):
    import numpy as _np
    import concourse.bacc as _bacc
    from concourse import mybir as _mybir
    from concourse.bass_utils import run_bass_kernel_spmd as _run

    nc = _bacc.Bacc("TRN2", target_bir_lowering=False, num_devices=1)
    host = {name: _np.ascontiguousarray(inputs[name]) for name in _WHOLE}
    for name, rows in VECTORS:
        host["v_" + name] = _np.ascontiguousarray(inputs[name]).reshape(rows, P)
    host["rope_cos"], host["rope_sin"] = rope_tables()
    host["dft"], host["dft_chan"] = dft_tables()
    arrays, aps = {}, {}
    for name, a in host.items():
        arrays[f"in_{name}_dram"] = a
        aps[name] = nc.dram_tensor(f"in_{name}_dram", a.shape, _mybir.dt.from_np(a.dtype), kind="ExternalInput").ap()
    out = nc.dram_tensor("out_0_dram", (1, T, D), _mybir.dt.float32, kind="ExternalOutput").ap()
    build_program(nc, aps, out)
    r = _run(nc, [arrays], core_ids=[0])
    return r.results[0]["out_0_dram"]
```

```python
import math
from contextlib import ExitStack

import numpy as np

import concourse.bass as bass
from concourse import mybir

P = 128
F32 = mybir.dt.float32
F32R = mybir.dt.float32r
ALU = mybir.AluOpType
ACT = mybir.ActivationFunctionType
AX_X = mybir.AxisListType.X

T = 1024
D = 1024
TT = T // P
KT = D // P
CH = 512
NCH = T // CH
TPC = CH // P
CTX = 256
CTT = CTX // P
D_FF = 4096
FB = 4
D_CONV = 512
Q0, K0, V0 = 3 * D_CONV, 3 * D_CONV + 512, 3 * D_CONV + 1024
HEADS = 4
QK = 64
KEYS = T + CTX
DEPTH = 2
ALPHA = (2.0 * DEPTH) ** 0.25
LAM_INIT = 0.2
META = 16
TM = T + META
CONV_K = 31
RG_K = 4
RG_C = 8.0
UNIT = 1024
N_RAW = 3
N_SPLIT = 5
N_TEMP = 5
N_SMALL = 24

VECTORS = [("c", 8), ("c_ctx", 8), ("conv_w", 12), ("subln_g", 1), ("mix_norm_g_2", 8), ("mlp_norm_g_2", 8),
           ("pool_scale_2", 2), ("convb_dw_b_2", 2), ("convb_ln_g_2", 2), ("convb_ln_b_2", 2),
           ("rg_conv_w_2", 16), ("rg_conv_b_2", 4), ("rg_b_a_2", 4), ("rg_b_x_2", 4), ("rg_lambda_2", 4),
           ("ada_b", 96), ("convb_dw_w_2", 62)]


def vector_columns():
    start, at, groups = {}, 0, []
    group, used = [], 0
    for name, rows in VECTORS:
        if used + rows > P:
            groups.append((group, used))
            at, group, used = at + used, [], 0
        start[name] = at + used
        group.append((name, rows, used))
        used += rows
    groups.append((group, used))
    return start, groups, at + used


class Later:

    def matmul(self, *operands, **options):
        self.step = lambda e: e.matmul(*operands, **options)

    def transpose(self, *operands, **options):
        self.step = lambda e: e.transpose(*operands, **options)

    def memset(self, *operands, **options):
        self.step = lambda e: e.memset(*operands, **options)

    def affine_select(self, *operands, **options):
        self.step = lambda e: e.affine_select(*operands, **options)

    def copy(self, *operands, **options):
        self.step = lambda e: e.copy(*operands, **options)

    def activation(self, *operands, **options):
        self.step = lambda e: e.activation(*operands, **options)

    def tensor_tensor(self, *operands, **options):
        self.step = lambda e: e.tensor_tensor(*operands, **options)

    def tensor_scalar(self, *operands, **options):
        self.step = lambda e: e.tensor_scalar(*operands, **options)

    def scalar_tensor_tensor(self, *operands, **options):
        self.step = lambda e: e.scalar_tensor_tensor(*operands, **options)

    def tensor_tensor_scan(self, *operands, **options):
        self.step = lambda e: e.tensor_tensor_scan(*operands, **options)

    def tensor_reduce(self, *operands, **options):
        self.step = lambda e: e.tensor_reduce(*operands, **options)

    def tensor_copy(self, *operands, **options):
        self.step = lambda e: e.tensor_copy(*operands, **options)

    def bn_stats(self, *operands, **options):
        self.step = lambda e: e.bn_stats(*operands, **options)

    def bn_aggr(self, *operands, **options):
        self.step = lambda e: e.bn_aggr(*operands, **options)

    def reciprocal(self, *operands, **options):
        self.step = lambda e: e.reciprocal(*operands, **options)

    def stream_shuffle(self, *operands, **options):
        self.step = lambda e: e.stream_shuffle(*operands, **options)


def later(emit):
    kept = Later()
    emit(kept)
    return kept.step


class Queue:

    def __init__(self, program, name):
        self.program, self.name = program, name
        self.steps, self.seen = [], {}
        self.stage, self.count = None, 0

    def begin(self, stage):
        self.stage, self.count = self.program.semaphore(f"{self.name}_{stage}"), 0

    def wait(self, *marks):
        for mark in marks:
            if mark is None:
                continue
            if isinstance(mark, list):
                self.wait(*mark)
                continue
            sem, value = mark
            if self.seen.get(id(sem), 0) < value:
                self.seen[id(sem)] = value
                self.steps.append(lambda e, s=sem, v=value: e.wait_ge(s, v))

    def do(self, emit):
        self.count += 1
        step = later(emit)
        self.steps.append(lambda e, s=self.stage: step(e).then_inc(s, 1))
        return (self.stage, self.count)

    def quiet(self, emit):
        self.steps.append(later(emit))

    def run(self, engine):
        for step in self.steps:
            step(engine)


class Unit:

    def __init__(self, pieces, after=None, gate=None, whole=False, zero=False, into=None, size=UNIT):
        self.pieces, self.after, self.gate, self.whole = pieces, after, gate, whole
        self.zero, self.into, self.size = zero, into, size
        self.hi = self.lo = self.both = self.raw = self.ready = None


class Program:
    def __init__(self, nc, a, out):
        self.nc, self.a, self.out = nc, a, out
        self.stack = ExitStack()
        self.pe, self.act, self.dve = Queue(self, "pe"), Queue(self, "act"), Queue(self, "dve")
        self.pool, self.sp = Queue(self, "pool"), Queue(self, "sp")

    def semaphore(self, name):
        return self.stack.enter_context(self.nc.semaphore(name))

    def sbuf(self, name, shape, dtype=F32, stack=None):
        return (stack or self.stack).enter_context(self.nc.sbuf_tensor(name, shape, dtype))

    def scratch(self, name, shape):
        return self.nc.dram_tensor(name, shape, F32, kind="Internal").ap()

    def allocate(self):
        sb = self.sbuf
        self.col_at, self.col_groups, n_cols = vector_columns()
        self.ident = sb("ident", [P, P])
        self.ones = sb("ones", [P, P])
        self.cols = sb("cols", [P, n_cols])
        self.cc = sb("cc", [P, KT, 2])
        self.mod = sb("mod", [P, DEPTH, 48])
        self.mod_ctx = sb("mod_ctx", [P, 16])
        self.eps = sb("eps", [P, 3])
        self.small = sb("small", [P, N_SMALL, 16])
        self.lam = sb("lam", [P, 8])
        self.softplus = sb("softplus", [P, 8, 4])
        self.sumsq = sb("sumsq", [P, TT, HEADS])
        self.U_meta_hi = sb("U_meta_hi", [P, KT, META], F32R)
        self.U_meta_lo = sb("U_meta_lo", [P, KT, META], F32R)
        self.temp = [sb(f"temp{i}", [P, CH]) for i in range(N_TEMP)]
        self.temp_free = [[] for _ in range(N_TEMP)]
        self.temp_next = 0
        self.raw = [sb(f"raw{i}", [P, UNIT]) for i in range(N_RAW)]
        self.split_slot = [sb(f"split{i}", [P, 2, UNIT], F32R) for i in range(N_SPLIT)]

        with ExitStack() as s:
            sb("U_lo_first", [P, KT, CH], stack=s)
            self.XH = [None, None]
            self.XH[0] = sb("XH0", [P, TPC, D], stack=s)
            sb("U_hi_first", [P, KT, CH], stack=s)
            self.XH[1] = sb("XH1", [P, TPC, D], stack=s)
        with ExitStack() as s:
            sb("U_lo_all", [P, NCH, KT, CH], stack=s)
            sb("U_hi_conv", [P, 4, CH], stack=s)
            prob02 = sb("prob02", [P, KEYS], stack=s)[:]
        self.U_lo = sb("U_lo", [P, NCH, KT, CH], F32R)
        self.U_hi = sb("U_hi", [P, NCH, KT, CH], F32R)

        with ExitStack() as s:
            self.prob0 = [sb(f"prob0{i}", [P, KEYS], stack=s)[:] for i in range(2)]
            self.prob1 = [sb(f"prob1{i}", [P, KEYS], stack=s)[:] for i in range(2)]
            self.PT_hi = sb("PT_hi", [P, KEYS // P, P], F32R, stack=s)
            self.PT_lo = sb("PT_lo", [P, KEYS // P, P], F32R, stack=s)
        self.prob0.append(prob02)
        with ExitStack() as s:
            self.conv_gc = sb("conv_gc", [P, T], stack=s)
            self.gv = sb("conv_gv", [P, T + 2], stack=s)
            self.cv = sb("conv_cv", [P, T], stack=s)
            self.cv2 = sb("conv_cv2", [P, T], stack=s)
        self.H = sb("H", [P, TT, D])

        with ExitStack() as s:
            self.Uc_hi = sb("Uc_hi", [P, KT, CTX], F32R, stack=s)
            self.Uc_lo = sb("Uc_lo", [P, KT, CTX], F32R, stack=s)
            self.rope_cos = sb("rope_cos", [P, T], stack=s)
            self.rope_sin = sb("rope_sin", [P, T], stack=s)
            self.stage_buf = [sb(f"stage{i}", [P, CH], stack=s) for i in range(4)]
        with ExitStack() as s:
            self.XHc = sb("XHc", [P, CTT, D], stack=s)
            self.ctx_raw = sb("ctx_raw", [P, CTT, D], stack=s)
            self.ada_x = sb("ada_x", [P, 2, UNIT], stack=s)
            self.ada_c = sb("ada_c", [P, 2, UNIT], stack=s)
        with ExitStack() as s:
            self.O = sb("O", [P, TT, HEADS * P], stack=s)
            self.conv_in = sb("conv_in", [P, 4, T], stack=s)
        with ExitStack() as s:
            self.XHall = sb("XHall", [P, TT, D], stack=s)
        with ExitStack() as s:
            self.table_hi = sb("table_hi", [P, UNIT], F32R, stack=s)
            self.table_lo = sb("table_lo", [P, UNIT], F32R, stack=s)
            self.PQ_hi = sb("PQ_hi", [P, 8, 2 * P], F32R, stack=s)
            self.PQ_lo = sb("PQ_lo", [P, 8, 2 * P], F32R, stack=s)
            self.chan_raw = sb("chan_raw", [P, 2 * P], stack=s)
            self.chan_hi = sb("chan_hi", [P, 2 * P], F32R, stack=s)
            self.chan_lo = sb("chan_lo", [P, 2 * P], F32R, stack=s)
        with ExitStack() as s:
            self.gated = [sb(f"gated{i}", [P, TM + 14], stack=s) for i in range(2)]
            self.dw = [sb(f"dw{i}", [P, T], stack=s) for i in range(2)]
            self.xc = [sb(f"xc{i}", [P, TM], stack=s) for i in range(4)]
            self.cx = sb("cx", [P, TM + 3], stack=s)
            self.work = sb("work", [P, TM], stack=s)
        with ExitStack() as s:
            self.meta_raw = sb("meta_raw", [META, D], stack=s)
            self.meta_hat = sb("meta_hat", [META, D], stack=s)
        self.A_hi = sb("A_hi", [P, FB, T], F32R)
        self.A_lo = sb("A_lo", [P, FB, T], F32R)
        self.row_gate = sb("row_gate", [P, D])
        self.row_g = sb("row_g", [P, D])
        self.row_b = sb("row_b", [P, D])

        self.psum = self.stack.enter_context(self.nc.psum_tensor("psum", [P, 8, CH], F32))
        self.bank_free = [[] for _ in range(8)]
        self.bank_next = 0
        self.small_next = 0
        self.d_q = self.scratch("d_q", (HEADS, P, T))
        self.d_k = self.scratch("d_k", (HEADS, P, T))
        self.d_kc = self.scratch("d_kc", (HEADS, P, CTX))
        self.d_v = self.scratch("d_v", (KEYS, HEADS * P))
        self.d_conv = self.scratch("d_conv", (4, P, T))
        self.d_pool = self.scratch("d_pool", (2, P, TM))
        self.d_gelu = self.scratch("d_gelu", (4, P, TM))
        self.s_raw = [[self.semaphore(f"s_raw{i}"), 0] for i in range(N_RAW)]
        self.s_store = [[self.semaphore(f"s_store{i}"), 0] for i in range(4)]

    def take_bank(self, n=None):
        if n is None:
            n = self.bank_next
            self.bank_next = (n + 1) % 8
        self.pe.wait(*self.bank_free[n])
        self.bank_free[n] = []
        return n

    def take_temp(self, *queues):
        n = self.temp_next
        self.temp_next = (n + 1) % N_TEMP
        for q in queues:
            q.wait(*self.temp_free[n])
        self.temp_free[n] = []
        return n

    def take_small(self):
        n = self.small_next
        self.small_next = (n + 1) % N_SMALL
        return self.small[:, n, :]

    def columns(self, name, i=0, n=1):
        at = self.col_at[name] + i
        return self.cols[:, at:at + n]

    def dma(self, queue, sem, dst, src):
        sem[1] += 16
        queue.steps.append(lambda e, s=sem[0]: e.dma_start(dst, src).then_inc(s, 16))
        return (sem[0], sem[1])

    def load(self, name, dst, src, *after, queue=None):
        queue = queue or self.pool
        queue.wait(*after)
        return self.dma(queue, [self.semaphore("s_" + name), 0], dst, src)

    def weights_begin(self, units):
        self.units = units
        self.raw_free = [[] for _ in range(N_RAW)]
        self.split_free = [[] for _ in range(N_SPLIT)]
        self.raw_marks = {}
        self.n_rows = 0
        self.n_load = self.n_split = self.n_take = self.n_slot = 0

    def pump(self):
        moved = True
        while moved:
            moved = False
            if self.n_load < len(self.units):
                u, slot = self.units[self.n_load], self.n_load % N_RAW
                after = u.after() if u.after else []
                if self.raw_free[slot] is not None and after is not None:
                    self.sp.wait(*self.raw_free[slot], *after)
                    self.raw_free[slot] = None
                    u.raw = self.raw[slot]
                    if u.zero:
                        self.dve.wait(*self.zero_after(slot))
                        self.sp.wait(self.dve.do(lambda e, r=u.raw: e.memset(r[:], 0.0)))
                    for dst, src in u.pieces:
                        u.ready = self.dma(self.sp, self.s_raw[slot], dst(u.raw), src)
                    u.loaded_slot = slot
                    self.n_load += 1
                    moved = True
            if self.n_split < self.n_load:
                u = self.units[self.n_split]
                if u.whole:
                    self.n_split += 1
                    moved = True
                    continue
                gate = u.gate() if u.gate else ()
                if gate is None:
                    continue
                if u.into:
                    got = u.into()
                    if got is None:
                        continue
                    hi, lo, free = got
                else:
                    slot = self.n_slot % N_SPLIT
                    if self.split_free[slot] is None:
                        continue
                    free = self.split_free[slot]
                    hi, lo = self.split_slot[slot][:, 0, :], self.split_slot[slot][:, 1, :]
                    u.both = self.split_slot[slot]
                    self.split_free[slot] = None
                    u.slot = slot
                    self.n_slot += 1
                n, raw = u.size, u.raw
                source = [u.ready]
                if gate:
                    row, made = gate
                    self.dve.wait(u.ready, made)
                    source = [self.dve.do(lambda e, r=raw, g=row: e.tensor_tensor(r[:], r[:], g[:], ALU.mult))]
                self.act.wait(*source, *free)
                m_hi = self.act.do(lambda e, h=hi, r=raw, n=n: e.copy(h[:, 0:n], r[:, 0:n]))
                self.dve.wait(*source, *free, m_hi)
                m_lo = self.dve.do(lambda e, h=hi, l=lo, r=raw, n=n: e.tensor_tensor(
                    l[:, 0:n], r[:, 0:n], h[:, 0:n].bitcast(F32), ALU.subtract))
                u.hi, u.lo, u.ready = hi, lo, [m_hi, m_lo]
                self.raw_marks[u.loaded_slot] = [m_hi, m_lo]
                self.raw_free[u.loaded_slot] = [m_hi, m_lo]
                self.n_split += 1
                moved = True

    def zero_after(self, slot):
        return self.raw_marks.get(slot, [])

    def take_unit(self, wait=True):
        self.pump()
        u = self.units[self.n_take]
        assert u.raw is not None and (u.whole or u.hi is not None), self.n_take
        self.n_take += 1
        if wait:
            self.pe.wait(*(u.ready if isinstance(u.ready, list) else [u.ready]))
        return u

    def release(self, u, mark):
        if u.whole:
            self.raw_free[u.loaded_slot] = list(mark)
            self.raw_marks[u.loaded_slot] = list(mark)
        elif not u.into:
            self.split_free[u.slot] = [mark]
        self.pump()

    def passes(self, out, l_hi, l_lo, r_hi, r_lo, start, stop):
        pe = self.pe
        pe.quiet(lambda e: e.matmul(out, l_hi, r_hi, start=start, stop=False))
        pe.quiet(lambda e: e.matmul(out, l_hi, r_lo, start=False, stop=False))
        last = lambda e: e.matmul(out, l_lo, r_hi, start=False, stop=stop)
        if stop:
            return pe.do(last)
        pe.quiet(last)
        return None

    def split(self, src, hi, lo, ready, free=()):
        self.act.wait(*ready, *free)
        m_hi = self.act.do(lambda e: e.copy(hi, src))
        self.dve.wait(*ready, *free, m_hi)
        m_lo = self.dve.do(lambda e: e.tensor_tensor(lo, src, hi.bitcast(F32), ALU.subtract))
        return [m_hi, m_lo]

    def statistics(self, src, rows, width, ready, rms=False, eps=0):
        dve, act = self.dve, self.act
        s = self.take_small()
        dve.wait(*ready)
        n = (width + CH - 1) // CH
        for i in range(n):
            m = dve.do(lambda e, i=i: e.bn_stats(s[0:rows, 6 * i:6 * i + 6], src[:, i * CH:min(width, (i + 1) * CH)]))
        dve.wait(m)
        mean, var, std, scale = (s[0:rows, 12 + i:13 + i] for i in range(4))
        m = dve.do(lambda e: e.bn_aggr(s[0:rows, 12:14], s[0:rows, 0:6 * n]))
        if rms:
            dve.wait(m)
            m = dve.do(lambda e: e.scalar_tensor_tensor(var, mean, mean, var, ALU.mult, ALU.add))
        act.wait(m)
        m = act.do(lambda e: e.activation(std, var, ACT.Sqrt, bias=self.eps[0:rows, eps:eps + 1]))
        dve.wait(m)
        m = dve.do(lambda e: e.reciprocal(scale, std))
        if rms:
            return scale, self.eps[0:rows, 2:3], [m]
        dve.wait(m)
        m = dve.do(lambda e: e.scalar_tensor_tensor(std, mean, -1.0, scale, ALU.mult, ALU.mult))
        return scale, std, [m]

    def normalize(self, src, dst, rows, ready, free=(), rms=False):
        scale, bias, got = self.statistics(src, rows, D, ready, rms)
        self.act.wait(*got, *free)
        return self.act.do(lambda e: e.activation(dst, src, ACT.Identity, bias=bias, scale=scale))

    def transpose_chunk(self, c, XH, ready, scale, shift, u_free, fold=None):
        pe, act, dve = self.pe, self.act, self.dve
        pe.wait(*ready)
        banks, marks = [], []
        for k in range(KT):
            b = self.take_bank()
            for i in range(TPC):
                emit = lambda e, b=b, i=i, k=k: e.transpose(self.psum[:, b, i * P:(i + 1) * P],
                                                            XH[:, i, k * P:(k + 1) * P], self.ident[:])
                if i < TPC - 1:
                    pe.quiet(emit)
            marks.append(pe.do(emit))
            banks.append(b)
        out = []
        for k, b in enumerate(banks):
            done = marks[-1] if c == 1 else marks[k]
            t = self.take_temp(act)
            v = self.temp[t]
            hi, lo = self.U_hi[:, c, k, :], self.U_lo[:, c, k, :]
            act.wait(done, *u_free)
            m_v = act.do(lambda e, v=v, b=b, k=k: e.activation(v[:], self.psum[:, b, :], ACT.Identity,
                                                               bias=shift(k), scale=scale(k)))
            self.bank_free[b] = [m_v]
            m = self.split(v[:], hi, lo, [m_v], u_free)
            self.temp_free[t] = m
            out += m
        return out

    def ada_take(self, layer, part, accumulators):
        u = self.take_unit(wait=False)
        k = self.ada_k
        marks = []
        dve, act, pool = self.dve, self.act, self.pool
        for acc, cond, free in accumulators:
            c = self.cc[:, k, cond:cond + 1]
            first = act if cond else dve
            if k == 0:
                first.wait(u.ready, self.cc_ready, *free)
                if cond:
                    m = act.do(lambda e: e.activation(acc, u.raw[:], ACT.Copy, scale=c))
                else:
                    m = dve.do(lambda e: e.tensor_scalar(acc, u.raw[:], c, None, ALU.mult))
                marks.append(m)
            elif cond:
                for half in range(2):
                    s = slice(half * CH, (half + 1) * CH)
                    t = self.take_temp(act)
                    v = self.temp[t]
                    act.wait(u.ready)
                    m = act.do(lambda e: e.activation(v[:], u.raw[:, s], ACT.Copy, scale=c))
                    marks.append(m)
                    pool.wait(m, self.ada_last[cond])
                    m = pool.do(lambda e: e.tensor_tensor(acc[:, s], acc[:, s], v[:], ALU.add))
                    self.temp_free[t] = [m]
            else:
                dve.wait(u.ready, self.ada_last[cond])
                m = dve.do(lambda e: e.scalar_tensor_tensor(acc, u.raw[:], c, acc, ALU.mult, ALU.add))
                marks.append(m)
            self.ada_last[cond] = m
        self.ada_k = (k + 1) % KT
        self.release(u, marks)
        return [self.ada_last[cond] for _, cond, _ in accumulators]

    def ada_sum(self, layer, part, accumulators, ready):
        pe, dve = self.pe, self.dve
        pe.wait(*ready, self.ones_ready)
        b = self.take_bank()
        for cond, (acc, _, _) in enumerate(accumulators):
            for i in range(KT):
                mark = pe.do(lambda e: e.matmul(self.psum[:, b, KT * cond + i:KT * cond + i + 1],
                                                acc[:, i * P:(i + 1) * P], self.ones[:, 0:1], start=True, stop=True))
        dve.wait(mark, self.cols_ready)
        bias = self.columns("ada_b", 48 * layer + KT * part, KT)
        one = 1.0 if part in (1, 4) else 0.0
        for cond, mod in enumerate((self.mod[:, layer], self.mod_ctx)[:len(accumulators)]):
            dst = mod[:, KT * part:KT * part + KT]
            m = dve.do(lambda e: e.scalar_tensor_tensor(dst, self.psum[:, b, KT * cond:KT * cond + KT], one, bias,
                                                        ALU.add, ALU.add))
        self.bank_free[b] = [m]
        self.mod_ready[(layer, part)] = m
        return mark

    def ada_fill(self, n):
        if self.ada_pending:
            layer, part, slot, ready = self.ada_pending
            self.ada_used[slot] = [self.ada_sum(layer, part, [(self.ada_acc[slot][:], 0, [])], ready)]
            self.ada_pending = None
        for _ in range(n):
            if not self.ada_parts:
                return
            layer, part = self.ada_parts[0]
            slot = part % 2
            ready = self.ada_take(layer, part, [(self.ada_acc[slot][:], 0, self.ada_used[slot] + self.rows_used)])
            if self.ada_k == 0:
                self.ada_parts.pop(0)
                self.ada_pending = (layer, part, slot, ready)

    def gate_row(self, layer, which):
        pe, act, dve = self.pe, self.act, self.dve
        col = 24 * which + 16
        ready = self.mod_ready[(layer, col // 8)]
        banks = [self.take_bank(), self.take_bank()]
        for k in range(KT):
            t = self.take_temp(dve)
            v = self.temp[t]
            dve.wait(ready)
            m = dve.do(lambda e, v=v, k=k: e.tensor_scalar(v[:, 0:P], self.ones[:],
                                                           self.mod[:, layer, col + k:col + k + 1], None, ALU.mult))
            pe.wait(m)
            m = pe.do(lambda e, v=v, k=k: e.matmul(self.psum[:, banks[k // 4], (k % 4) * P:(k % 4 + 1) * P],
                                                   v[:, 0:P], self.ident[:], start=True, stop=True))
            self.temp_free[t] = [m]
        act.wait(m, *self.gate_used)
        for i in range(2):
            m = act.do(lambda e, i=i: e.copy(self.row_gate[:, i * CH:(i + 1) * CH], self.psum[:, banks[i], :]))
            self.bank_free[banks[i]] = [m]
        self.gate_ready[(layer, which)] = m

    def up_group(self, n, chunk_ready, evacuate, before_chunk=None, chunk_major=False, extra=None,
                 beside=None):
        units = []
        order = [(i, c) for c in range(NCH) for i in range(n)] if chunk_major else \
                [(i, c) for i in range(n) for c in range(NCH)]
        for i, c in order:
            if before_chunk and chunk_major and i == 0:
                before_chunk(c)
            if i == len(units):
                units.append(self.take_unit())
            u = units[i]
            W_hi = u.hi[:].rearrange("p (k m) -> p k m", k=KT)
            W_lo = u.lo[:].rearrange("p (k m) -> p k m", k=KT)
            if beside and c == (NCH - 1 if chunk_major else 0):
                beside(i)
            self.pe.wait(*chunk_ready(c))
            b = self.take_bank()
            for k in range(KT):
                mark = self.passes(self.psum[:, b, :], W_hi[:, k, :], W_lo[:, k, :], self.U_hi[:, c, k, :],
                                   self.U_lo[:, c, k, :], k == 0, k == KT - 1)
            self.u_read = mark
            evacuate(i, c, b, mark)
            if c == NCH - 1:
                if extra:
                    mark = extra(i, W_hi, W_lo)
                self.release(u, mark)

    def down_block(self, lhs, lhs_ready, alpha=1.0, after_tile=None, beside=None):
        pe, dve = self.pe, self.dve
        units = [self.take_unit(wait=False) for _ in range(FB)]
        for tt in range(TT):
            if beside and tt < TT - 1:
                beside(tt)
            banks = [self.take_bank(), self.take_bank()]
            for j in range(FB):
                pe.wait(*units[j].ready, *lhs_ready(j, tt))
                l_hi, l_lo = lhs(j, tt)
                for half in range(2):
                    s = slice(half * CH, (half + 1) * CH)
                    mark = self.passes(self.psum[:, banks[half], :], l_hi, l_lo, units[j].hi[:, s], units[j].lo[:, s],
                                       j == 0, j == FB - 1)
                    if j == FB - 1:
                        dve.wait(mark, *self.h_ready[tt])
                        h = self.H[:, tt, s]
                        acc = self.psum[:, banks[half], :]
                        if alpha == 1.0:
                            m = dve.do(lambda e, h=h, acc=acc: e.tensor_tensor(h, h, acc, ALU.add))
                        else:
                            m = dve.do(lambda e, h=h, acc=acc: e.scalar_tensor_tensor(h, h, alpha, acc, ALU.mult, ALU.add))
                        self.bank_free[banks[half]] = [m]
            self.h_ready[tt] = [m]
            self.tile_read[tt] = mark
            if tt == TT - 1:
                for u in units:
                    self.release(u, mark)
            if after_tile:
                after_tile(tt)
        return mark

    def mlp(self, name, chunk_ready, before_chunk, fill=None, after_tile=None, alpha=1.0, gate=None):
        for q in (self.pe, self.act, self.dve):
            q.begin(name)
        ready = {}

        def evacuate(j, c, b, mark):
            act, dve = self.act, self.dve
            t1, t2 = self.take_temp(act), self.take_temp(dve)
            r, a = self.temp[t1], self.temp[t2]
            act.wait(mark)
            m_r = act.do(lambda e: e.activation(r[:], self.psum[:, b, :], ACT.Relu))
            self.bank_free[b] = [m_r]
            dve.wait(m_r)
            m_a = dve.do(lambda e: e.tensor_tensor(a[:], r[:], r[:], ALU.mult))
            self.temp_free[t1] = [m_a]
            s = slice(c * CH, (c + 1) * CH)
            m = self.split(a[:], self.A_hi[:, j, s], self.A_lo[:, j, s], [m_a], self.a_read)
            self.temp_free[t2] = m
            ready[(j, c)] = m

        blocks = D_FF // (P * FB)
        for blk in range(blocks):
            self.up_group(FB, chunk_ready, evacuate, before_chunk if blk == 0 else None, chunk_major=(blk == 0))
            if gate and blk == 0:
                self.gate_row(*gate)
            last = blk == blocks - 1
            mark = self.down_block(
                lambda j, tt: (self.A_hi[:, j, tt * P:(tt + 1) * P], self.A_lo[:, j, tt * P:(tt + 1) * P]),
                lambda j, tt: ready[(j, tt // TPC)], alpha if blk == 0 else 1.0,
                after_tile if last else None, (lambda tt: fill(1)) if fill and not last else None)
            self.a_read = [mark]

    def u_lhs(self, first):
        return lambda j, tt: (self.U_hi[:, tt // TPC, first + j, (tt % TPC) * P:(tt % TPC + 1) * P],
                              self.U_lo[:, tt // TPC, first + j, (tt % TPC) * P:(tt % TPC + 1) * P])

    def boundary(self, post, rms, scale, shift, from_u=False, fourier=False):
        state = {"xh": [None] * TT, "chunk": [[], []], "todo": []}
        rows_ready = self.load_rows(*post) if post else []
        self.tile_read = {}
        u_read = [self.u_read]
        place = [self.XHall[:, 0:TPC] if from_u else self.XH[0], self.XH[1]]
        if fourier:
            place = [self.XHall[:, 0:TPC], self.XHall[:, TPC:TT]]

        def pre_norm(tt, h, ready, norm):
            sc, bi, got = norm
            c = tt // TPC
            if fourier or (from_u and c == 1):
                free = [self.tile_read[TT - 1]]
            else:
                free = self.a_read if from_u else u_read
            self.act.wait(*got, *free)
            m = self.act.do(lambda e: e.activation(place[c][:, tt % TPC, :], h, ACT.Identity, bias=bi, scale=sc))
            state["xh"][tt] = m
            self.h_ready[tt] = ready + [m]

        def after_tile(tt):
            h = self.H[:, tt, :]
            ready = self.h_ready[tt]
            if post:
                m = self.normalize(h, h, P, ready)
                self.dve.wait(m, *rows_ready)
                m = self.dve.do(lambda e: e.tensor_tensor(h, h, self.row_g[:], ALU.mult))
                self.dve.wait(m)
                m = self.dve.do(lambda e: e.tensor_tensor(h, h, self.row_b[:], ALU.add))
                self.rows_used = [m]
                ready = self.h_ready[tt] = [m]
            norm = self.statistics(h, P, D, ready, rms)
            if fourier or (from_u and tt >= TPC):
                state["todo"].append((tt, h, ready, norm))
            else:
                pre_norm(tt, h, ready, norm)
            if tt == TT - 1:
                for late in state["todo"]:
                    pre_norm(*late)

        def make(c):
            u_free = [self.tile_read[c * TPC + TPC - 1]] if from_u else u_read
            state["chunk"][c] = self.transpose_chunk(c, place[c], state["xh"][c * TPC:(c + 1) * TPC], scale, shift,
                                                     u_free)

        return after_tile, make, lambda c: state["chunk"][c], state["xh"]

    def load_rows(self, g, b):
        n = self.n_rows = self.n_rows + 1
        return [self.load(f"row_g{n}", self.row_g[:], g.partition_broadcast(P), *self.rows_used, self.ada_used[0]),
                self.load(f"row_b{n}", self.row_b[:], b.partition_broadcast(P), *self.rows_used, self.ada_used[1])]

    def plan_units(self):
        a = self.a
        units = []

        def up(w, col):
            v = w[:, col:col + P].rearrange("(k p) m -> p k m", p=P)
            return Unit([(lambda r: r[:].rearrange("p (k m) -> p k m", k=KT), v)])

        def down(w, row, gate=None):
            return Unit([(lambda r: r[:], w[row:row + P, :])], gate=gate)

        def ada(layer, part):
            return [Unit([(lambda r: r[:], a["ada_w"][layer, k * P:(k + 1) * P, part * UNIT:(part + 1) * UNIT])],
                         whole=True) for k in range(KT)]

        def gate(layer, which):
            def ask():
                m = self.gate_ready.get((layer, which))
                return None if m is None else (self.row_gate, m)
            return ask

        def mlp(w1, w2, g=None, fill=None):
            for blk in range(D_FF // (P * FB)):
                for j in range(FB):
                    units.append(up(w1, (blk * FB + j) * P))
                for j in range(FB):
                    units.append(down(w2, (blk * FB + j) * P, g))
                if fill and blk < D_FF // (P * FB) - 1:
                    fill(TT - 1)

        units += ada(0, 1) + ada(0, 0)
        w_in = a["w_in"][0]
        rest = [u for part in range(2, 6) for u in ada(0, part)]
        layer1 = [u for part in range(6) for u in ada(1, part)]

        def ada_fill(n, of):
            for _ in range(min(n, len(of))):
                units.append(of.pop(0))
        for i in range(4):
            units.append(up(w_in, Q0 + i * P))
        for i in range(4):
            units.append(up(w_in, K0 + i * P))
            ada_fill(2, rest)
        for i in range(4):
            v = w_in[2 * i * P:(2 * i + 2) * P, V0:V0 + 512].rearrange("(k p) n -> p k n", p=P)
            units.append(Unit([(lambda r: r[:].rearrange("p (k n) -> p k n", k=2), v)]))
        for i in range(4):
            for part in (1, 2, 0):
                units.append(up(w_in, part * D_CONV + i * P))
                ada_fill(2, rest)
        for h in range(HEADS):
            stored = lambda key: (lambda: self.stored.get(key))
            units.append(Unit([(lambda r: r[:], self.d_q[h])], after=stored(("q", h))))
            units.append(Unit([(lambda r: r[:], self.d_k[h])], after=stored(("k", h))))
            v = self.d_v[:, h * P:(h + 1) * P].rearrange("(k p) n -> p k n", p=P)
            units.append(Unit([(lambda r: r[:, 0:256], self.d_kc[h]),
                               (lambda r: r[:, 256:512].rearrange("p (k n) -> p k n", k=2), v[:, TT:TT + CTT, :])],
                              after=stored("ctx"), size=512))
            units.append(Unit([(lambda r: r[:].rearrange("p (k n) -> p k n", k=TT), v[:, 0:TT, :])],
                              after=stored("v")))
        for k in range(KT):
            units.append(down(a["w_out_mix"][0], k * P, gate(0, 0)))
        mlp(a["mlp_w1"][0], a["mlp_w2"][0], gate(0, 1), lambda n: ada_fill(n, layer1))
        for i in range(6):
            into = (lambda: None if self.table_free is None else (self.table_hi, self.table_lo, self.table_free)) \
                if i == 5 else None
            units.append(Unit([(lambda r: r[:], a["dft"][i])], into=into))
        for k in range(KT):
            units.append(down(a["w_out_fourier"][0], k * P, gate(1, 0)))
        mlp(a["mlp_w1"][1], a["mlp_w2"][1], gate(1, 1))
        w = a["w_in_2"][0]
        for m in (4, 5, 2, 3, 10, 11, 12, 13, 0, 1, 6, 7, 8, 9):
            units.append(up(w, m * P))
        pieces = []
        for e in range(2):
            s = slice(64 * e, 64 * e + 64)
            pieces.append((lambda r, s=s: r[s, 0:256].rearrange("p (j n) -> p j n", j=2)[:, :, s],
                           a["pool_w_2"][0].rearrange("(j e) c d -> e c j d", e=2)[e]))
        pieces.append((lambda r: r[:, 256:768].rearrange("p (k n) -> p k n", k=2),
                       a["convb_pw_w_2"][0].rearrange("(k p) n -> p k n", p=P)))
        units.append(Unit(pieces, zero=True, size=768))
        pieces = []
        for i, name in enumerate(("rg_w_a_2", "rg_w_x_2")):
            for e in range(2):
                s = slice(64 * e, 64 * e + 64)
                pieces.append((lambda r, s=s, i=i: r[s, 512 * i:512 * i + 512].rearrange("p (j n) -> p j n", j=4)[:, :, s],
                               a[name][0].rearrange("(j e) c d -> e c j d", e=2)[e]))
        units.append(Unit(pieces, zero=True))
        for k in range(KT):
            units.append(down(a["w_out_2"][0], k * P))
        mlp(a["w_up_2"][0], a["w_down_2"][0])
        return units

    def start(self):
        pe, act, dve, pool, a = self.pe, self.act, self.dve, self.pool, self.a
        for q in (pe, act, dve, pool):
            q.begin("start")
        self.gate_ready, self.mod_ready, self.stored = {}, {}, {}
        self.gate_used, self.rows_used, self.a_read = [], [], []
        self.table_free = None
        self.tile_read = {}
        self.u_read = None
        vec_loaded, at = [], 0
        for g, (names, used) in enumerate(self.col_groups):
            vec_loaded.append(self.dma(self.sp, [self.semaphore(f"s_vectors{g}"), 0], self.conv_gather(g)[0:used, :],
                                       a["vectors"][at:at + used, :]))
            at += used
        m = pool.do(lambda e: e.memset(self.ident[:], 0.0))
        pool.wait(m)
        self.ident_ready = pool.do(lambda e: e.affine_select(
            out=self.ident[:], in_=self.ident[:], compare_op=ALU.not_equal, fill=1.0, base=0,
            pattern=[[-1, P]], channel_multiplier=1))
        m = dve.do(lambda e: e.memset(self.ones[:], 1.0))
        for i, v in enumerate((1e-6, 1e-5, 0.0)):
            m_eps = dve.do(lambda e, i=i, v=v: e.memset(self.eps[:, i:i + 1], v))
        self.ones_ready = m_eps
        act.wait(m_eps)
        x = a["x"][0].rearrange("(t p) d -> p t d", p=P)
        self.h_ready = []
        for t in range(TT):
            self.h_ready.append([self.load(f"x{t}", self.H[:, t, :], x[:, t, :], queue=act)])
        ctx = a["ctx"][0].rearrange("(t p) d -> p t d", p=P)
        ctx_loaded = self.load("ctx", self.ctx_raw[:], ctx, queue=act)
        lq_loaded = self.load("lambda", self.temp[4][:, 0:256],
                              a["lambda_qk"][0].rearrange("a d -> (a d)").partition_broadcast(P))
        pe.wait(self.ident_ready, *vec_loaded)
        at = 0
        for g, (names, used) in enumerate(self.col_groups):
            b = self.take_bank()
            m = pe.do(lambda e, g=g, b=b, used=used: e.transpose(self.psum[:, b, 0:used], self.conv_gather(g)[0:used, :],
                                                                 self.ident[0:used, 0:used]))
            dve.wait(m)
            m = dve.do(lambda e, b=b, used=used, at=at: e.tensor_copy(self.cols[:, at:at + used], self.psum[:, b, 0:used]))
            self.bank_free[b] = [m]
            at += used
        self.cols_ready = m
        act.wait(m)
        act.do(lambda e: e.activation(self.cc[:, :, 0], self.columns("c", 0, 8), ACT.Silu))
        self.cc_ready = act.do(lambda e: e.activation(self.cc[:, :, 1], self.columns("c_ctx", 0, 8), ACT.Silu))
        lq = self.temp[4]
        dve.wait(lq_loaded)
        v = lq[:, 0:256].rearrange("p (a b d) -> p a b d", a=2, b=2)
        m = dve.do(lambda e: e.tensor_tensor(lq[:, 256:384].rearrange("p (a d) -> p a d", a=2), v[:, :, 0, :], v[:, :, 1, :], ALU.mult))
        dve.wait(m)
        m = dve.do(lambda e: e.tensor_reduce(self.lam[:, 0:2], lq[:, 256:384].rearrange("p (a d) -> p a d", a=2), AX_X, ALU.add))
        self.temp_free[4] = [m]
        act.wait(m)
        m = act.do(lambda e: e.activation(self.lam[:, 2:4], self.lam[:, 0:2], ACT.Exp))
        dve.wait(m)
        m = dve.do(lambda e: e.tensor_tensor(self.lam[:, 4:5], self.lam[:, 3:4], self.lam[:, 2:3], ALU.subtract))
        dve.wait(m)
        self.lam_ready = dve.do(lambda e: e.tensor_scalar(self.lam[:, 4:5], self.lam[:, 4:5], -LAM_INIT, None, ALU.add))
        xh = [None] * TT
        self.ada_k, self.ada_last, self.ada_pending = 0, [None, None], None
        self.ada_acc, self.ada_used = (self.row_g, self.row_b), [[], []]
        self.ada_parts = [(0, part) for part in range(2, 6)] + [(1, part) for part in range(6)]
        xhc = [self.normalize(self.ctx_raw[:, t, :], self.XHc[:, t, :], P, [ctx_loaded]) for t in range(CTT)]
        for t in range(TT):
            xh[t] = self.normalize(self.H[:, t, :], self.XH[t // TPC][:, t % TPC, :], P, self.h_ready[t])
            self.h_ready[t] = self.h_ready[t] + [xh[t]]
        for n, part in enumerate((1, 0)):
            acc = [(self.ada_x[:, n, :], 0, []), (self.ada_c[:, n, :], 1, [])]
            for _ in range(KT):
                ready = self.ada_take(0, part, acc)
            self.ada_sum(0, part, acc, ready)
        self.start_done = (pe.stage, pe.count)
        return xh, xhc

    def conv_gather(self, g):
        return self.temp[g][:, 0:P]

    def project_attention(self, xh, xhc):
        pe, act, dve, pool, a = self.pe, self.act, self.dve, self.pool, self.a
        for q in (pe, act, dve, pool):
            q.begin("project")
        mod_done = [self.mod_ready[(0, 0)], self.mod_ready[(0, 1)]]
        act.wait(*mod_done)
        scale = lambda k: self.mod[:, 0, 8 + k:9 + k]
        shift = lambda k: self.mod[:, 0, k:k + 1]
        pe.wait(*xhc)
        uc_ready = []
        banks = []
        for k in range(KT):
            if k % 2 == 0:
                b = self.take_bank()
            for t in range(CTT):
                m = pe.do(lambda e, b=b, k=k, t=t: e.transpose(
                    self.psum[:, b, (k % 2) * CTX + t * P:(k % 2) * CTX + (t + 1) * P],
                    self.XHc[:, t, k * P:(k + 1) * P], self.ident[:]))
            banks.append(b)
        all_read = m
        for k in range(KT):
            t = self.take_temp(act)
            v, b = self.temp[t], banks[k]
            act.wait(all_read)
            m_v = act.do(lambda e, v=v, b=b, k=k: e.activation(
                v[:, 0:CTX], self.psum[:, b, (k % 2) * CTX:(k % 2 + 1) * CTX], ACT.Identity,
                bias=self.mod_ctx[:, k:k + 1], scale=self.mod_ctx[:, 8 + k:9 + k]))
            self.bank_free[b] = [m_v]
            m = self.split(v[:, 0:CTX], self.Uc_hi[:, k, :], self.Uc_lo[:, k, :], [m_v], [all_read])
            self.temp_free[t] = m
            uc_ready += m
        rope_loaded = [self.load("rope_cos", self.rope_cos[:], a["rope_cos"], all_read),
                       self.load("rope_sin", self.rope_sin[:], a["rope_sin"], all_read)]
        chunk = [[], []]

        def before_chunk(c):
            chunk[c] = self.transpose_chunk(c, self.XH[c], xh[c * TPC:(c + 1) * TPC], scale, shift, [])

        stage_next, stage_free = [0], [[all_read], [all_read], [all_read], [all_read]]

        def take_stage(*queues):
            n = stage_next[0]
            stage_next[0] = (n + 1) % 4
            for q in queues:
                q.wait(*stage_free[n])
            return n

        def store(n, dst, src, ready):
            pool.wait(*ready)
            m = self.dma(pool, self.s_store[n], dst, src)
            stage_free[n] = [m]
            return m

        swap = [(i + 16) % 32 for i in range(32)]

        def rope(dram):
            marks = {}

            def evacuate(i, c, b, mark):
                s = slice(c * CH, (c + 1) * CH)
                t1, t2 = self.take_temp(dve), self.take_temp(dve)
                sw, xcos = self.temp[t1], self.temp[t2]
                x = self.psum[:, b, :]
                act_copy = act
                act_copy.wait(mark, *self.temp_free[t2])
                n = take_stage(act, dve)
                st = self.stage_buf[n]
                m_x = act.do(lambda e: e.copy(st[:], x))
                self.bank_free[b] = [m_x]
                dve.wait(m_x, *rope_loaded)
                m = dve.do(lambda e: e.stream_shuffle(sw[:], st[:], swap))
                m2 = dve.do(lambda e: e.tensor_tensor(xcos[:], st[:], self.rope_cos[:, s], ALU.mult))
                dve.wait(m)
                m = dve.do(lambda e: e.tensor_tensor(sw[:], sw[:], self.rope_sin[:, s], ALU.mult))
                dve.wait(m, m2)
                m = dve.do(lambda e: e.tensor_tensor(st[:], sw[:], xcos[:], ALU.add))
                self.temp_free[t1] = self.temp_free[t2] = [m]
                marks.setdefault(i, []).append(store(n, dram(i)[:, s], st[:], [m]))
            return evacuate, marks

        evac_q, q_marks = rope(lambda i: self.d_q[i])
        self.up_group(4, lambda c: chunk[c], evac_q, before_chunk, chunk_major=True)
        for h in range(HEADS):
            self.stored[("q", h)] = q_marks[h]

        kc_marks = []

        def keys_of_context(i, W_hi, W_lo):
            pe.wait(*uc_ready)
            b = self.take_bank()
            for k in range(KT):
                mark = self.passes(self.psum[:, b, 0:CTX], W_hi[:, k, :], W_lo[:, k, :], self.Uc_hi[:, k, :],
                                   self.Uc_lo[:, k, :], k == 0, k == KT - 1)
            n = take_stage(act)
            act.wait(mark)
            m = act.do(lambda e: e.copy(self.stage_buf[n][:, 0:CTX], self.psum[:, b, 0:CTX]))
            self.bank_free[b] = [m]
            kc_marks.append(store(n, self.d_kc[self.head], self.stage_buf[n][:, 0:CTX], [m]))
            return mark

        for h in range(HEADS):
            self.head = h
            evac_k, k_marks = rope(lambda i, h=h: self.d_k[h])
            self.up_group(1, lambda c: chunk[c], evac_k, extra=keys_of_context,
                          beside=lambda i: self.ada_fill(2))
            self.stored[("k", h)] = k_marks[0]
        units = [self.take_unit() for _ in range(4)]
        v_marks = []
        for t in range(TT + CTT):
            b = self.take_bank()
            for k in range(KT):
                u = units[k // 2]
                s = slice((k % 2) * CH, (k % 2 + 1) * CH)
                if t < TT:
                    l = [U[:, t // TPC, k, (t % TPC) * P:(t % TPC + 1) * P] for U in (self.U_hi, self.U_lo)]
                else:
                    l = [U[:, k, (t - TT) * P:(t - TT + 1) * P] for U in (self.Uc_hi, self.Uc_lo)]
                mark = self.passes(self.psum[:, b, :], l[0], l[1], u.hi[:, s], u.lo[:, s], k == 0, k == KT - 1)
            n = take_stage(act)
            act.wait(mark)
            m = act.do(lambda e, n=n, b=b: e.copy(self.stage_buf[n][:], self.psum[:, b, :]))
            self.bank_free[b] = [m]
            v_marks.append(store(n, self.d_v[t * P:(t + 1) * P, :], self.stage_buf[n][:], [m]))
        for u in units:
            self.release(u, mark)
        self.stored["v"] = v_marks[-4:] 
        self.stored["ctx"] = kc_marks[-1:] + v_marks[-4:]
        h_read = [m for r in self.h_ready for m in r]
        dve.wait(*h_read)
        zero = dve.do(lambda e: e.memset(self.gv[:, 0:1], 0.0))
        zero = dve.do(lambda e: e.memset(self.gv[:, T + 1:T + 2], 0.0))
        state = {"gc": [], "gv": [], "free_gc": h_read, "free_gv": [], "free_cv": [[], []], "cv": None}
        conv_marks = []
        self.stored["conv"] = conv_marks
        for i in range(4):
            cv = (self.cv, self.cv2)[i % 2]

            def evac(part, c, b, mark, i=i, cv=cv):
                s = slice(c * CH, (c + 1) * CH)
                x = self.psum[:, b, :]
                if part == 0:
                    act.wait(mark, *state["free_gc"])
                    m = act.do(lambda e: e.copy(self.conv_gc[:, s], x))
                    state["gc"] = [m]
                elif part == 1:
                    dve.wait(mark, *state["gc"], *state["free_gv"])
                    m = dve.do(lambda e: e.tensor_tensor(self.gv[:, 1 + c * CH:1 + (c + 1) * CH], x, self.conv_gc[:, s], ALU.mult))
                    state["free_gc"] = [m]
                    if c == 1:
                        w = [self.columns("conv_w", 4 * tap + i) for tap in range(3)]
                        dve.wait(m, zero, *state["free_cv"][i % 2])
                        mm = dve.do(lambda e: e.tensor_scalar(cv[:], self.gv[:, 0:T], w[0], None, ALU.mult))
                        for tap in (1, 2):
                            dve.wait(mm)
                            mm = dve.do(lambda e, tap=tap: e.scalar_tensor_tensor(
                                cv[:], self.gv[:, tap:tap + T], w[tap], cv[:], ALU.mult, ALU.add))
                        state["free_gv"] = state["cv"] = [mm]
                else:
                    n = take_stage(dve)
                    st = self.stage_buf[n]
                    dve.wait(mark, *state["cv"])
                    m = dve.do(lambda e: e.tensor_tensor(st[:], x, cv[:, s], ALU.mult))
                    state["free_cv"][i % 2] = [m]
                    conv_marks.append(store(n, self.d_conv[i, :, s], st[:], [m]))
                self.bank_free[b] = [m]

            self.up_group(3, lambda c: chunk[c], evac, beside=lambda i: self.ada_fill(2))
        self.ada_fill(0)
        self.h_region_free = list(state["free_cv"][0]) + list(state["free_cv"][1]) + state["free_gc"]
        self.stage_all = [m for s in stage_free for m in s]
        self.uc_read = mark
        self.project_done = self.u_read

    def attention(self):
        pe, act, dve, pool = self.pe, self.act, self.dve, self.pool
        for q in (pe, act, dve, pool):
            q.begin("attention")
        T_BANKS = (5, 6, 7)
        scale = QK ** -0.5
        conv_loaded = self.load("conv_in", self.conv_in[:], self.d_conv.rearrange("k p t -> p k t"),
                                self.project_done, self.uc_read, *self.stage_all, *self.stored["conv"])
        act.wait(self.project_done, self.uc_read, *self.stage_all, *self.h_region_free)
        dve.wait(self.project_done, self.uc_read, *self.stage_all, *self.h_region_free)
        flat = self.psum[:, 0:5, :].rearrange("p b n -> p (b n)")
        S = [flat[:, 0:KEYS], flat[:, KEYS:2 * KEYS]]
        units = {}
        o_read = []
        prev = None
        prob0_free, prob1_free = [[], [], []], [[], []]
        pt_free = []
        conv_done = []
        T_PARTS = ((0, 4), (4, 4), (8, 2))
        o_marks = [[] for _ in range(TT)]

        def scores(h, qt, places):
            if qt == 0 and h not in units:
                units[h] = [self.take_unit() for _ in range(3)]
            uq, uk, uc = units[h][:3]
            for c, b, of_context, first, at in places:
                s = slice(64 * c, 64 * c + 64)
                src, n = (uc, CTX) if of_context else (uk, CH)
                if (c, b) == (1, 2):
                    pe.wait(mark)
                else:
                    self.take_bank(b)
                mark = self.passes(flat[:, at:at + n], uq.hi[s, qt * P:(qt + 1) * P],
                                   uq.lo[s, qt * P:(qt + 1) * P], src.hi[s, first:first + n],
                                   src.lo[s, first:first + n], True, True)
            return mark

        FIRST_SCORES = ((0, 0, False, 0, 0), (0, 1, False, 512, 512), (0, 2, True, 0, 1024), (1, 2, True, 0, 1280))
        SECOND_SCORES = ((1, 3, False, 0, 1536), (1, 4, False, 512, 2048))

        def maximum(c, ready):
            sm = self.take_small()
            dve.wait(*ready)
            m = dve.do(lambda e: e.tensor_reduce(sm[:, 0:1], S[c], AX_X, ALU.max))
            dve.wait(m)
            return sm, dve.do(lambda e: e.tensor_scalar(sm[:, 1:2], sm[:, 0:1], -scale, None, ALU.mult))

        def exponential(c, i, sm, m):
            numerators, free = ((self.prob0, prob0_free), (self.prob1, prob1_free))[c]
            n = i % len(numerators)
            act.wait(m, *free[n])
            m = act.do(lambda e: e.activation(numerators[n], S[c], ACT.Exp, bias=sm[:, 1:2], scale=scale,
                                              accum_out=sm[:, 2:3]))
            for b in ((0, 1), (2, 3, 4))[c]:
                self.bank_free[b] = [m]
            return m

        def coefficients(sm0, sm1, m0, m1):
            dve.wait(m0, m1, self.lam_ready)
            m = dve.do(lambda e: e.reciprocal(sm1[:, 3:4], sm1[:, 2:3]))
            m_r0 = dve.do(lambda e: e.reciprocal(sm0[:, 3:4], sm0[:, 2:3]))
            dve.wait(m)
            m = dve.do(lambda e: e.scalar_tensor_tensor(sm1[:, 4:5], sm1[:, 3:4], sm0[:, 2:3], self.lam[:, 4:5],
                                                        ALU.mult, ALU.mult))
            return sm1[:, 4:5], m, sm0[:, 3:4], m_r0

        def mix(i, coefficient, m, r0, m_r0):
            p0, p1 = self.prob0[i % 3], self.prob1[i % 2]
            act.wait(m)
            m = act.do(lambda e: e.activation(p1, p1, ACT.Copy, scale=coefficient))
            pool.wait(m)
            pool.do(lambda e: e.tensor_tensor(p0[:, 0:T], p0[:, 0:T], p1[:, CTX:KEYS], ALU.add))
            m = pool.do(lambda e: e.tensor_tensor(p0[:, T:KEYS], p0[:, T:KEYS], p1[:, 0:CTX], ALU.add))
            prob1_free[i % 2] = [m]
            return m, r0, m_r0

        def transposes(i, mixed):
            p0 = self.prob0[i % 3]
            pe.wait(mixed)
            marks = []
            for (first, n), b in zip(T_PARTS, T_BANKS):
                self.take_bank(b)
                for k in range(n):
                    m = pe.do(lambda e: e.transpose(self.psum[:, b, k * P:(k + 1) * P],
                                                    p0[:, (first + k) * P:(first + k + 1) * P], self.ident[:]))
                marks.append(m)
            prob0_free[i % 3] = [m]
            return marks

        def split_transposed(marks):
            places = []
            for (first, n), b, m in zip(T_PARTS, T_BANKS, marks):
                s = slice(first, first + n)
                src = self.psum[:, b, 0:n * P]
                hi, lo = (x[:, s, :].rearrange("p k n -> p (k n)") for x in (self.PT_hi, self.PT_lo))
                act.wait(m, *pt_free)
                places.append((src, hi, lo, b, act.do(lambda e: e.copy(hi, src))))

            def low():
                ready = []
                for src, hi, lo, b, m_hi in places:
                    dve.wait(m_hi)
                    m_lo = dve.do(lambda e: e.tensor_tensor(lo, src, hi.bitcast(F32), ALU.subtract))
                    self.bank_free[b] = [m_hi, m_lo]
                    ready.append([m_hi, m_lo])
                return ready
            return low

        def values(h, qt, ready, r0, m_r0):
            nonlocal pt_free
            uc, uv = units[h][2], units[h][3]
            self.take_bank(5)
            for k in range(KEYS // P):
                pe.wait(*ready[k // 4])
                v, at = (uv, k * P) if k < TT else (uc, 256 + (k - TT) * P)
                v = v.both[:, :, at:at + P]
                both = self.psum[:, 5, 0:2 * P].rearrange("p (a n) -> p a n", a=2)
                pe.quiet(lambda e: e.matmul(both, self.PT_hi[:, k, :], v, start=k == 0, stop=False))
                mark = pe.do(lambda e: e.matmul(both, self.PT_lo[:, k, :], v, start=False, stop=k == KEYS // P - 1))
            pt_free = [mark]
            t = self.take_temp(act)
            low = self.temp[t][:, 0:P]
            act.wait(mark, m_r0)
            m = act.do(lambda e: e.activation(low, self.psum[:, 5, P:2 * P], ACT.Copy, scale=r0))
            dve.wait(m)
            m = dve.do(lambda e: e.scalar_tensor_tensor(self.O[:, qt, h * P:(h + 1) * P], self.psum[:, 5, 0:P], r0, low,
                                                        ALU.mult, ALU.add))
            self.temp_free[t] = self.bank_free[5] = [m]
            o_marks[qt] = [m]
            if qt == TT - 1:
                self.release(uc, mark)
                self.release(uv, mark)

        def squares(qt):
            t = self.take_temp(dve)
            sq = self.temp[t]
            o = self.O[:, qt, :]
            dve.wait(*o_marks[qt])
            m = dve.do(lambda e: e.tensor_tensor(sq[:], o, o, ALU.mult))
            dve.wait(m)
            m = dve.do(lambda e: e.tensor_reduce(self.sumsq[:, qt, :], sq[:].rearrange("p (h d) -> p h d", h=HEADS),
                                                 AX_X, ALU.add))
            self.temp_free[t] = [m]
            o_marks[qt] = [m]

        steps = [(h, qt) for h in range(HEADS) for qt in range(TT)]
        sums, mixed = {}, {}
        for i in range(len(steps) + 2):
            now = steps[i] if i < len(steps) else None
            old = steps[i - 2] if i >= 2 else None
            if now:
                m = scores(*now, FIRST_SCORES)
                sm0, m_max = maximum(0, [m])
            if i - 1 in sums:
                mixed[i - 1] = mix(i - 1, *sums.pop(i - 1))
            if old:
                m, r0, m_r0 = mixed.pop(i - 2)
                low = split_transposed(transposes(i - 2, m))
            if now:
                m0 = exponential(0, i, sm0, m_max)
                m_second = scores(*now, SECOND_SCORES)
                if now[1] == TT - 1:
                    self.release(units[now[0]][0], m_second)
                    self.release(units[now[0]][1], m_second)
            if old:
                got = low()
            if now:
                sm1, m = maximum(1, [m_second, m0])
                m1 = exponential(1, i, sm1, m)
            if old:
                if old[1] == 0:
                    units[old[0]].append(self.take_unit())
                values(*old, got, r0, m_r0)
            if now:
                sums[i] = coefficients(sm0, sm1, m0, m1)
            if old and old[0] == HEADS - 1:
                squares(old[1])
            if 4 <= i < 12:
                k, c = (i - 4) // 2, (i - 4) % 2
                conv_done += self.split(self.conv_in[:, k, c * CH:(c + 1) * CH], self.U_hi[:, c, k, :],
                                        self.U_lo[:, c, k, :], [conv_loaded, self.project_done])
        self.bank_next = 0
        last_values = pt_free
        x = self.a["x"][0].rearrange("(t p) d -> p t d", p=P)
        free = [*prob0_free, *prob1_free, pt_free]
        for t in range(TT):
            self.h_ready[t] = [self.load(f"xx{t}", self.H[:, t, :], x[:, t, :], *free)]
        return conv_done, o_marks

    def attention_out(self, conv_done, o_marks):
        pe, act, dve = self.pe, self.act, self.dve
        ss = self.sumsq[:].rearrange("p t h -> p (t h)")
        act.wait(*[m for ms in o_marks for m in ms])
        m = act.do(lambda e: e.activation(ss, ss, ACT.Sqrt, bias=self.eps[:, 1:2], scale=1.0 / P))
        dve.wait(m)
        m_r = dve.do(lambda e: e.reciprocal(ss, ss))
        g = self.softplus[:, 7, 0:1]
        m_g = dve.do(lambda e: e.tensor_scalar(g, self.columns("subln_g"), 1.0 - LAM_INIT, None, ALU.mult))
        act.wait(m_g)
        normed = []
        dve.wait(m_r)
        for t in range(TT):
            o = self.O[:, t, :].rearrange("p (h d) -> p h d", h=HEADS)
            normed.append(dve.do(lambda e, o=o, t=t: e.tensor_tensor(
                o, o, self.sumsq[:, t, :].unsqueeze(2).to_broadcast([P, HEADS, P]), ALU.mult)))
        self.down_block(self.u_lhs(0), lambda j, tt: conv_done, ALPHA)
        ready = []
        for c in range(NCH):
            for h in range(HEADS):
                b = self.take_bank()
                pe.wait(*normed[c * TPC:(c + 1) * TPC])
                for i in range(TPC):
                    m = pe.do(lambda e, b=b, i=i, h=h, c=c: e.transpose(
                        self.psum[:, b, i * P:(i + 1) * P], self.O[:, c * TPC + i, h * P:(h + 1) * P], self.ident[:]))
                t = self.take_temp(act)
                v = self.temp[t]
                act.wait(m)
                m = act.do(lambda e, v=v, b=b: e.activation(v[:], self.psum[:, b, :], ACT.Copy, scale=g))
                self.bank_free[b] = [m]
                m = self.split(v[:], self.U_hi[:, c, 4 + h, :], self.U_lo[:, c, 4 + h, :], [m])
                self.temp_free[t] = m
                ready.append(m)
        return ready

    def fourier(self, xh, chunk_unused=None):
        pe, act, dve = self.pe, self.act, self.dve
        for q in (pe, act, dve):
            q.begin("fourier")
        scale = lambda k: self.mod[:, 1, 8 + k:9 + k]
        shift = lambda k: self.mod[:, 1, k:k + 1]
        act.wait(self.mod_ready[(1, 0)], self.mod_ready[(1, 1)])
        u_ready = {}
        for k in range(KT):
            vs = []
            for c in range(2):
                b = self.take_bank()
                pe.wait(*xh[c * TPC:(c + 1) * TPC])
                for i in range(TPC):
                    m = pe.do(lambda e, b=b, i=i, c=c, k=k: e.transpose(
                        self.psum[:, b, i * P:(i + 1) * P], self.XHall[:, c * TPC + i, k * P:(k + 1) * P], self.ident[:]))
                self.xh_read = m
                t = self.take_temp(act)
                act.wait(m)
                m = act.do(lambda e, t=t, b=b, k=k: e.activation(self.temp[t][:], self.psum[:, b, :], ACT.Identity,
                                                                 bias=shift(k), scale=scale(k)))
                self.bank_free[b] = [m]
                vs.append((t, m))
            (t0, m0), (t1, m1) = vs
            v0, v1 = self.temp[t0], self.temp[t1]
            t2 = self.take_temp(dve)
            odd = self.temp[t2]
            dve.wait(m0, m1)
            m = dve.do(lambda e, odd=odd, v0=v0, v1=v1: e.tensor_tensor(odd[:], v0[:], v1[:], ALU.subtract))
            m_e = dve.do(lambda e, v0=v0, v1=v1: e.tensor_tensor(v0[:], v0[:], v1[:], ALU.add))
            ready = self.split(odd[:], self.U_hi[:, 0, k, :], self.U_lo[:, 0, k, :], [m, self.u_read])
            self.temp_free[t2] = ready
            q = CH // 2
            dve.wait(m_e)
            m = dve.do(lambda e, v0=v0, v1=v1: e.tensor_tensor(v1[:, 0:q], v0[:, 0:q], v0[:, q:CH], ALU.subtract))
            m2 = dve.do(lambda e, v0=v0, v1=v1: e.tensor_tensor(v1[:, q:CH], v0[:, 0:q], v0[:, q:CH], ALU.add))
            self.temp_free[t0] = [m2]
            got = self.split(v1[:], self.U_hi[:, 1, k, :], self.U_lo[:, 1, k, :], [m, m2, self.u_read])
            self.temp_free[t1] = got
            u_ready[k] = ready + got
        chan = self.load("chan", self.chan_raw[:], self.a["dft_chan"], self.xh_read)
        chan_ready = self.split(self.chan_raw[:], self.chan_hi[:], self.chan_lo[:], [chan, self.xh_read])
        self.table_free = [self.xh_read]
        tables = [self.take_unit() for _ in range(6)]
        pq_free, y_ready = [], []
        act.wait(self.xh_read)
        for g in range(KT):
            pe.wait(*chan_ready, *u_ready[g])
            pq_ready = []
            for half in range(2):
                for pair in range(2):
                    b = self.take_bank()
                    for i in range(2):
                        s = slice((2 * pair + i) * P, (2 * pair + i + 1) * P)
                        mark = self.passes(self.psum[:, b, i * 2 * P:(i + 1) * 2 * P], self.U_hi[:, half, g, s],
                                           self.U_lo[:, half, g, s], self.chan_hi[:], self.chan_lo[:], True, True)
                    at = 4 * half + 2 * pair
                    m = self.split(self.psum[:, b, :], self.PQ_hi[:, at:at + 2, :].rearrange("p a n -> p (a n)"),
                                   self.PQ_lo[:, at:at + 2, :].rearrange("p a n -> p (a n)"), [mark], pq_free)
                    self.bank_free[b] = m
                    pq_ready.append(m)
            u_taken = mark
            b_odd, b_even = self.take_bank(), self.take_bank()
            for cls, (tiles, first, n, b, col) in enumerate(((4, 0, CH, b_odd, 0), (2, 4, CH // 2, b_even, 0),
                                                             (2, 6, CH // 2, b_even, CH // 2))):
                for t in range(tiles):
                    pe.wait(*pq_ready[(first + t) // 2])
                    for cs in range(2):
                        if cls == 0:
                            r = [x[:, cs * CH:(cs + 1) * CH] for x in (tables[t].hi, tables[t].lo)]
                        else:
                            u = tables[3 + cls]
                            at = (2 * t + cs) * n
                            r = [x[:, at:at + n] for x in (u.hi, u.lo)]
                        l = [x[:, first + t, cs * P:(cs + 1) * P] for x in (self.PQ_hi, self.PQ_lo)]
                        mark = self.passes(self.psum[:, b, col:col + n], l[0], l[1], r[0], r[1],
                                           t == 0 and cs == 0, t == tiles - 1 and cs == 1)
                if cls == 0:
                    odd_done = mark
            pq_free = [mark]
            dst = lambda off, step: [x[:, :, g, off::step] for x in (self.U_hi, self.U_lo)]
            hi, lo = dst(1, 2)
            got = [self.split(self.psum[:, b_odd, :].rearrange("p (c n) -> p c n", c=2), hi, lo, [odd_done, u_taken])]
            evens = [(self.psum[:, b_even, i * 256:(i + 1) * 256].rearrange("p (c n) -> p c n", c=2), *dst(off, 4))
                     for i, off in ((0, 2), (1, 0))]
            act.wait(mark, u_taken)
            m_hi = [act.do(lambda e, src=src, hi=hi: e.copy(hi, src)) for src, hi, lo in evens]
            dve.wait(mark, u_taken, *m_hi)
            m_lo = [dve.do(lambda e, src=src, hi=hi, lo=lo: e.tensor_tensor(lo, src, hi.bitcast(F32), ALU.subtract))
                    for src, hi, lo in evens]
            got.append(m_hi + m_lo)
            self.bank_free[b_odd], self.bank_free[b_even] = got
            y_ready.append(got[0] + got[1])
        for u in tables:
            self.release(u, mark)
        self.a_read = [mark]
        self.gate_used = self.gate_used_now()
        return y_ready

    def gate_used_now(self):
        return [(self.dve.stage, self.dve.count)] if self.dve.count else []

    def mixers(self, chunk_ready, before_chunk):
        pe, act, dve, pool, a = self.pe, self.act, self.dve, self.pool, self.a
        for q in (pe, act, dve, pool):
            q.begin("mixers")
        region = [self.a_read, *[m for r in self.h_ready for m in r], self.rows_used]
        meta = self.load("meta", self.meta_raw[:], a["meta_tokens_2"], *region)
        act.wait(*region)
        dve.wait(*region)
        m = self.normalize(self.meta_raw[:], self.meta_hat[:], META, [meta], rms=True)
        pe.wait(m)
        b = self.take_bank()
        for k in range(KT):
            m = pe.do(lambda e, k=k: e.transpose(self.psum[:, b, k * META:(k + 1) * META],
                                                 self.meta_hat[:, k * P:(k + 1) * P], self.ident[0:META, 0:META]))
        t = self.take_temp(dve)
        v = self.temp[t]
        dve.wait(m)
        g = self.columns("mix_norm_g_2", 0, KT).unsqueeze(2).to_broadcast([P, KT, META])
        vv = v[:, 0:KT * META].rearrange("p (k m) -> p k m", k=KT)
        meta_read = m
        m = dve.do(lambda e: e.tensor_tensor(vv, self.psum[:, b, 0:KT * META].rearrange("p (k m) -> p k m", k=KT), g, ALU.mult))
        self.bank_free[b] = [m]
        meta_ready = self.split(vv, self.U_meta_hi[:], self.U_meta_lo[:], [m])
        self.temp_free[t] = meta_ready
        act.wait(meta_read)
        dve.wait(meta_read)
        for buf in self.gated:
            pad = dve.do(lambda e, buf=buf: e.memset(buf[:, 0:14], 0.0))
        pad = dve.do(lambda e: e.memset(self.cx[:, 0:3], 0.0))
        dve.wait(pad)

        background = []
        s_stage = [[self.semaphore(f"s_mix{i}"), 0] for i in range(2)]
        stage_free = [[], []]
        gated_m = [[], []]
        cx_m, cx_free, xc_m = [], [], {}
        work_free, dw_m, pool_m, gelu_m = [], [], [], []
        self.work_free = []

        def place(dst, off):
            return lambda c: dst[:, off:off + META] if c < 0 else dst[:, off + META + c * CH:off + META + (c + 1) * CH]

        def evac(unit, c, b, mark):
            n = META if c < 0 else CH
            x = self.psum[:, b, 0:n]
            if unit < 2:
                act.wait(mark)
                m = act.do(lambda e: e.activation(place(self.gated[unit], 14)(c), x, ACT.Sigmoid))
                gated_m[unit].append(m)
            elif unit < 4:
                dst = place(self.gated[unit - 2], 14)(c)
                dve.wait(mark, *gated_m[unit - 2])
                m = dve.do(lambda e: e.tensor_tensor(dst, x, dst, ALU.mult))
                gated_m[unit - 2].append(m)
            elif unit < 8:
                act.wait(mark, *cx_free)
                m = act.do(lambda e: e.copy(place(self.cx, 3)(c), x))
                cx_m.append(m)
            else:
                act.wait(mark, *self.work_free)
                f = ACT.Copy if unit < 10 else ACT.Gelu_apprx_tanh
                m = act.do(lambda e: e.activation(place(self.work, 0)(c), x, f))
                work_m.append(m)
            self.bank_free[b] = [m]

        work_m = []

        def taps(i):
            src, dst = self.gated[i], self.dw[i]

            def first():
                dve.wait(*gated_m[i])
                dw_m[:] = [dve.do(lambda e: e.tensor_scalar(dst[:], src[:, 0:T], self.columns("convb_dw_w_2", i),
                                                            self.columns("convb_dw_b_2", i), ALU.mult, ALU.add))]
            background.append(first)
            for tap in range(1, CONV_K):
                def one(tap=tap):
                    dve.wait(*dw_m)
                    dw_m[:] = [dve.do(lambda e: e.scalar_tensor_tensor(
                        dst[:], src[:, tap:tap + T], self.columns("convb_dw_w_2", 2 * tap + i), dst[:], ALU.mult, ALU.add))]
                background.append(one)

        def after_unit(unit):
            if unit == 3:
                taps(0)
                taps(1)
            if 4 <= unit < 8:
                j = unit - 4
                dst = self.xc[j]
                dve.wait(*cx_m)
                m = dve.do(lambda e: e.tensor_scalar(dst[:], self.cx[:, 0:TM], self.columns("rg_conv_w_2", j),
                                                     self.columns("rg_conv_b_2", j), ALU.mult, ALU.add))
                for tap in range(1, RG_K):
                    dve.wait(m)
                    m = dve.do(lambda e, tap=tap: e.scalar_tensor_tensor(
                        dst[:], self.cx[:, tap:tap + TM], self.columns("rg_conv_w_2", 4 * tap + j), dst[:], ALU.mult, ALU.add))
                cx_free[:] = [m]
                cx_m.clear()
                xc_m[j] = [m]
            if unit >= 8:
                i = unit - 8 if unit < 10 else unit - 10
                dram = self.d_pool[i] if unit < 10 else self.d_gelu[i]
                pool.wait(*work_m)
                m = self.dma(pool, s_stage[0], dram, self.work[:])
                (pool_m if unit < 10 else gelu_m).append(m)
                self.work_free = [m]
                work_m.clear()
            for _ in range(6):
                if background:
                    background.pop(0)()

        count = [0]

        def extra_at(first):
            def extra(i, W_hi, W_lo):
                pe.wait(*meta_ready)
                b = self.take_bank()
                for k in range(KT):
                    mark = self.passes(self.psum[:, b, 0:META], W_hi[:, k, :], W_lo[:, k, :], self.U_meta_hi[:, k, :],
                                       self.U_meta_lo[:, k, :], k == 0, k == KT - 1)
                evac(first + i, -1, b, mark)
                after_unit(first + i)
                return mark
            return extra

        self.up_group(4, chunk_ready, evac, before_chunk, chunk_major=True, extra=extra_at(0))
        for unit in range(4, 14):
            self.up_group(1, chunk_ready, lambda i, c, b, mark, unit=unit: evac(unit, c, b, mark), extra=extra_at(unit))
        u_done = self.u_read_all = (pe.stage, pe.count)
        while background:
            background.pop(0)()
        Yslot = lambda k, c: (self.U_hi[:, c, k, :], self.U_lo[:, c, k, :])
        unit_small = self.take_unit()
        unit_rg = self.take_unit()

        y_ready = {}
        gated_free = list(dw_m)
        L = TM
        for i in range(2):
            x_t = self.work
            pool.wait(*self.work_free, *pool_m)
            loaded = self.dma(pool, s_stage[0], self.work[:], self.d_pool[i])
            s_a, s_b = self.gated[0], self.gated[1]
            dve.wait(loaded, *gated_free)
            m = dve.do(lambda e: e.tensor_tensor(s_a[:, 1:L], x_t[:, 1:L], x_t[:, 0:L - 1], ALU.add))
            dve.wait(m)
            if i == 0:
                m = dve.do(lambda e: e.tensor_tensor(s_b[64:P, 3:L], s_a[64:P, 3:L], s_a[64:P, 1:L - 2], ALU.add))
                parts = ((0, s_a, 2), (64, s_b, 4))
            else:
                m = dve.do(lambda e: e.tensor_tensor(s_b[:, 3:L], s_a[:, 3:L], s_a[:, 1:L - 2], ALU.add))
                dve.wait(m)
                m = dve.do(lambda e: e.tensor_tensor(s_a[:, 7:L], s_b[:, 7:L], s_b[:, 3:L - 4], ALU.add))
                dve.wait(m)
                m = dve.do(lambda e: e.tensor_tensor(s_b[64:P, 15:L], s_a[64:P, 15:L], s_a[64:P, 7:L - 8], ALU.add))
                parts = ((0, s_a, 8), (64, s_b, 16))
            dve.wait(m)
            for p0, src, w in parts:
                m = dve.do(lambda e, p0=p0, src=src, w=w: e.scalar_tensor_tensor(
                    src[p0:p0 + 64, META:TM], src[p0:p0 + 64, META:TM], 1.0 / w, x_t[p0:p0 + 64, META:TM],
                    ALU.mult, ALU.subtract))
            dve.wait(m)
            m = dve.do(lambda e: e.tensor_copy(s_a[64:P, META:TM], s_b[64:P, META:TM]))
            self.work_free = [m]
            for c in range(NCH):
                hi, lo = Yslot(i, c)
                got = self.split(s_a[:, META + c * CH:META + (c + 1) * CH], hi, lo, [m], [u_done])
                gated_free = got
                b = self.take_bank()
                pe.wait(*got)
                mark = self.passes(self.psum[:, b, :], unit_small.hi[:, i * P:(i + 1) * P],
                                   unit_small.lo[:, i * P:(i + 1) * P], hi, lo, True, True)
                t = self.take_temp(act)
                act.wait(mark)
                mv = act.do(lambda e, t=t, b=b, i=i: e.activation(self.temp[t][:], self.psum[:, b, :], ACT.Copy,
                                                                  scale=self.columns("pool_scale_2", i)))
                self.bank_free[b] = [mv]
                got2 = self.split(self.temp[t][:], hi, lo, [mv, mark])
                self.temp_free[t] = got2
                y_ready[(i, c)] = got2
        for c in range(NCH):
            back = [self.take_bank(), self.take_bank()]
            for half in range(2):
                b = self.take_bank()
                pe.wait(*dw_m)
                for i in range(2):
                    for k in range(2):
                        s = slice(c * CH + (2 * half + i) * P, c * CH + (2 * half + i + 1) * P)
                        m = pe.do(lambda e, i=i, k=k, s=s, b=b: e.transpose(
                            self.psum[:, b, (2 * i + k) * P:(2 * i + k + 1) * P], self.dw[k][:, s], self.ident[:]))
                t = self.take_temp(act)
                v = self.temp[t]
                stats = [(self.psum[:, b, 2 * i * P:(2 * i + 2) * P], self.statistics(
                    self.psum[:, b, 2 * i * P:(2 * i + 2) * P], P, 2 * P, [m])) for i in range(2)]
                for i, (src, (sc, bi, _)) in enumerate(stats):
                    act.wait(*stats[1][1][2])
                    mn = act.do(lambda e, i=i, v=v, src=src, sc=sc, bi=bi: e.activation(
                        v[:, 2 * i * P:(2 * i + 2) * P], src, ACT.Identity, bias=bi, scale=sc))
                self.bank_free[b] = [mn]
                pe.wait(mn)
                for i in range(2):
                    for k in range(2):
                        m = pe.do(lambda e, i=i, k=k, v=v, half=half: e.transpose(
                            self.psum[:, back[k], (2 * half + i) * P:(2 * half + i + 1) * P],
                            v[:, (2 * i + k) * P:(2 * i + k + 1) * P], self.ident[:]))
                self.temp_free[t] = [m]
            z = []
            for k in range(2):
                t = self.take_temp(act)
                act.wait(m)
                mv = act.do(lambda e, t=t, k=k: e.activation(self.temp[t][:], self.psum[:, back[k], :], ACT.Silu,
                                                             bias=self.columns("convb_ln_b_2", k),
                                                             scale=self.columns("convb_ln_g_2", k)))
                self.bank_free[back[k]] = [mv]
                hi, lo = Yslot(2 + k, c)
                got = self.split(self.temp[t][:], hi, lo, [mv], [u_done])
                self.temp_free[t] = got
                z += got
            pe.wait(*z)
            outs = []
            for j in range(2):
                b = self.take_bank()
                for k in range(2):
                    s = slice(256 + k * 256 + j * P, 256 + k * 256 + (j + 1) * P)
                    hi, lo = Yslot(2 + k, c)
                    mark = self.passes(self.psum[:, b, :], unit_small.hi[:, s], unit_small.lo[:, s], hi, lo, k == 0, k == 1)
                outs.append(b)
            for j, b in enumerate(outs):
                hi, lo = Yslot(2 + j, c)
                got = self.split(self.psum[:, b, :], hi, lo, [mark])
                self.bank_free[b] = got
                y_ready[(2 + j, c)] = got
        self.release(unit_small, mark)
        sp = [self.softplus[:, i, :] for i in range(8)]
        lam = self.columns("rg_lambda_2", 0, 4)
        m = act.do(lambda e: e.activation(sp[0], lam, ACT.Abs))
        act.wait(m)
        m = act.do(lambda e: e.activation(sp[1], sp[0], ACT.Exp, scale=-1.0))
        dve.wait(m)

        def chain(emit):
            mm = dve.do(emit)
            dve.wait(mm)
            return mm
        chain(lambda e: e.tensor_scalar(sp[2], sp[1], 2.0, None, ALU.add))
        chain(lambda e: e.reciprocal(sp[2], sp[2]))
        chain(lambda e: e.tensor_tensor(sp[2], sp[2], sp[1], ALU.mult))
        chain(lambda e: e.tensor_tensor(sp[3], sp[2], sp[2], ALU.mult))
        chain(lambda e: e.memset(sp[4], 1.0 / 19))
        for n in (17, 15, 13, 11, 9, 7, 5, 3, 1):
            chain(lambda e: e.tensor_tensor(sp[4], sp[4], sp[3], ALU.mult))
            chain(lambda e, n=n: e.tensor_scalar(sp[4], sp[4], 1.0 / n, None, ALU.add))
        chain(lambda e: e.tensor_tensor(sp[4], sp[4], sp[2], ALU.mult))
        chain(lambda e: e.tensor_scalar(sp[5], lam, -1.0, 0.0, ALU.mult, ALU.max))
        chain(lambda e: e.scalar_tensor_tensor(sp[4], sp[4], 2.0, sp[5], ALU.mult, ALU.add))
        chain(lambda e: e.tensor_scalar(sp[5], sp[4], -RG_C, None, ALU.mult))
        c8 = chain(lambda e: e.tensor_scalar(sp[6], sp[4], RG_C, None, ALU.mult))
        act.wait(c8)
        w0, w1, w2, w3 = self.gated[0][:, 0:TM], self.gated[1][:, 0:TM], self.cx[:, 0:TM], self.work[:]
        parts = ((-1, 0, META), (0, META, CH), (1, META + CH, CH))
        free = [gated_free, cx_free, self.work_free]
        for j in range(4):
            xc = self.xc[j]
            ready = []
            for c, at, n in parts:
                hi, lo = Yslot(4 + j, c) if c >= 0 else (self.U_meta_hi[:, 4 + j, :], self.U_meta_lo[:, 4 + j, :])
                ready.append(self.split(xc[:, at:at + n], hi, lo, xc_m[j], [u_done]))
            sig = []
            for which, dst, bias in ((0, w0, "rg_b_a_2"), (1, w1, "rg_b_x_2")):
                for (c, at, n), got in zip(parts, ready):
                    hi, lo = Yslot(4 + j, c) if c >= 0 else (self.U_meta_hi[:, 4 + j, :], self.U_meta_lo[:, 4 + j, :])
                    pe.wait(*got)
                    b = self.take_bank()
                    s = slice(which * 512 + j * P, which * 512 + (j + 1) * P)
                    mark = self.passes(self.psum[:, b, 0:n], unit_rg.hi[:, s], unit_rg.lo[:, s], hi, lo, True, True)
                    act.wait(mark, *free)
                    m = act.do(lambda e, dst=dst, at=at, n=n, b=b, bias=bias, j=j: e.activation(
                        dst[:, at:at + n], self.psum[:, b, 0:n], ACT.Sigmoid, bias=self.columns(bias, j)))
                    self.bank_free[b] = [m]
                    sig.append(m)
            read = mark
            dve.wait(*sig)
            m_ix = dve.do(lambda e, xc=xc: e.tensor_tensor(w1, w1, xc[:], ALU.mult))
            m_a = None
            act.wait(*sig, *free)
            m_a = act.do(lambda e, j=j: e.activation(w2, w0, ACT.Exp, scale=sp[5][:, j:j + 1]))
            m_t = act.do(lambda e, j=j: e.activation(w3, w0, ACT.Tanh, scale=sp[6][:, j:j + 1]))
            dve.wait(m_a, m_t)
            m = chain(lambda e: e.tensor_tensor(w0, w2, w2, ALU.mult))
            m = chain(lambda e: e.scalar_tensor_tensor(w0, w0, 1.0, w3, ALU.add, ALU.mult))
            pool.wait(m, *gelu_m)
            gl = self.dma(pool, s_stage[1], w3, self.d_gelu[j])
            act.wait(m)
            m = act.do(lambda e: e.activation(w0, w0, ACT.Sqrt))
            dve.wait(m, m_ix)
            m = chain(lambda e: e.tensor_tensor(w1, w1, w0, ALU.mult))
            m = chain(lambda e: e.tensor_tensor_scan(w0, w2, w1, 0.0, ALU.mult, ALU.add))
            dve.wait(gl)
            m = chain(lambda e: e.tensor_tensor(w1, w0, w3, ALU.mult))
            for c in range(NCH):
                hi, lo = Yslot(4 + j, c)
                at = META + c * CH
                got = self.split(w1[:, at:at + CH], hi, lo, [m, read])
                y_ready[(4 + j, c)] = got
            free = [got]
        self.release(unit_rg, mark)
        self.a_read = [m, y_ready[(7, 1)], mark]
        return y_ready

    def finish(self):
        rows = [self.load("final_g", self.row_g[:], self.a["final_norm_g_2"].partition_broadcast(P), *self.rows_used,
                          self.a_read)]
        out = self.out[0].rearrange("(t p) d -> p t d", p=P)
        stores = []

        def after_tile(tt):
            h = self.H[:, tt, :]
            m = self.normalize(h, h, P, self.h_ready[tt], rms=True)
            self.dve.wait(m, *rows)
            m = self.dve.do(lambda e: e.tensor_tensor(h, h, self.row_g[:], ALU.mult))
            self.pool.wait(m)
            stores.append(self.dma(self.pool, [self.semaphore(f"s_out{tt}"), 0], out[:, tt, :], h))
            self.pool_last = stores
        return after_tile, stores

    def build(self):
        a = self.a
        modulation = lambda layer, which: (lambda k: self.mod[:, layer, 24 * which + 8 + k:24 * which + 9 + k],
                                           lambda k: self.mod[:, layer, 24 * which + k:24 * which + k + 1])
        gain = lambda name: (lambda k: self.columns(name, k), lambda k: self.eps[:, 2:3])
        self.allocate()
        self.weights_begin(self.plan_units())
        xh, xhc = self.start()
        self.project_attention(xh, xhc)
        self.gate_row(0, 0)
        conv_done, o_marks = self.attention()
        o_ready = self.attention_out(conv_done, o_marks)
        for q in (self.pe, self.act, self.dve):
            q.begin("mix_out")
        self.a_read = [m for ready in o_ready for m in ready]
        after, make, ready, _ = self.boundary((a["ln_g"][0, 0], a["ln_b"][0, 0]), False, *modulation(0, 1), from_u=True)
        self.down_block(self.u_lhs(4), lambda j, tt: o_ready[(tt // TPC) * HEADS + j], 1.0, after)
        self.a_read = []
        self.gate_used = self.gate_used_now()
        late = {}

        def then_fourier(tt):
            if tt == 0:
                self.ada_fill(0)
                late["b"] = self.boundary((a["ln_g"][0, 1], a["ln_b"][0, 1]), False, None, None, fourier=True)
            late["b"][0](tt)

        self.mlp("mlp0", ready, make, self.ada_fill, then_fourier, ALPHA, gate=(0, 1))
        self.gate_used = self.gate_used_now()
        self.gate_row(1, 0)
        y_ready = self.fourier(late["b"][3])
        self.down_block(self.u_lhs(0), lambda j, tt: y_ready[j], ALPHA)
        after, make, ready, _ = self.boundary((a["ln_g"][1, 0], a["ln_b"][1, 0]), False, *modulation(1, 1), from_u=True)
        self.down_block(self.u_lhs(4), lambda j, tt: y_ready[4 + j], 1.0, after)
        self.gate_used = self.gate_used_now()

        def then_mixers(tt):
            if tt == 0:
                late["b"] = self.boundary((a["ln_g"][1, 1], a["ln_b"][1, 1]), True, *gain("mix_norm_g_2"))
            late["b"][0](tt)
        self.mlp("mlp1", ready, make, None, then_mixers, ALPHA, gate=(1, 1))
        _, make, ready, _ = late["b"]
        y_ready = self.mixers(ready, make)
        self.down_block(self.u_lhs(0), lambda j, tt: y_ready[(j, tt // TPC)], 1.0)
        after, make, ready, _ = self.boundary(None, True, *gain("mlp_norm_g_2"), from_u=True)
        self.down_block(self.u_lhs(4), lambda j, tt: y_ready[(4 + j, tt // TPC)], 1.0, after)
        after_last, stores = self.finish()
        self.mlp("mlp2", ready, make, None, after_last)
        self.pool.wait(*stores)
        self.sp.wait(*stores)

    def run(self):
        nc = self.nc
        block = self.stack.enter_context(nc.Block())

        @block.sync
        def _(e):
            self.sp.run(e)

        @block.scalar
        def _(e):
            self.act.run(e)

        @block.vector
        def _(e):
            self.dve.run(e)

        @block.gpsimd
        def _(e):
            self.pool.run(e)

        @block.tensor
        def _(e):
            self.pe.run(e)


def build_program(nc, arrays, out):
    program = Program(nc, arrays, out)
    with program.stack:
        program.build()
        program.run()


def rope_tables():
    d = np.arange(P) % QK
    inv = (np.float32(10000.0) ** (-np.arange(16, dtype=np.float32) / np.float32(16))).astype(np.float32)
    tok = np.arange(T)
    pos = np.where((d < 32)[:, None], tok[None, :] // 64, tok[None, :] % 64).astype(np.float32)
    ang = (pos * inv[d % 16][:, None]).astype(np.float32).astype(np.float64)
    sign = np.where(d % 32 < 16, -1.0, 1.0)[:, None]
    return np.cos(ang).astype(np.float32), (np.sin(ang) * sign).astype(np.float32)


def dft_tables():
    out = np.zeros((6, P, UNIT), np.float32)
    n = np.arange(P)[:, None]
    for t in range(4):
        ang = 2 * np.pi * (((n + P * t) * (2 * np.arange(CH) + 1)[None, :]) % T) / T
        out[t] = np.concatenate([np.cos(ang), -np.sin(ang)], 1)
    for c, off in ((4, 2), (5, 0)):
        parts = []
        for t in range(2):
            ang = 2 * np.pi * (((n + P * t) * (4 * np.arange(CH // 2) + off)[None, :]) % T) / T
            parts += [np.cos(ang), -np.sin(ang)]
        out[c] = np.concatenate(parts, 1)
    ang = 2 * np.pi * ((n * np.arange(P)[None, :]) % P) / P
    chan = np.concatenate([np.cos(ang), np.sin(ang)], 1) / math.sqrt(T * P)
    return out, chan.astype(np.float32)


_WHOLE = ["x", "ctx", "ada_w", "ln_g", "ln_b", "mlp_w1", "mlp_w2", "w_in", "lambda_qk", "w_out_mix", "w_out_fourier",
          "meta_tokens_2", "w_in_2", "pool_w_2", "convb_pw_w_2", "rg_w_a_2", "rg_w_x_2", "w_out_2", "w_up_2",
          "w_down_2", "final_norm_g_2"]


def kernel(**inputs):
    import numpy as _np
    import concourse.bacc as _bacc
    from concourse import mybir as _mybir
    from concourse.bass_utils import run_bass_kernel_spmd as _run

    nc = _bacc.Bacc("TRN2", target_bir_lowering=False, num_devices=1)
    host = {name: _np.ascontiguousarray(inputs[name]) for name in _WHOLE}
    host["vectors"] = _np.concatenate([_np.ascontiguousarray(inputs[name]).reshape(rows, P) for name, rows in VECTORS])
    host["rope_cos"], host["rope_sin"] = rope_tables()
    host["dft"], host["dft_chan"] = dft_tables()
    arrays, aps = {}, {}
    for name, a in host.items():
        arrays[f"in_{name}_dram"] = a
        aps[name] = nc.dram_tensor(f"in_{name}_dram", a.shape, _mybir.dt.from_np(a.dtype), kind="ExternalInput").ap()
    out = nc.dram_tensor("out_0_dram", (1, T, D), _mybir.dt.float32, kind="ExternalOutput").ap()
    build_program(nc, aps, out)
    r = _run(nc, [arrays], core_ids=[0])
    return r.results[0]["out_0_dram"]
```

```python
import math
from contextlib import ExitStack

import numpy as np

import concourse.bass as bass
from concourse import mybir

P = 128
F32 = mybir.dt.float32
F32R = mybir.dt.float32r
ALU = mybir.AluOpType
ACT = mybir.ActivationFunctionType
AX_X = mybir.AxisListType.X

T = 1024
D = 1024
TT = T // P
KT = D // P
CH = 512
NCH = T // CH
TPC = CH // P
CTX = 256
CTT = CTX // P
D_FF = 4096
FB = 4
D_CONV = 512
Q0, K0, V0 = 3 * D_CONV, 3 * D_CONV + 512, 3 * D_CONV + 1024
HEADS = 4
QK = 64
KEYS = T + CTX
DEPTH = 2
ALPHA = (2.0 * DEPTH) ** 0.25
LAM_INIT = 0.2
META = 16
TM = T + META
CONV_K = 31
RG_K = 4
RG_C = 8.0
UNIT = 1024
N_RAW = 3
N_SPLIT = 5
N_TEMP = 5
N_SMALL = 24

VECTORS = [("c", 8), ("c_ctx", 8), ("conv_w", 12), ("subln_g", 1), ("mix_norm_g_2", 8), ("mlp_norm_g_2", 8),
           ("pool_scale_2", 2), ("convb_dw_b_2", 2), ("convb_ln_g_2", 2), ("convb_ln_b_2", 2),
           ("rg_conv_w_2", 16), ("rg_conv_b_2", 4), ("rg_b_a_2", 4), ("rg_b_x_2", 4), ("rg_lambda_2", 4),
           ("ada_b", 96), ("convb_dw_w_2", 62)]


def vector_columns():
    start, at, groups = {}, 0, []
    group, used = [], 0
    for name, rows in VECTORS:
        if used + rows > P:
            groups.append((group, used))
            at, group, used = at + used, [], 0
        start[name] = at + used
        group.append((name, rows, used))
        used += rows
    groups.append((group, used))
    return start, groups, at + used


class Later:

    def matmul(self, *operands, **options):
        self.step = lambda e: e.matmul(*operands, **options)

    def transpose(self, *operands, **options):
        self.step = lambda e: e.transpose(*operands, **options)

    def memset(self, *operands, **options):
        self.step = lambda e: e.memset(*operands, **options)

    def affine_select(self, *operands, **options):
        self.step = lambda e: e.affine_select(*operands, **options)

    def copy(self, *operands, **options):
        self.step = lambda e: e.copy(*operands, **options)

    def activation(self, *operands, **options):
        self.step = lambda e: e.activation(*operands, **options)

    def tensor_tensor(self, *operands, **options):
        self.step = lambda e: e.tensor_tensor(*operands, **options)

    def tensor_scalar(self, *operands, **options):
        self.step = lambda e: e.tensor_scalar(*operands, **options)

    def scalar_tensor_tensor(self, *operands, **options):
        self.step = lambda e: e.scalar_tensor_tensor(*operands, **options)

    def tensor_tensor_scan(self, *operands, **options):
        self.step = lambda e: e.tensor_tensor_scan(*operands, **options)

    def tensor_reduce(self, *operands, **options):
        self.step = lambda e: e.tensor_reduce(*operands, **options)

    def tensor_copy(self, *operands, **options):
        self.step = lambda e: e.tensor_copy(*operands, **options)

    def bn_stats(self, *operands, **options):
        self.step = lambda e: e.bn_stats(*operands, **options)

    def bn_aggr(self, *operands, **options):
        self.step = lambda e: e.bn_aggr(*operands, **options)

    def reciprocal(self, *operands, **options):
        self.step = lambda e: e.reciprocal(*operands, **options)

    def stream_shuffle(self, *operands, **options):
        self.step = lambda e: e.stream_shuffle(*operands, **options)


def later(emit):
    kept = Later()
    emit(kept)
    return kept.step


class Queue:

    def __init__(self, program, name):
        self.program, self.name = program, name
        self.steps, self.seen = [], {}
        self.stage, self.count = None, 0

    def begin(self, stage):
        self.stage, self.count = self.program.semaphore(f"{self.name}_{stage}"), 0

    def wait(self, *marks):
        for mark in marks:
            if mark is None:
                continue
            if isinstance(mark, list):
                self.wait(*mark)
                continue
            sem, value = mark
            if self.seen.get(id(sem), 0) < value:
                self.seen[id(sem)] = value
                self.steps.append(lambda e, s=sem, v=value: e.wait_ge(s, v))

    def do(self, emit):
        self.count += 1
        step = later(emit)
        self.steps.append(lambda e, s=self.stage: step(e).then_inc(s, 1))
        return (self.stage, self.count)

    def quiet(self, emit):
        self.steps.append(later(emit))

    def run(self, engine):
        for step in self.steps:
            step(engine)


class Unit:

    def __init__(self, pieces, after=None, gate=None, whole=False, zero=False, into=None, size=UNIT):
        self.pieces, self.after, self.gate, self.whole = pieces, after, gate, whole
        self.zero, self.into, self.size = zero, into, size
        self.hi = self.lo = self.both = self.raw = self.ready = None


class Program:
    def __init__(self, nc, a, out):
        self.nc, self.a, self.out = nc, a, out
        self.stack = ExitStack()
        self.pe, self.act, self.dve = Queue(self, "pe"), Queue(self, "act"), Queue(self, "dve")
        self.pool, self.sp = Queue(self, "pool"), Queue(self, "sp")

    def semaphore(self, name):
        return self.stack.enter_context(self.nc.semaphore(name))

    def sbuf(self, name, shape, dtype=F32, stack=None):
        return (stack or self.stack).enter_context(self.nc.sbuf_tensor(name, shape, dtype))

    def scratch(self, name, shape):
        return self.nc.dram_tensor(name, shape, F32, kind="Internal").ap()

    def allocate(self):
        sb = self.sbuf
        self.col_at, self.col_groups, n_cols = vector_columns()
        self.ident = sb("ident", [P, P])
        self.ones = sb("ones", [P, P])
        self.cols = sb("cols", [P, n_cols])
        self.cc = sb("cc", [P, KT, 2])
        self.mod = sb("mod", [P, DEPTH, 48])
        self.mod_ctx = sb("mod_ctx", [P, 16])
        self.eps = sb("eps", [P, 3])
        self.small = sb("small", [P, N_SMALL, 16])
        self.lam = sb("lam", [P, 8])
        self.softplus = sb("softplus", [P, 8, 4])
        self.sumsq = sb("sumsq", [P, TT, HEADS])
        self.U_meta_hi = sb("U_meta_hi", [P, KT, META], F32R)
        self.U_meta_lo = sb("U_meta_lo", [P, KT, META], F32R)
        self.temp = [sb(f"temp{i}", [P, CH]) for i in range(N_TEMP)]
        self.temp_free = [[] for _ in range(N_TEMP)]
        self.temp_next = 0
        self.raw = [sb(f"raw{i}", [P, UNIT]) for i in range(N_RAW)]
        self.split_slot = [sb(f"split{i}", [P, 2, UNIT], F32R) for i in range(N_SPLIT)]

        with ExitStack() as s:
            sb("U_lo_first", [P, KT, CH], stack=s)
            self.XH = [None, None]
            self.XH[0] = sb("XH0", [P, TPC, D], stack=s)
            sb("U_hi_first", [P, KT, CH], stack=s)
            self.XH[1] = sb("XH1", [P, TPC, D], stack=s)
        with ExitStack() as s:
            sb("U_lo_all", [P, NCH, KT, CH], stack=s)
            sb("U_hi_conv", [P, 4, CH], stack=s)
            prob02 = sb("prob02", [P, KEYS], stack=s)[:]
        self.U_lo = sb("U_lo", [P, NCH, KT, CH], F32R)
        self.U_hi = sb("U_hi", [P, NCH, KT, CH], F32R)

        with ExitStack() as s:
            self.prob0 = [sb(f"prob0{i}", [P, KEYS], stack=s)[:] for i in range(2)]
            self.prob1 = [sb(f"prob1{i}", [P, KEYS], stack=s)[:] for i in range(2)]
            self.PT_hi = sb("PT_hi", [P, KEYS // P, P], F32R, stack=s)
            self.PT_lo = sb("PT_lo", [P, KEYS // P, P], F32R, stack=s)
        self.prob0.append(prob02)
        with ExitStack() as s:
            self.conv_gc = sb("conv_gc", [P, T], stack=s)
            self.gv = sb("conv_gv", [P, T + 2], stack=s)
            self.cv = sb("conv_cv", [P, T], stack=s)
            self.cv2 = sb("conv_cv2", [P, T], stack=s)
        self.H = sb("H", [P, TT, D])

        with ExitStack() as s:
            self.Uc_hi = sb("Uc_hi", [P, KT, CTX], F32R, stack=s)
            self.Uc_lo = sb("Uc_lo", [P, KT, CTX], F32R, stack=s)
            self.rope_cos = sb("rope_cos", [P, T], stack=s)
            self.rope_sin = sb("rope_sin", [P, T], stack=s)
            self.stage_buf = [sb(f"stage{i}", [P, CH], stack=s) for i in range(4)]
        with ExitStack() as s:
            self.XHc = sb("XHc", [P, CTT, D], stack=s)
            self.ctx_raw = sb("ctx_raw", [P, CTT, D], stack=s)
            self.ada_x = sb("ada_x", [P, 2, UNIT], stack=s)
            self.ada_c = sb("ada_c", [P, 2, UNIT], stack=s)
        with ExitStack() as s:
            self.O = sb("O", [P, TT, HEADS * P], stack=s)
            self.conv_in = sb("conv_in", [P, 4, T], stack=s)
        with ExitStack() as s:
            self.XHall = sb("XHall", [P, TT, D], stack=s)
        with ExitStack() as s:
            self.table_hi = sb("table_hi", [P, UNIT], F32R, stack=s)
            self.table_lo = sb("table_lo", [P, UNIT], F32R, stack=s)
            self.PQ_hi = sb("PQ_hi", [P, 8, 2 * P], F32R, stack=s)
            self.PQ_lo = sb("PQ_lo", [P, 8, 2 * P], F32R, stack=s)
        with ExitStack() as s:
            sb("before_row_g", [P, TT + 1, D], stack=s)
            self.chan_hi = sb("chan_hi", [P, 2 * P], F32R, stack=s)
            self.chan_lo = sb("chan_lo", [P, 2 * P], F32R, stack=s)
            sb("rest_of_row_g", [P, D - 4 * P], stack=s)
            self.odd = [sb(f"odd{i}", [P, CH], stack=s) for i in range(2)]
        with ExitStack() as s:
            sb("before_gate", [P, TT, D], stack=s)
            self.even = [sb(f"even{i}", [P, CH], stack=s) for i in range(2)]
        with ExitStack() as s:
            self.gated = [sb(f"gated{i}", [P, TM + 14], stack=s) for i in range(2)]
            self.dw = [sb(f"dw{i}", [P, TM], stack=s) for i in range(2)]
            self.xc = [sb(f"xc{i}", [P, TM], stack=s) for i in range(4)]
            self.cx = sb("cx", [P, TM + 3], stack=s)
            self.work = sb("work", [P, TM], stack=s)
        with ExitStack() as s:
            sb("gated_and_dw", [P, 2 * (TM + 14) + 2 * TM], stack=s)
            self.meta_raw = sb("meta_raw", [META, D], stack=s)
            self.meta_hat = sb("meta_hat", [META, D], stack=s)
        self.A_hi = sb("A_hi", [P, FB, T], F32R)
        self.A_lo = sb("A_lo", [P, FB, T], F32R)
        self.row_gate = sb("row_gate", [P, D])
        self.row_g = sb("row_g", [P, D])
        self.row_b = sb("row_b", [P, D])

        self.psum = self.stack.enter_context(self.nc.psum_tensor("psum", [P, 8, CH], F32))
        self.bank_free = [[] for _ in range(8)]
        self.bank_next = 0
        self.small_next = 0
        self.d_q = self.scratch("d_q", (HEADS, P, T))
        self.d_k = self.scratch("d_k", (HEADS, P, T))
        self.d_kc = self.scratch("d_kc", (HEADS, P, CTX))
        self.d_v = self.scratch("d_v", (KEYS, HEADS * P))
        self.d_conv = self.scratch("d_conv", (4, P, T))
        self.d_pool = self.scratch("d_pool", (2, P, TM))
        self.d_gelu = self.scratch("d_gelu", (4, P, TM))
        self.s_raw = [[self.semaphore(f"s_raw{i}"), 0] for i in range(N_RAW)]
        self.s_store = [[self.semaphore(f"s_store{i}"), 0] for i in range(4)]

    def take_bank(self, n=None):
        if n is None:
            n = self.bank_next
            self.bank_next = (n + 1) % 8
        self.pe.wait(*self.bank_free[n])
        self.bank_free[n] = []
        return n

    def take_temp(self, *queues):
        n = self.temp_next
        self.temp_next = (n + 1) % N_TEMP
        for q in queues:
            q.wait(*self.temp_free[n])
        self.temp_free[n] = []
        return n

    def take_small(self):
        n = self.small_next
        self.small_next = (n + 1) % N_SMALL
        return self.small[:, n, :]

    def columns(self, name, i=0, n=1):
        at = self.col_at[name] + i
        return self.cols[:, at:at + n]

    def dma(self, queue, sem, dst, src):
        sem[1] += 16
        queue.steps.append(lambda e, s=sem[0]: e.dma_start(dst, src).then_inc(s, 16))
        return (sem[0], sem[1])

    def load(self, name, dst, src, *after, queue=None):
        queue = queue or self.pool
        queue.wait(*after)
        return self.dma(queue, [self.semaphore("s_" + name), 0], dst, src)

    def weights_begin(self, units):
        self.units = units
        self.raw_free = [[] for _ in range(N_RAW)]
        self.split_free = [[] for _ in range(N_SPLIT)]
        self.raw_marks = {}
        self.n_rows = 0
        self.n_load = self.n_split = self.n_take = self.n_slot = 0

    def pump(self, needed=False):
        moved = True
        loaded_before = self.n_load
        while moved:
            moved = False
            if self.n_load < len(self.units):
                u, slot = self.units[self.n_load], self.n_load % N_RAW
                after = u.after() if u.after else []
                if self.raw_free[slot] is not None and after is not None:
                    self.sp.wait(*self.raw_free[slot], *after)
                    self.raw_free[slot] = None
                    u.raw = self.raw[slot]
                    if u.zero:
                        self.dve.wait(*self.zero_after(slot))
                        self.sp.wait(self.dve.do(lambda e, r=u.raw: e.memset(r[:], 0.0)))
                    for dst, src in u.pieces:
                        u.ready = self.dma(self.sp, self.s_raw[slot], dst(u.raw), src)
                    u.loaded_slot = slot
                    self.n_load += 1
                    moved = True
            if self.n_split < (self.n_take + 1 if needed else loaded_before) and self.n_split < self.n_load:
                u = self.units[self.n_split]
                if u.whole:
                    self.n_split += 1
                    moved = True
                    continue
                gate = u.gate() if u.gate else ()
                if gate is None:
                    continue
                if u.into:
                    got = u.into()
                    if got is None:
                        continue
                    hi, lo, free = got
                else:
                    slot = self.n_slot % N_SPLIT
                    if self.split_free[slot] is None:
                        continue
                    free = self.split_free[slot]
                    hi, lo = self.split_slot[slot][:, 0, :], self.split_slot[slot][:, 1, :]
                    u.both = self.split_slot[slot]
                    self.split_free[slot] = None
                    u.slot = slot
                    self.n_slot += 1
                n, raw = u.size, u.raw
                source = [u.ready]
                if gate:
                    row, made = gate
                    self.dve.wait(u.ready, made)
                    source = [self.dve.do(lambda e, r=raw, g=row: e.tensor_tensor(r[:], r[:], g[:], ALU.mult))]
                self.act.wait(*source, *free)
                m_hi = self.act.do(lambda e, h=hi, r=raw, n=n: e.copy(h[:, 0:n], r[:, 0:n]))
                self.dve.wait(*source, *free, m_hi)
                m_lo = self.dve.do(lambda e, h=hi, l=lo, r=raw, n=n: e.tensor_tensor(
                    l[:, 0:n], r[:, 0:n], h[:, 0:n].bitcast(F32), ALU.subtract))
                u.hi, u.lo, u.ready = hi, lo, [m_hi, m_lo]
                self.raw_marks[u.loaded_slot] = [m_hi, m_lo]
                self.raw_free[u.loaded_slot] = [m_hi, m_lo]
                self.n_split += 1
                moved = True

    def zero_after(self, slot):
        return self.raw_marks.get(slot, [])

    def take_unit(self, wait=True):
        self.pump()
        if self.n_split <= self.n_take:
            self.pump(needed=True)
        u = self.units[self.n_take]
        assert u.raw is not None and (u.whole or u.hi is not None), self.n_take
        self.n_take += 1
        if wait:
            self.pe.wait(*(u.ready if isinstance(u.ready, list) else [u.ready]))
        return u

    def release(self, u, mark, pump=True):
        if u.whole:
            self.raw_free[u.loaded_slot] = list(mark)
            self.raw_marks[u.loaded_slot] = list(mark)
        elif not u.into:
            self.split_free[u.slot] = [mark]
        if pump:
            self.pump()

    def passes(self, out, l_hi, l_lo, r_hi, r_lo, start, stop):
        pe = self.pe
        pe.quiet(lambda e: e.matmul(out, l_hi, r_hi, start=start, stop=False))
        pe.quiet(lambda e: e.matmul(out, l_hi, r_lo, start=False, stop=False))
        last = lambda e: e.matmul(out, l_lo, r_hi, start=False, stop=stop)
        if stop:
            return pe.do(last)
        pe.quiet(last)
        return None

    def split(self, src, hi, lo, ready, free=()):
        self.act.wait(*ready, *free)
        m_hi = self.act.do(lambda e: e.copy(hi, src))
        self.dve.wait(*ready, *free, m_hi)
        m_lo = self.dve.do(lambda e: e.tensor_tensor(lo, src, hi.bitcast(F32), ALU.subtract))
        return [m_hi, m_lo]

    def statistics(self, src, rows, width, ready, rms=False, eps=0):
        return self.scale_and_bias(*self.moments(src, rows, width, ready, rms, eps), rms)

    def moments(self, src, rows, width, ready, rms=False, eps=0):
        dve, act = self.dve, self.act
        s = self.take_small()
        dve.wait(*ready)
        n = (width + CH - 1) // CH
        for i in range(n):
            m = dve.do(lambda e, i=i: e.bn_stats(s[0:rows, 6 * i:6 * i + 6], src[:, i * CH:min(width, (i + 1) * CH)]))
        dve.wait(m)
        mean, var, std, scale = (s[0:rows, 12 + i:13 + i] for i in range(4))
        m = dve.do(lambda e: e.bn_aggr(s[0:rows, 12:14], s[0:rows, 0:6 * n]))
        if rms:
            dve.wait(m)
            m = dve.do(lambda e: e.scalar_tensor_tensor(var, mean, mean, var, ALU.mult, ALU.add))
        act.wait(m)
        m = act.do(lambda e: e.activation(std, var, ACT.Sqrt, bias=self.eps[0:rows, eps:eps + 1]))
        return mean, std, scale, rows, m

    def scale_and_bias(self, mean, std, scale, rows, rooted, rms=False):
        dve = self.dve
        dve.wait(rooted)
        m = dve.do(lambda e: e.reciprocal(scale, std))
        if rms:
            return scale, self.eps[0:rows, 2:3], [m]
        dve.wait(m)
        m = dve.do(lambda e: e.scalar_tensor_tensor(std, mean, -1.0, scale, ALU.mult, ALU.mult))
        return scale, std, [m]

    def normalize(self, src, dst, rows, ready, free=(), rms=False):
        scale, bias, got = self.statistics(src, rows, D, ready, rms)
        self.act.wait(*got, *free)
        return self.act.do(lambda e: e.activation(dst, src, ACT.Identity, bias=bias, scale=scale))

    def transpose_chunk(self, c, XH, ready, scale, shift, u_free, channels=(0, KT)):
        pe, act = self.pe, self.act
        pe.wait(*ready)
        marks = []
        for k in range(*channels):
            b = self.take_bank()
            for i in range(TPC):
                emit = lambda e: e.transpose(self.psum[:, b, i * P:(i + 1) * P], XH[:, i, k * P:(k + 1) * P],
                                             self.ident[:])
                if i < TPC - 1:
                    pe.quiet(emit)
            marks.append((k, b, pe.do(emit)))
        out = []
        for k, b, done in marks:
            if c == 1:
                done = marks[-1][2]
            t = self.take_temp(act)
            v = self.temp[t]
            hi, lo = self.U_hi[:, c, k, :], self.U_lo[:, c, k, :]
            act.wait(done, *u_free)
            m_v = act.do(lambda e: e.activation(v[:], self.psum[:, b, :], ACT.Identity, bias=shift(k), scale=scale(k)))
            self.bank_free[b] = [m_v]
            m = self.split(v[:], hi, lo, [m_v], u_free)
            self.temp_free[t] = m
            out += m
        return out

    def ada_take(self, layer, part, accumulators):
        u = self.take_unit(wait=False)
        k = self.ada_k
        marks = []
        dve, act, pool = self.dve, self.act, self.pool
        for acc, cond, free in accumulators:
            c = self.cc[:, k, cond:cond + 1]
            first = act if cond else dve
            if k == 0:
                first.wait(u.ready, self.cc_ready, *free)
                if cond:
                    m = act.do(lambda e: e.activation(acc, u.raw[:], ACT.Copy, scale=c))
                else:
                    m = dve.do(lambda e: e.tensor_scalar(acc, u.raw[:], c, None, ALU.mult))
                marks.append(m)
            elif cond:
                for half in range(2):
                    s = slice(half * CH, (half + 1) * CH)
                    t = self.take_temp(act)
                    v = self.temp[t]
                    act.wait(u.ready)
                    m = act.do(lambda e: e.activation(v[:], u.raw[:, s], ACT.Copy, scale=c))
                    marks.append(m)
                    pool.wait(m, self.ada_last[cond])
                    m = pool.do(lambda e: e.tensor_tensor(acc[:, s], acc[:, s], v[:], ALU.add))
                    self.temp_free[t] = [m]
            else:
                dve.wait(u.ready, self.ada_last[cond])
                m = dve.do(lambda e: e.scalar_tensor_tensor(acc, u.raw[:], c, acc, ALU.mult, ALU.add))
                marks.append(m)
            self.ada_last[cond] = m
        self.ada_k = (k + 1) % KT
        self.release(u, marks)
        return [self.ada_last[cond] for _, cond, _ in accumulators]

    def ada_sum(self, layer, part, accumulators, ready):
        pe, dve = self.pe, self.dve
        pe.wait(*ready, self.ones_ready)
        b = self.take_bank()
        for cond, (acc, _, _) in enumerate(accumulators):
            for i in range(KT):
                mark = pe.do(lambda e: e.matmul(self.psum[:, b, KT * cond + i:KT * cond + i + 1],
                                                acc[:, i * P:(i + 1) * P], self.ones[:, 0:1], start=True, stop=True))
        dve.wait(mark, self.cols_ready)
        bias = self.columns("ada_b", 48 * layer + KT * part, KT)
        one = 1.0 if part in (1, 4) else 0.0
        for cond, mod in enumerate((self.mod[:, layer], self.mod_ctx)[:len(accumulators)]):
            dst = mod[:, KT * part:KT * part + KT]
            m = dve.do(lambda e: e.scalar_tensor_tensor(dst, self.psum[:, b, KT * cond:KT * cond + KT], one, bias,
                                                        ALU.add, ALU.add))
        self.bank_free[b] = [m]
        self.mod_ready[(layer, part)] = m
        return mark

    def ada_fill(self, n):
        if self.ada_pending:
            layer, part, slot, ready = self.ada_pending
            self.ada_used[slot] = [self.ada_sum(layer, part, [(self.ada_acc[slot][:], 0, [])], ready)]
            self.ada_pending = None
        for _ in range(n):
            if not self.ada_parts:
                return
            layer, part = self.ada_parts[0]
            slot = part % 2
            ready = self.ada_take(layer, part, [(self.ada_acc[slot][:], 0, self.ada_used[slot] + self.rows_used)])
            if self.ada_k == 0:
                self.ada_parts.pop(0)
                self.ada_pending = (layer, part, slot, ready)

    def gate_row(self, layer, which):
        pe, act, dve = self.pe, self.act, self.dve
        col = 24 * which + 16
        ready = self.mod_ready[(layer, col // 8)]
        banks = [self.take_bank(), self.take_bank()]
        for k in range(KT):
            t = self.take_temp(dve)
            v = self.temp[t]
            dve.wait(ready)
            m = dve.do(lambda e, v=v, k=k: e.tensor_scalar(v[:, 0:P], self.ones[:],
                                                           self.mod[:, layer, col + k:col + k + 1], None, ALU.mult))
            pe.wait(m)
            m = pe.do(lambda e, v=v, k=k: e.matmul(self.psum[:, banks[k // 4], (k % 4) * P:(k % 4 + 1) * P],
                                                   v[:, 0:P], self.ident[:], start=True, stop=True))
            self.temp_free[t] = [m]
        act.wait(m, *self.gate_used)
        for i in range(2):
            m = act.do(lambda e, i=i: e.copy(self.row_gate[:, i * CH:(i + 1) * CH], self.psum[:, banks[i], :]))
            self.bank_free[banks[i]] = [m]
        self.gate_ready[(layer, which)] = m

    def up_group(self, n, chunk_ready, evacuate, before_chunk=None, chunk_major=False, extra=None,
                 beside=None):
        units = []
        order = [(i, c) for c in range(NCH) for i in range(n)] if chunk_major else \
                [(i, c) for i in range(n) for c in range(NCH)]
        for i, c in order:
            if before_chunk and (i, c) in ((0, 0), (n - 1, 0)):
                before_chunk(c if i == 0 else 1)
            if i == len(units):
                units.append(self.take_unit())
            u = units[i]
            W_hi = u.hi[:].rearrange("p (k m) -> p k m", k=KT)
            W_lo = u.lo[:].rearrange("p (k m) -> p k m", k=KT)
            if beside and c == (NCH - 1 if chunk_major else 0):
                beside(i)
            marks = chunk_ready(c)
            b = self.take_bank()
            for k in range(KT):
                self.pe.wait(*marks[2 * k:2 * k + 2])
                mark = self.passes(self.psum[:, b, :], W_hi[:, k, :], W_lo[:, k, :], self.U_hi[:, c, k, :],
                                   self.U_lo[:, c, k, :], k == 0, k == KT - 1)
            self.u_read = mark
            evacuate(i, c, b, mark)
            if c == NCH - 1:
                if extra:
                    mark = extra(i, W_hi, W_lo)
                self.release(u, mark)

    def down_block(self, lhs, lhs_ready, alpha=1.0, after_tile=None, beside=None, tile_first=False):
        pe, dve = self.pe, self.dve
        units = [self.take_unit(wait=False) for _ in range(FB)]
        for tt in range(TT):
            if beside and tt < TT - 1:
                beside(tt)
            banks = [self.take_bank(), self.take_bank()]
            for j in range(FB):
                pe.wait(*units[j].ready, *lhs_ready(j, tt))
                l_hi, l_lo = lhs(j, tt)
                for half in range(2):
                    s = slice(half * CH, (half + 1) * CH)
                    mark = self.passes(self.psum[:, banks[half], :], l_hi, l_lo, units[j].hi[:, s], units[j].lo[:, s],
                                       j == 0, j == FB - 1)
                    if j == FB - 1:
                        dve.wait(mark, *self.h_ready[tt])
                        h = self.H[:, tt, s]
                        acc = self.psum[:, banks[half], :]
                        if alpha == 1.0:
                            m = dve.do(lambda e, h=h, acc=acc: e.tensor_tensor(h, h, acc, ALU.add))
                        else:
                            m = dve.do(lambda e, h=h, acc=acc: e.scalar_tensor_tensor(h, h, alpha, acc, ALU.mult, ALU.add))
                        self.bank_free[banks[half]] = [m]
            self.h_ready[tt] = [m]
            self.tile_read[tt] = mark
            if after_tile and tile_first:
                after_tile(tt)
            if tt == TT - 1:
                for j, u in enumerate(units):
                    self.release(u, mark, pump=j == FB - 1)
            if after_tile and not tile_first:
                after_tile(tt)
        return mark

    def mlp(self, name, chunk_ready, before_chunk, fill=None, after_tile=None, alpha=1.0, gate=None,
            tile_first=False):
        for q in (self.pe, self.act, self.dve):
            q.begin(name)
        ready = {}

        def evacuate(j, c, b, mark):
            act, dve = self.act, self.dve
            t1, t2 = self.take_temp(act), self.take_temp(dve)
            r, a = self.temp[t1], self.temp[t2]
            act.wait(mark)
            m_r = act.do(lambda e: e.activation(r[:], self.psum[:, b, :], ACT.Relu))
            self.bank_free[b] = [m_r]
            dve.wait(m_r)
            m_a = dve.do(lambda e: e.tensor_tensor(a[:], r[:], r[:], ALU.mult))
            self.temp_free[t1] = [m_a]
            s = slice(c * CH, (c + 1) * CH)
            m = self.split(a[:], self.A_hi[:, j, s], self.A_lo[:, j, s], [m_a], self.a_read)
            self.temp_free[t2] = m
            ready[(j, c)] = m

        blocks = D_FF // (P * FB)
        for blk in range(blocks):
            self.up_group(FB, chunk_ready, evacuate, before_chunk if blk == 0 else None, chunk_major=(blk == 0),
                          beside=(lambda i: self.gate_row(*gate) if i == 1 else None) if gate and blk == 0 else None)
            last = blk == blocks - 1
            mark = self.down_block(
                lambda j, tt: (self.A_hi[:, j, tt * P:(tt + 1) * P], self.A_lo[:, j, tt * P:(tt + 1) * P]),
                lambda j, tt: ready[(j, tt // TPC)], alpha if blk == 0 else 1.0,
                after_tile if last else None, (lambda tt: fill(1)) if fill and not last else None, tile_first)
            self.a_read = [mark]

    def u_lhs(self, first):
        return lambda j, tt: (self.U_hi[:, tt // TPC, first + j, (tt % TPC) * P:(tt % TPC + 1) * P],
                              self.U_lo[:, tt // TPC, first + j, (tt % TPC) * P:(tt % TPC + 1) * P])

    def boundary(self, post, rms, scale, shift, from_u=False, fourier=False):
        dve, act, pool = self.dve, self.act, self.pool
        xh = [None] * TT
        chunk = [[], []]
        rows_ready = self.load_rows(*post) if post else []
        self.tile_read = {}
        u_read = [self.u_read]
        place = [self.XHall[:, 0:TPC] if from_u else self.XH[0], self.XH[1]]
        if fourier:
            place = [self.XHall[:, 0:TPC], self.XHall[:, TPC:TT]]
        tile = lambda tt: self.H[:, tt, :]
        waiting = []
        normed = {}

        def pre_norm(tt, sc, bi, got, on_vector=False):
            c = tt // TPC
            if fourier or (from_u and c == 1):
                free = [self.tile_read[TT - 1]]
            else:
                free = self.a_read if from_u else u_read
            dst = place[c][:, tt % TPC, :]
            if on_vector:
                dve.wait(*got, *free)
                m = dve.do(lambda e: e.tensor_scalar(dst, tile(tt), sc, bi, ALU.mult, ALU.add))
            else:
                act.wait(*got, *free)
                m = act.do(lambda e: e.activation(dst, tile(tt), ACT.Identity, bias=bi, scale=sc))
            xh[tt] = m
            self.h_ready[tt] = self.h_ready[tt] + [m]

        def turn(n):
            new, gained, old = (n, n - 1, n - 2) if post else (-1, -1, n)
            inside = lambda tt: 0 <= tt < TT
            first = self.moments(tile(new), P, D, self.h_ready[new]) if inside(new) else None
            second = self.moments(tile(old), P, D, self.h_ready[old], rms) if inside(old) else None
            if inside(gained):
                queue = pool if gained < TT - 2 else dve
                queue.wait(normed[gained], *rows_ready)
                m = queue.do(lambda e: e.tensor_tensor(tile(gained), tile(gained), self.row_g[:], ALU.mult))
                queue.wait(m)
                m = queue.do(lambda e: e.tensor_tensor(tile(gained), tile(gained), self.row_b[:], ALU.add))
                self.rows_used = self.h_ready[gained] = [m]
            if first:
                sc, bi, got = self.scale_and_bias(*first)
                act.wait(*got)
                normed[new] = act.do(lambda e: e.activation(tile(new), tile(new), ACT.Identity, bias=bi, scale=sc))
            if second:
                norm = (old, *self.scale_and_bias(*second, rms))
                if fourier or (from_u and old >= TPC):
                    waiting.append(norm)
                else:
                    pre_norm(*norm)

        def after_tile(tt):
            turn(tt)
            if scale and tt == TT - 2:
                u_free = [self.tile_read[TPC - 1]] if from_u else u_read
                chunk[0] += self.transpose_chunk(0, place[0], xh[0:TPC], scale, shift, u_free)
            if tt == TT - 1:
                for n in (TT, TT + 1, None) if post else (None,):
                    for i, norm in enumerate(waiting):
                        pre_norm(*norm, on_vector=i % 2 == 1)
                    waiting.clear()
                    if n:
                        turn(n)

        def make(c):
            if c == 1:
                u_free = [self.tile_read[TT - 1]] if from_u else u_read
                chunk[1] += self.transpose_chunk(1, place[1], xh[TPC:TT], scale, shift, u_free)

        return after_tile, make, lambda c: chunk[c], xh

    def load_rows(self, g, b):
        n = self.n_rows = self.n_rows + 1
        return [self.load(f"row_g{n}", self.row_g[:], g.partition_broadcast(P), *self.rows_used, self.ada_used[0]),
                self.load(f"row_b{n}", self.row_b[:], b.partition_broadcast(P), *self.rows_used, self.ada_used[1])]

    def plan_units(self):
        a = self.a
        units = []

        def up(w, col):
            v = w[:, col:col + P].rearrange("(k p) m -> p k m", p=P)
            return Unit([(lambda r: r[:].rearrange("p (k m) -> p k m", k=KT), v)])

        def down(w, row, gate=None):
            return Unit([(lambda r: r[:], w[row:row + P, :])], gate=gate)

        def ada(layer, part):
            return [Unit([(lambda r: r[:], a["ada_w"][layer, k * P:(k + 1) * P, part * UNIT:(part + 1) * UNIT])],
                         whole=True) for k in range(KT)]

        def gate(layer, which):
            def ask():
                m = self.gate_ready.get((layer, which))
                return None if m is None else (self.row_gate, m)
            return ask

        def mlp(w1, w2, g=None, fill=None):
            for blk in range(D_FF // (P * FB)):
                for j in range(FB):
                    units.append(up(w1, (blk * FB + j) * P))
                for j in range(FB):
                    units.append(down(w2, (blk * FB + j) * P, g))
                if fill and blk < D_FF // (P * FB) - 1:
                    fill(TT - 1)

        units += ada(0, 1) + ada(0, 0)
        w_in = a["w_in"][0]
        rest = [u for part in range(2, 6) for u in ada(0, part)]
        layer1 = [u for part in range(6) for u in ada(1, part)]

        def ada_fill(n, of):
            for _ in range(min(n, len(of))):
                units.append(of.pop(0))
        for i in range(4):
            units.append(up(w_in, Q0 + i * P))
        for i in range(4):
            units.append(up(w_in, K0 + i * P))
            ada_fill(2, rest)
        for i in range(4):
            v = w_in[2 * i * P:(2 * i + 2) * P, V0:V0 + 512].rearrange("(k p) n -> p k n", p=P)
            units.append(Unit([(lambda r: r[:].rearrange("p (k n) -> p k n", k=2), v)]))
        for i in range(4):
            for part in (1, 2, 0):
                units.append(up(w_in, part * D_CONV + i * P))
                ada_fill(2, rest)
        for h in range(HEADS):
            stored = lambda key: (lambda: self.stored.get(key))
            units.append(Unit([(lambda r: r[:], self.d_q[h])], after=stored(("q", h))))
            units.append(Unit([(lambda r: r[:], self.d_k[h])], after=stored(("k", h))))
            v = self.d_v[:, h * P:(h + 1) * P].rearrange("(k p) n -> p k n", p=P)
            units.append(Unit([(lambda r: r[:, 0:256], self.d_kc[h]),
                               (lambda r: r[:, 256:512].rearrange("p (k n) -> p k n", k=2), v[:, TT:TT + CTT, :])],
                              after=stored("ctx"), size=512))
            units.append(Unit([(lambda r: r[:].rearrange("p (k n) -> p k n", k=TT), v[:, 0:TT, :])],
                              after=stored("v")))
        for k in range(KT):
            units.append(down(a["w_out_mix"][0], k * P, gate(0, 0)))
        mlp(a["mlp_w1"][0], a["mlp_w2"][0], gate(0, 1), lambda n: ada_fill(n, layer1))
        for i in range(6):
            into = (lambda: None if self.table_free is None else (self.table_hi, self.table_lo, self.table_free)) \
                if i == 5 else None
            units.append(Unit([(lambda r: r[:], a["dft"][i])], into=into))
        for k in range(KT):
            units.append(down(a["w_out_fourier"][0], k * P, gate(1, 0)))
        mlp(a["mlp_w1"][1], a["mlp_w2"][1], gate(1, 1))
        w = a["w_in_2"][0]
        for m in (4, 5, 2, 3, 10, 11, 12, 13, 0, 1, 6, 7, 8, 9):
            units.append(up(w, m * P))
        pieces = []
        for e in range(2):
            s = slice(64 * e, 64 * e + 64)
            pieces.append((lambda r, s=s: r[s, 0:256].rearrange("p (j n) -> p j n", j=2)[:, :, s],
                           a["pool_w_2"][0].rearrange("(j e) c d -> e c j d", e=2)[e]))
        pieces.append((lambda r: r[:, 256:768].rearrange("p (k n) -> p k n", k=2),
                       a["convb_pw_w_2"][0].rearrange("(k p) n -> p k n", p=P)))
        units.append(Unit(pieces, zero=True, size=768))
        pieces = []
        for i, name in enumerate(("rg_w_a_2", "rg_w_x_2")):
            for e in range(2):
                s = slice(64 * e, 64 * e + 64)
                pieces.append((lambda r, s=s, i=i: r[s, 512 * i:512 * i + 512].rearrange("p (j n) -> p j n", j=4)[:, :, s],
                               a[name][0].rearrange("(j e) c d -> e c j d", e=2)[e]))
        units.append(Unit(pieces, zero=True))
        for k in range(KT):
            units.append(down(a["w_out_2"][0], k * P))
        mlp(a["w_up_2"][0], a["w_down_2"][0])
        return units

    def start(self):
        pe, act, dve, pool, a = self.pe, self.act, self.dve, self.pool, self.a
        for q in (pe, act, dve, pool):
            q.begin("start")
        self.gate_ready, self.mod_ready, self.stored = {}, {}, {}
        self.gate_used, self.rows_used, self.a_read = [], [], []
        self.table_free = None
        self.tile_read = {}
        self.u_read = None
        vec_loaded, at = [], 0
        for g, (names, used) in enumerate(self.col_groups):
            vec_loaded.append(self.dma(self.sp, [self.semaphore(f"s_vectors{g}"), 0], self.vector_rows(g)[0:used, :],
                                       a["vectors"][at:at + used, :]))
            at += used
        m = pool.do(lambda e: e.memset(self.ident[:], 0.0))
        pool.wait(m)
        self.ident_ready = pool.do(lambda e: e.affine_select(
            out=self.ident[:], in_=self.ident[:], compare_op=ALU.not_equal, fill=1.0, base=0,
            pattern=[[-1, P]], channel_multiplier=1))
        m = dve.do(lambda e: e.memset(self.ones[:], 1.0))
        for i, v in enumerate((1e-6, 1e-5, 0.0)):
            m_eps = dve.do(lambda e, i=i, v=v: e.memset(self.eps[:, i:i + 1], v))
        self.ones_ready = m_eps
        act.wait(m_eps)
        x = a["x"][0].rearrange("(t p) d -> p t d", p=P)
        self.h_ready = []
        ctx = a["ctx"][0].rearrange("(t p) d -> p t d", p=P)
        sources = [(f"x{t}", self.H[:, t, :], x[:, t, :], self.XH[t // TPC][:, t % TPC, :]) for t in range(TT)] + \
            [(f"ctx{t}", self.ctx_raw[:, t, :], ctx[:, t, :], self.XHc[:, t, :]) for t in range(CTT)]
        loaded, hats = [], []

        def next_load():
            if len(loaded) < len(sources):
                name, dst, src, _ = sources[len(loaded)]
                loaded.append(self.load(name, dst, src, queue=act))

        def next_norm():
            t = len(hats)
            _, tile, _, hat = sources[t]
            hats.append(self.normalize(tile, hat, P, [loaded[t]]))
            next_load()

        for _ in range(3):
            next_load()
        lq_loaded = self.load("lambda", self.temp[4][:, 0:256],
                              a["lambda_qk"][0].rearrange("a d -> (a d)").partition_broadcast(P))
        pe.wait(self.ident_ready, *vec_loaded)
        at = 0
        for g, (names, used) in enumerate(self.col_groups):
            b = self.take_bank()
            m = pe.do(lambda e, g=g, b=b, used=used: e.transpose(self.psum[:, b, 0:used], self.vector_rows(g)[0:used, :],
                                                                 self.ident[0:used, 0:used]))
            dve.wait(m)
            m = dve.do(lambda e, b=b, used=used, at=at: e.tensor_copy(self.cols[:, at:at + used], self.psum[:, b, 0:used]))
            self.bank_free[b] = [m]
            at += used
        self.cols_ready = m
        act.wait(m)
        act.do(lambda e: e.activation(self.cc[:, :, 0], self.columns("c", 0, 8), ACT.Silu))
        self.cc_ready = act.do(lambda e: e.activation(self.cc[:, :, 1], self.columns("c_ctx", 0, 8), ACT.Silu))
        lq = self.temp[4]
        dve.wait(lq_loaded)
        v = lq[:, 0:256].rearrange("p (a b d) -> p a b d", a=2, b=2)
        m = dve.do(lambda e: e.tensor_tensor(lq[:, 256:384].rearrange("p (a d) -> p a d", a=2), v[:, :, 0, :], v[:, :, 1, :], ALU.mult))
        dve.wait(m)
        m = dve.do(lambda e: e.tensor_reduce(self.lam[:, 0:2], lq[:, 256:384].rearrange("p (a d) -> p a d", a=2), AX_X, ALU.add))
        self.temp_free[4] = [m]
        act.wait(m)
        m = act.do(lambda e: e.activation(self.lam[:, 2:4], self.lam[:, 0:2], ACT.Exp))
        dve.wait(m)
        m = dve.do(lambda e: e.tensor_tensor(self.lam[:, 4:5], self.lam[:, 3:4], self.lam[:, 2:3], ALU.subtract))
        dve.wait(m)
        self.lam_ready = dve.do(lambda e: e.tensor_scalar(self.lam[:, 4:5], self.lam[:, 4:5], -LAM_INIT, None, ALU.add))
        self.ada_k, self.ada_last, self.ada_pending = 0, [None, None], None
        self.ada_acc, self.ada_used = (self.row_g, self.row_b), [[], []]
        self.ada_parts = [(0, part) for part in range(2, 6)] + [(1, part) for part in range(6)]
        next_norm()
        for n, part in enumerate((1, 0)):
            acc = [(self.ada_x[:, n, :], 0, []), (self.ada_c[:, n, :], 1, [])]
            for k in range(KT):
                ready = self.ada_take(0, part, acc)
                if (n, k) == (1, 3):
                    self.ada_sum(0, 1, *first_part)
                if len(hats) < len(sources) * (n * KT + k + 2) // (2 * KT):
                    next_norm()
            if n == 0:
                first_part = (acc, ready)
        self.ada_sum(0, part, acc, ready)
        xh, xhc = hats[0:TT], hats[TT:]
        self.h_ready = [[loaded[t], xh[t]] for t in range(TT)]
        return xh, xhc

    def vector_rows(self, g):
        return self.temp[g][:, 0:P]

    def project_attention(self, xh, xhc):
        pe, act, dve, pool, a = self.pe, self.act, self.dve, self.pool, self.a
        for q in (pe, act, dve, pool):
            q.begin("project")
        mod_done = [self.mod_ready[(0, 0)], self.mod_ready[(0, 1)]]
        act.wait(*mod_done)
        scale = lambda k: self.mod[:, 0, 8 + k:9 + k]
        shift = lambda k: self.mod[:, 0, k:k + 1]
        pe.wait(*xhc)
        uc_ready = []
        banks = []
        for k in range(KT):
            if k % 2 == 0:
                b = self.take_bank()
            for t in range(CTT):
                m = pe.do(lambda e, b=b, k=k, t=t: e.transpose(
                    self.psum[:, b, (k % 2) * CTX + t * P:(k % 2) * CTX + (t + 1) * P],
                    self.XHc[:, t, k * P:(k + 1) * P], self.ident[:]))
            banks.append(b)
        all_read = m
        for k in range(KT):
            t = self.take_temp(act)
            v, b = self.temp[t], banks[k]
            act.wait(all_read)
            m_v = act.do(lambda e, v=v, b=b, k=k: e.activation(
                v[:, 0:CTX], self.psum[:, b, (k % 2) * CTX:(k % 2 + 1) * CTX], ACT.Identity,
                bias=self.mod_ctx[:, k:k + 1], scale=self.mod_ctx[:, 8 + k:9 + k]))
            self.bank_free[b] = [m_v]
            m = self.split(v[:, 0:CTX], self.Uc_hi[:, k, :], self.Uc_lo[:, k, :], [m_v], [all_read])
            self.temp_free[t] = m
            uc_ready += m
        rope_loaded = [self.load("rope_cos", self.rope_cos[:], a["rope_cos"], all_read),
                       self.load("rope_sin", self.rope_sin[:], a["rope_sin"], all_read)]
        chunk = [[], []]

        def before_chunk(c):
            chunk[c] = self.transpose_chunk(c, self.XH[c], xh[c * TPC:(c + 1) * TPC], scale, shift, [])

        stage_next, stage_free = [0], [[all_read], [all_read], [all_read], [all_read]]

        def take_stage(*queues):
            n = stage_next[0]
            stage_next[0] = (n + 1) % 4
            for q in queues:
                q.wait(*stage_free[n])
            return n

        def store(n, dst, src, ready):
            pool.wait(*ready)
            m = self.dma(pool, self.s_store[n], dst, src)
            stage_free[n] = [m]
            return m

        swap = [(i + 16) % 32 for i in range(32)]

        def rope(dram):
            marks = {}

            def evacuate(i, c, b, mark):
                s = slice(c * CH, (c + 1) * CH)
                t1, t2 = self.take_temp(dve), self.take_temp(dve)
                sw, xcos = self.temp[t1], self.temp[t2]
                x = self.psum[:, b, :]
                act.wait(mark, *self.temp_free[t2])
                n = take_stage(act, dve)
                st = self.stage_buf[n]
                m_x = act.do(lambda e: e.copy(st[:], x))
                self.bank_free[b] = [m_x]
                dve.wait(m_x, *rope_loaded)
                m = dve.do(lambda e: e.stream_shuffle(sw[:], st[:], swap))
                m2 = dve.do(lambda e: e.tensor_tensor(xcos[:], st[:], self.rope_cos[:, s], ALU.mult))
                dve.wait(m)
                m = dve.do(lambda e: e.tensor_tensor(sw[:], sw[:], self.rope_sin[:, s], ALU.mult))
                dve.wait(m, m2)
                m = dve.do(lambda e: e.tensor_tensor(st[:], sw[:], xcos[:], ALU.add))
                self.temp_free[t1] = self.temp_free[t2] = [m]
                marks.setdefault(i, []).append(store(n, dram(i)[:, s], st[:], [m]))
            return evacuate, marks

        evac_q, q_marks = rope(lambda i: self.d_q[i])
        self.up_group(4, lambda c: chunk[c], evac_q, before_chunk, chunk_major=True)
        for h in range(HEADS):
            self.stored[("q", h)] = q_marks[h]

        kc_marks = []

        def keys_of_context(i, W_hi, W_lo):
            pe.wait(*uc_ready)
            b = self.take_bank()
            for k in range(KT):
                mark = self.passes(self.psum[:, b, 0:CTX], W_hi[:, k, :], W_lo[:, k, :], self.Uc_hi[:, k, :],
                                   self.Uc_lo[:, k, :], k == 0, k == KT - 1)
            n = take_stage(act)
            act.wait(mark)
            m = act.do(lambda e: e.copy(self.stage_buf[n][:, 0:CTX], self.psum[:, b, 0:CTX]))
            self.bank_free[b] = [m]
            kc_marks.append(store(n, self.d_kc[self.head], self.stage_buf[n][:, 0:CTX], [m]))
            return mark

        for h in range(HEADS):
            self.head = h
            evac_k, k_marks = rope(lambda i, h=h: self.d_k[h])
            self.up_group(1, lambda c: chunk[c], evac_k, extra=keys_of_context,
                          beside=lambda i: self.ada_fill(2))
            self.stored[("k", h)] = k_marks[0]
        units = [self.take_unit() for _ in range(4)]
        v_marks = []
        for t in range(TT + CTT):
            b = self.take_bank()
            for k in range(KT):
                u = units[k // 2]
                s = slice((k % 2) * CH, (k % 2 + 1) * CH)
                if t < TT:
                    l = [U[:, t // TPC, k, (t % TPC) * P:(t % TPC + 1) * P] for U in (self.U_hi, self.U_lo)]
                else:
                    l = [U[:, k, (t - TT) * P:(t - TT + 1) * P] for U in (self.Uc_hi, self.Uc_lo)]
                mark = self.passes(self.psum[:, b, :], l[0], l[1], u.hi[:, s], u.lo[:, s], k == 0, k == KT - 1)
            n = take_stage(act)
            act.wait(mark)
            m = act.do(lambda e, n=n, b=b: e.copy(self.stage_buf[n][:], self.psum[:, b, :]))
            self.bank_free[b] = [m]
            v_marks.append(store(n, self.d_v[t * P:(t + 1) * P, :], self.stage_buf[n][:], [m]))
        for u in units:
            self.release(u, mark)
        self.stored["v"] = v_marks[-4:] 
        self.stored["ctx"] = kc_marks[-1:] + v_marks[-4:]
        h_read = [m for r in self.h_ready for m in r]
        dve.wait(*h_read)
        zero = dve.do(lambda e: e.memset(self.gv[:, 0:1], 0.0))
        zero = dve.do(lambda e: e.memset(self.gv[:, T + 1:T + 2], 0.0))
        state = {"gc": [], "gv": [], "free_gc": h_read, "free_gv": [], "free_cv": [[], []], "cv": None}
        conv_marks = []
        self.stored["conv"] = conv_marks
        for i in range(4):
            cv = (self.cv, self.cv2)[i % 2]

            def evac(part, c, b, mark, i=i, cv=cv):
                s = slice(c * CH, (c + 1) * CH)
                x = self.psum[:, b, :]
                if part == 0:
                    act.wait(mark, *state["free_gc"])
                    m = act.do(lambda e: e.copy(self.conv_gc[:, s], x))
                    state["gc"] = [m]
                elif part == 1:
                    dve.wait(mark, *state["gc"], *state["free_gv"])
                    m = dve.do(lambda e: e.tensor_tensor(self.gv[:, 1 + c * CH:1 + (c + 1) * CH], x, self.conv_gc[:, s], ALU.mult))
                    state["free_gc"] = [m]
                    if c == 1:
                        w = [self.columns("conv_w", 4 * tap + i) for tap in range(3)]
                        dve.wait(m, zero, *state["free_cv"][i % 2])
                        mm = dve.do(lambda e: e.tensor_scalar(cv[:], self.gv[:, 0:T], w[0], None, ALU.mult))
                        for tap in (1, 2):
                            dve.wait(mm)
                            mm = dve.do(lambda e, tap=tap: e.scalar_tensor_tensor(
                                cv[:], self.gv[:, tap:tap + T], w[tap], cv[:], ALU.mult, ALU.add))
                        state["free_gv"] = state["cv"] = [mm]
                else:
                    n = take_stage(dve)
                    st = self.stage_buf[n]
                    dve.wait(mark, *state["cv"])
                    m = dve.do(lambda e: e.tensor_tensor(st[:], x, cv[:, s], ALU.mult))
                    state["free_cv"][i % 2] = [m]
                    conv_marks.append(store(n, self.d_conv[i, :, s], st[:], [m]))
                self.bank_free[b] = [m]

            self.up_group(3, lambda c: chunk[c], evac, beside=lambda i: self.ada_fill(2))
        self.ada_fill(0)
        self.h_region_free = list(state["free_cv"][0]) + list(state["free_cv"][1]) + state["free_gc"]
        self.stage_all = [m for s in stage_free for m in s]
        self.uc_read = mark
        self.project_done = self.u_read

    def attention(self):
        pe, act, dve, pool = self.pe, self.act, self.dve, self.pool
        for q in (pe, act, dve, pool):
            q.begin("attention")
        T_BANKS = (5, 6, 7)
        scale = QK ** -0.5
        conv_loaded = self.load("conv_in", self.conv_in[:], self.d_conv.rearrange("k p t -> p k t"),
                                self.project_done, self.uc_read, *self.stage_all, *self.stored["conv"])
        act.wait(self.project_done, self.uc_read, *self.stage_all, *self.h_region_free)
        dve.wait(self.project_done, self.uc_read, *self.stage_all, *self.h_region_free)
        flat = self.psum[:, 0:5, :].rearrange("p b n -> p (b n)")
        S = [flat[:, 0:KEYS], flat[:, KEYS:2 * KEYS]]
        units = {}
        o_read = []
        prob0_free, prob1_free = [[], [], []], [[], []]
        pt_free = []
        conv_done = []
        T_PARTS = ((0, 4), (4, 4), (8, 2))
        o_marks = [[] for _ in range(TT)]

        def scores(h, qt, places):
            if qt == 0 and h not in units:
                units[h] = [self.take_unit() for _ in range(3)]
            uq, uk, uc = units[h][:3]
            for c, b, of_context, first, at in places:
                s = slice(64 * c, 64 * c + 64)
                src, n = (uc, CTX) if of_context else (uk, CH)
                if (c, b) == (1, 2):
                    pe.wait(mark)
                else:
                    self.take_bank(b)
                mark = self.passes(flat[:, at:at + n], uq.hi[s, qt * P:(qt + 1) * P],
                                   uq.lo[s, qt * P:(qt + 1) * P], src.hi[s, first:first + n],
                                   src.lo[s, first:first + n], True, True)
            return mark

        FIRST_SCORES = ((0, 0, False, 0, 0), (0, 1, False, 512, 512), (0, 2, True, 0, 1024), (1, 2, True, 0, 1280))
        SECOND_SCORES = ((1, 3, False, 0, 1536), (1, 4, False, 512, 2048))

        def maximum(c, ready):
            sm = self.take_small()
            dve.wait(*ready)
            m = dve.do(lambda e: e.tensor_reduce(sm[:, 0:1], S[c], AX_X, ALU.max))
            dve.wait(m)
            return sm, dve.do(lambda e: e.tensor_scalar(sm[:, 1:2], sm[:, 0:1], -scale, None, ALU.mult))

        def exponential(c, i, sm, m):
            numerators, free = ((self.prob0, prob0_free), (self.prob1, prob1_free))[c]
            n = i % len(numerators)
            act.wait(m, *free[n])
            m = act.do(lambda e: e.activation(numerators[n], S[c], ACT.Exp, bias=sm[:, 1:2], scale=scale,
                                              accum_out=sm[:, 2:3]))
            for b in ((0, 1), (2, 3, 4))[c]:
                self.bank_free[b] = [m]
            return m

        def coefficients(sm0, sm1, m0, m1):
            dve.wait(m0, m1, self.lam_ready)
            m = dve.do(lambda e: e.reciprocal(sm1[:, 3:4], sm1[:, 2:3]))
            m_r0 = dve.do(lambda e: e.reciprocal(sm0[:, 3:4], sm0[:, 2:3]))
            dve.wait(m)
            m = dve.do(lambda e: e.scalar_tensor_tensor(sm1[:, 4:5], sm1[:, 3:4], sm0[:, 2:3], self.lam[:, 4:5],
                                                        ALU.mult, ALU.mult))
            return sm1[:, 4:5], m, sm0[:, 3:4], m_r0

        def mix(i, coefficient, m, r0, m_r0):
            p0, p1 = self.prob0[i % 3], self.prob1[i % 2]
            act.wait(m)
            m = act.do(lambda e: e.activation(p1, p1, ACT.Copy, scale=coefficient))
            pool.wait(m)
            pool.do(lambda e: e.tensor_tensor(p0[:, 0:T], p0[:, 0:T], p1[:, CTX:KEYS], ALU.add))
            m = pool.do(lambda e: e.tensor_tensor(p0[:, T:KEYS], p0[:, T:KEYS], p1[:, 0:CTX], ALU.add))
            prob1_free[i % 2] = [m]
            return m, r0, m_r0

        def transposes(i, mixed):
            p0 = self.prob0[i % 3]
            pe.wait(mixed)
            marks = []
            for (first, n), b in zip(T_PARTS, T_BANKS):
                self.take_bank(b)
                for k in range(n):
                    m = pe.do(lambda e: e.transpose(self.psum[:, b, k * P:(k + 1) * P],
                                                    p0[:, (first + k) * P:(first + k + 1) * P], self.ident[:]))
                marks.append(m)
            prob0_free[i % 3] = [m]
            return marks

        def split_transposed(marks):
            places = []
            for (first, n), b, m in zip(T_PARTS, T_BANKS, marks):
                s = slice(first, first + n)
                src = self.psum[:, b, 0:n * P]
                hi, lo = (x[:, s, :].rearrange("p k n -> p (k n)") for x in (self.PT_hi, self.PT_lo))
                act.wait(m, *pt_free)
                places.append((src, hi, lo, b, act.do(lambda e: e.copy(hi, src))))

            def low():
                ready = []
                for src, hi, lo, b, m_hi in places:
                    dve.wait(m_hi)
                    m_lo = dve.do(lambda e: e.tensor_tensor(lo, src, hi.bitcast(F32), ALU.subtract))
                    self.bank_free[b] = [m_hi, m_lo]
                    ready.append([m_hi, m_lo])
                return ready
            return low

        def values(h, qt, ready, r0, m_r0):
            nonlocal pt_free
            uc, uv = units[h][2], units[h][3]
            self.take_bank(5)
            for k in range(KEYS // P):
                pe.wait(*ready[k // 4])
                v, at = (uv, k * P) if k < TT else (uc, 256 + (k - TT) * P)
                v = v.both[:, :, at:at + P]
                both = self.psum[:, 5, 0:2 * P].rearrange("p (a n) -> p a n", a=2)
                pe.quiet(lambda e: e.matmul(both, self.PT_hi[:, k, :], v, start=k == 0, stop=False))
                mark = pe.do(lambda e: e.matmul(both, self.PT_lo[:, k, :], v, start=False, stop=k == KEYS // P - 1))
            pt_free = [mark]
            t = self.take_temp(act)
            low = self.temp[t][:, 0:P]
            act.wait(mark, m_r0)
            m = act.do(lambda e: e.activation(low, self.psum[:, 5, P:2 * P], ACT.Copy, scale=r0))
            dve.wait(m)
            m = dve.do(lambda e: e.scalar_tensor_tensor(self.O[:, qt, h * P:(h + 1) * P], self.psum[:, 5, 0:P], r0, low,
                                                        ALU.mult, ALU.add))
            self.temp_free[t] = self.bank_free[5] = [m]
            o_marks[qt] = [m]
            if qt == TT - 1:
                self.release(uc, mark)
                self.release(uv, mark)

        def squares(qt):
            t = self.take_temp(dve)
            sq = self.temp[t]
            o = self.O[:, qt, :]
            dve.wait(*o_marks[qt])
            m = dve.do(lambda e: e.tensor_tensor(sq[:], o, o, ALU.mult))
            dve.wait(m)
            m = dve.do(lambda e: e.tensor_reduce(self.sumsq[:, qt, :], sq[:].rearrange("p (h d) -> p h d", h=HEADS),
                                                 AX_X, ALU.add))
            self.temp_free[t] = [m]
            o_marks[qt] = [m]

        steps = [(h, qt) for h in range(HEADS) for qt in range(TT)]
        sums, mixed = {}, {}
        for i in range(len(steps) + 2):
            now = steps[i] if i < len(steps) else None
            old = steps[i - 2] if i >= 2 else None
            if now:
                m = scores(*now, FIRST_SCORES)
                sm0, m_max = maximum(0, [m])
            if i - 1 in sums:
                mixed[i - 1] = mix(i - 1, *sums.pop(i - 1))
            if old:
                m, r0, m_r0 = mixed.pop(i - 2)
                low = split_transposed(transposes(i - 2, m))
            if now:
                m0 = exponential(0, i, sm0, m_max)
                m_second = scores(*now, SECOND_SCORES)
                if now[1] == TT - 1:
                    self.release(units[now[0]][0], m_second, pump=False)
                    self.release(units[now[0]][1], m_second, pump=now[0] < HEADS - 1)
            if old:
                got = low()
            if now:
                sm1, m = maximum(1, [m_second, m0])
                m1 = exponential(1, i, sm1, m)
            if old:
                if old[1] == 0:
                    units[old[0]].append(self.take_unit())
                values(*old, got, r0, m_r0)
            if now:
                sums[i] = coefficients(sm0, sm1, m0, m1)
            if old and old[0] == HEADS - 1:
                squares(old[1])
            if 4 <= i < 12:
                k, c = (i - 4) // 2, (i - 4) % 2
                conv_done += self.split(self.conv_in[:, k, c * CH:(c + 1) * CH], self.U_hi[:, c, k, :],
                                        self.U_lo[:, c, k, :], [conv_loaded, self.project_done])
        self.bank_next = 0
        x = self.a["x"][0].rearrange("(t p) d -> p t d", p=P)
        free = [*prob0_free, *prob1_free, pt_free]
        for t in range(TT):
            self.h_ready[t] = [self.load(f"xx{t}", self.H[:, t, :], x[:, t, :], *free)]
        return conv_done, o_marks

    def attention_out(self, conv_done, o_marks):
        pe, act, dve = self.pe, self.act, self.dve
        ss = self.sumsq[:].rearrange("p t h -> p (t h)")
        act.wait(*[m for ms in o_marks for m in ms])
        m = act.do(lambda e: e.activation(ss, ss, ACT.Sqrt, bias=self.eps[:, 1:2], scale=1.0 / P))
        dve.wait(m)
        m_r = dve.do(lambda e: e.reciprocal(ss, ss))
        g = self.softplus[:, 7, 0:1]
        m_g = dve.do(lambda e: e.tensor_scalar(g, self.columns("subln_g"), 1.0 - LAM_INIT, None, ALU.mult))
        act.wait(m_g)
        normed = []
        dve.wait(m_r)
        for t in range(TT):
            o = self.O[:, t, :].rearrange("p (h d) -> p h d", h=HEADS)
            normed.append(dve.do(lambda e, o=o, t=t: e.tensor_tensor(
                o, o, self.sumsq[:, t, :].unsqueeze(2).to_broadcast([P, HEADS, P]), ALU.mult)))
        ready = []

        def heads_to_u(c, h):
            b = self.take_bank()
            pe.wait(*normed[c * TPC:(c + 1) * TPC])
            for i in range(TPC):
                m = pe.do(lambda e: e.transpose(self.psum[:, b, i * P:(i + 1) * P],
                                                self.O[:, c * TPC + i, h * P:(h + 1) * P], self.ident[:]))
            t = self.take_temp(act)
            v = self.temp[t]
            act.wait(m)
            m = act.do(lambda e: e.activation(v[:], self.psum[:, b, :], ACT.Copy, scale=g))
            self.bank_free[b] = [m]
            m = self.split(v[:], self.U_hi[:, c, 4 + h, :], self.U_lo[:, c, 4 + h, :], [m])
            self.temp_free[t] = m
            ready.append(m)

        def beside(tt):
            if 2 <= tt <= 5:
                for n in (2 * tt - 4, 2 * tt - 3):
                    heads_to_u(n // HEADS, n % HEADS)

        self.down_block(self.u_lhs(0), lambda j, tt: conv_done, ALPHA, beside=beside)
        return ready

    def fourier(self, xh):
        pe, act, dve = self.pe, self.act, self.dve
        for q in (pe, act, dve, self.pool):
            q.begin("fourier")
        scale = lambda k: self.mod[:, 1, 8 + k:9 + k]
        shift = lambda k: self.mod[:, 1, k:k + 1]
        act.wait(self.mod_ready[(1, 0)], self.mod_ready[(1, 1)])
        t = self.take_temp(self.pool)
        chan_raw = self.temp[t][:, 0:2 * P]
        chan = self.load("chan", chan_raw, self.a["dft_chan"])
        chan_ready = self.temp_free[t] = self.split(chan_raw, self.chan_hi[:], self.chan_lo[:], [chan],
                                                      self.rows_used)
        u_ready = {}
        odd_free = [[self.rows_used, self.gate_used], [self.rows_used, self.gate_used]]
        folded = None

        def fold(k, t0, m0, t1, m1):
            v0, v1, odd = self.temp[t0], self.temp[t1], self.odd[k % 2]
            q = CH // 2
            even = self.even[k % 2]
            self.pool.wait(m0, m1, *odd_free[k % 2])
            m_odd = self.pool.do(lambda e: e.tensor_tensor(odd[:], v0[:], v1[:], ALU.subtract))
            dve.wait(m0, m1, *odd_free[k % 2])
            m = dve.do(lambda e: e.tensor_tensor(even[:], v0[:], v1[:], ALU.add))
            self.temp_free[t0] = [m_odd, m]
            dve.wait(m_odd, m)
            m = dve.do(lambda e: e.tensor_tensor(v1[:, 0:q], even[:, 0:q], even[:, q:CH], ALU.subtract))
            m2 = dve.do(lambda e: e.tensor_tensor(v1[:, q:CH], even[:, 0:q], even[:, q:CH], ALU.add))
            ready = self.split(odd[:], self.U_hi[:, 0, k, :], self.U_lo[:, 0, k, :], [m_odd, self.u_read])
            odd_free[k % 2] = [ready, m2]
            got = self.split(v1[:], self.U_hi[:, 1, k, :], self.U_lo[:, 1, k, :], [m, m2, self.u_read])
            self.temp_free[t1] = got
            u_ready[k] = ready + got

        for k in range(KT):
            halves = []
            for c in range(2):
                b = self.take_bank()
                pe.wait(*xh[c * TPC:(c + 1) * TPC])
                for i in range(TPC):
                    m = pe.do(lambda e: e.transpose(self.psum[:, b, i * P:(i + 1) * P],
                                                    self.XHall[:, c * TPC + i, k * P:(k + 1) * P], self.ident[:]))
                self.xh_read = m
                t = self.take_temp(act)
                act.wait(m)
                m = act.do(lambda e: e.activation(self.temp[t][:], self.psum[:, b, :], ACT.Identity,
                                                  bias=shift(k), scale=scale(k)))
                self.bank_free[b] = [m]
                halves += [t, m]
            if folded:
                fold(*folded)
            folded = (k, *halves)
        fold(*folded)
        self.table_free = [self.xh_read]
        tables = [self.take_unit(wait=False) for _ in range(6)]
        pq_free, y_ready = [], []
        act.wait(self.xh_read)
        for g in range(KT):
            pe.wait(*chan_ready, *u_ready[g])
            pq_ready = []
            for half in range(2):
                for pair in range(2):
                    b = self.take_bank()
                    for i in range(2):
                        s = slice((2 * pair + i) * P, (2 * pair + i + 1) * P)
                        mark = self.passes(self.psum[:, b, i * 2 * P:(i + 1) * 2 * P], self.U_hi[:, half, g, s],
                                           self.U_lo[:, half, g, s], self.chan_hi[:], self.chan_lo[:], True, True)
                    at = 4 * half + 2 * pair
                    m = self.split(self.psum[:, b, :], self.PQ_hi[:, at:at + 2, :].rearrange("p a n -> p (a n)"),
                                   self.PQ_lo[:, at:at + 2, :].rearrange("p a n -> p (a n)"), [mark], pq_free)
                    self.bank_free[b] = m
                    pq_ready.append(m)
            u_taken = mark
            if g == 1:
                self.gate_row(1, 0)
            b_odd, b_even = self.take_bank(), self.take_bank()
            for cls, (tiles, first, n, b, col) in enumerate(((4, 0, CH, b_odd, 0), (2, 4, CH // 2, b_even, 0),
                                                             (2, 6, CH // 2, b_even, CH // 2))):
                for t in range(tiles):
                    pe.wait(*pq_ready[(first + t) // 2], *tables[t if cls == 0 else 3 + cls].ready)
                    for cs in range(2):
                        if cls == 0:
                            r = [x[:, cs * CH:(cs + 1) * CH] for x in (tables[t].hi, tables[t].lo)]
                        else:
                            u = tables[3 + cls]
                            at = (2 * t + cs) * n
                            r = [x[:, at:at + n] for x in (u.hi, u.lo)]
                        l = [x[:, first + t, cs * P:(cs + 1) * P] for x in (self.PQ_hi, self.PQ_lo)]
                        mark = self.passes(self.psum[:, b, col:col + n], l[0], l[1], r[0], r[1],
                                           t == 0 and cs == 0, t == tiles - 1 and cs == 1)
                if cls == 0:
                    odd_done = mark
            pq_free = [mark]
            dst = lambda off, step: [x[:, :, g, off::step] for x in (self.U_hi, self.U_lo)]
            hi, lo = dst(1, 2)
            got = [self.split(self.psum[:, b_odd, :].rearrange("p (c n) -> p c n", c=2), hi, lo, [odd_done, u_taken])]
            evens = [(self.psum[:, b_even, i * 256:(i + 1) * 256].rearrange("p (c n) -> p c n", c=2), *dst(off, 4))
                     for i, off in ((0, 2), (1, 0))]
            act.wait(mark, u_taken)
            m_hi = [act.do(lambda e, src=src, hi=hi: e.copy(hi, src)) for src, hi, lo in evens]
            dve.wait(mark, u_taken, *m_hi)
            m_lo = [dve.do(lambda e, src=src, hi=hi, lo=lo: e.tensor_tensor(lo, src, hi.bitcast(F32), ALU.subtract))
                    for src, hi, lo in evens]
            got.append(m_hi + m_lo)
            self.bank_free[b_odd], self.bank_free[b_even] = got
            y_ready.append(got[0] + got[1])
        for u in tables:
            self.release(u, mark)
        self.a_read = self.rows_used = [mark]
        self.gate_used = self.gate_used_now()
        return y_ready

    def gate_used_now(self):
        return [(self.dve.stage, self.dve.count)] if self.dve.count else []

    def mixers(self, chunk_ready, before_chunk):
        pe, act, dve, pool, a = self.pe, self.act, self.dve, self.pool, self.a
        for q in (pe, act, dve, pool):
            q.begin("mixers")
        region = [self.a_read, *[m for r in self.h_ready for m in r], self.rows_used]
        for q in (act, dve, pool):
            q.wait(*self.a_read)
        meta_ready = []

        def meta_tokens():
            meta = self.load("meta", self.meta_raw[:], a["meta_tokens_2"], self.a_read)
            m = self.normalize(self.meta_raw[:], self.meta_hat[:], META, [meta], rms=True)
            pe.wait(m)
            b = self.take_bank()
            for k in range(KT):
                m = pe.do(lambda e: e.transpose(self.psum[:, b, k * META:(k + 1) * META],
                                                self.meta_hat[:, k * P:(k + 1) * P], self.ident[0:META, 0:META]))
            t = self.take_temp(dve)
            v = self.temp[t]
            dve.wait(m)
            g = self.columns("mix_norm_g_2", 0, KT).unsqueeze(2).to_broadcast([P, KT, META])
            vv = v[:, 0:KT * META].rearrange("p (k m) -> p k m", k=KT)
            m = dve.do(lambda e: e.tensor_tensor(vv, self.psum[:, b, 0:KT * META].rearrange("p (k m) -> p k m", k=KT),
                                                 g, ALU.mult))
            self.bank_free[b] = [m]
            meta_ready[:] = self.split(vv, self.U_meta_hi[:], self.U_meta_lo[:], [m])
            self.temp_free[t] = list(meta_ready)
            for buf in self.gated:
                pad = dve.do(lambda e: e.memset(buf[:, 0:14], 0.0))
            dve.wait(*region)
            pad = dve.do(lambda e: e.memset(self.cx[:, 0:3], 0.0))
            for q in (act, dve, pool):
                q.wait(pad, *meta_ready, *region)

        def before_mixers_chunk(c):
            if c == 1:
                meta_tokens()
            before_chunk(c)

        background, beside = [], []
        s_stage = [[self.semaphore(f"s_mix{i}"), 0] for i in range(4)]
        stage_free = [[], []]
        gated_m = [[], []]
        cx_m, cx_free, xc_m = [], [], {}
        dw_m, pool_m, gelu_m = [[], []], [], []
        self.work_free = []

        def place(dst, off):
            return lambda c: dst[:, off:off + META] if c < 0 else dst[:, off + META + c * CH:off + META + (c + 1) * CH]

        def evac(unit, c, b, mark):
            n = META if c < 0 else CH
            x = self.psum[:, b, 0:n]
            if unit < 2:
                act.wait(mark)
                m = act.do(lambda e: e.activation(place(self.gated[unit], 14)(c), x, ACT.Sigmoid))
                gated_m[unit].append(m)
            elif unit < 4:
                dst = place(self.gated[unit - 2], 14)(c)
                dve.wait(mark, *gated_m[unit - 2])
                m = dve.do(lambda e: e.tensor_tensor(dst, x, dst, ALU.mult))
                gated_m[unit - 2].append(m)
            elif unit < 8:
                act.wait(mark, *cx_free)
                m = act.do(lambda e: e.copy(place(self.cx, 3)(c), x))
                cx_m.append(m)
            else:
                act.wait(mark, *self.work_free)
                f = ACT.Copy if unit < 10 else ACT.Gelu_apprx_tanh
                m = act.do(lambda e: e.activation(place(self.work, 0)(c), x, f))
                work_m.append(m)
            self.bank_free[b] = [m]

        work_m = []

        sp = [self.softplus[:, i, :] for i in range(8)]
        rates = []

        def chain(emit):
            m = dve.do(emit)
            dve.wait(m)
            return m

        def softplus():
            lam = self.columns("rg_lambda_2", 0, 4)
            m = act.do(lambda e: e.activation(sp[0], lam, ACT.Abs))
            act.wait(m)
            m = act.do(lambda e: e.activation(sp[1], sp[0], ACT.Exp, scale=-1.0))
            dve.wait(m)

            chain(lambda e: e.tensor_scalar(sp[2], sp[1], 2.0, None, ALU.add))
            chain(lambda e: e.reciprocal(sp[2], sp[2]))
            chain(lambda e: e.tensor_tensor(sp[2], sp[2], sp[1], ALU.mult))
            chain(lambda e: e.tensor_tensor(sp[3], sp[2], sp[2], ALU.mult))
            chain(lambda e: e.memset(sp[4], 1.0 / 19))
            for n in (17, 15, 13, 11, 9, 7, 5, 3, 1):
                chain(lambda e: e.tensor_tensor(sp[4], sp[4], sp[3], ALU.mult))
                chain(lambda e, n=n: e.tensor_scalar(sp[4], sp[4], 1.0 / n, None, ALU.add))
            chain(lambda e: e.tensor_tensor(sp[4], sp[4], sp[2], ALU.mult))
            chain(lambda e: e.tensor_scalar(sp[5], lam, -1.0, 0.0, ALU.mult, ALU.max))
            chain(lambda e: e.scalar_tensor_tensor(sp[4], sp[4], 2.0, sp[5], ALU.mult, ALU.add))
            chain(lambda e: e.tensor_scalar(sp[5], sp[4], -RG_C, None, ALU.mult))
            c8 = chain(lambda e: e.tensor_scalar(sp[6], sp[4], RG_C, None, ALU.mult))
            rates.append(c8)

        def vector_taps():
            src, dst = self.gated[0], self.dw[0]

            def first():
                dve.wait(*gated_m[0])
                dw_m[0] = [dve.do(lambda e: e.tensor_scalar(dst[:, 0:T], src[:, 0:T], self.columns("convb_dw_w_2", 0),
                                                            self.columns("convb_dw_b_2", 0), ALU.mult, ALU.add))]
            background.append(first)
            for tap in range(1, CONV_K):
                def one(tap=tap):
                    dve.wait(*dw_m[0])
                    dw_m[0] = [dve.do(lambda e: e.scalar_tensor_tensor(
                        dst[:, 0:T], src[:, tap:tap + T], self.columns("convb_dw_w_2", 2 * tap), dst[:, 0:T],
                        ALU.mult, ALU.add))]
                background.append(one)

        def other_taps():
            src, dst = self.gated[1], self.dw[1]

            def first():
                act.wait(*gated_m[1])
                dw_m[1] = [act.do(lambda e: e.activation(dst[:, 0:T], src[:, 0:T], ACT.Identity,
                                                         bias=self.columns("convb_dw_b_2", 1),
                                                         scale=self.columns("convb_dw_w_2", 1)))]
            beside.append(first)
            for tap in range(1, CONV_K):
                def one(tap=tap):
                    last = dw_m[1]
                    dw_m[1] = []
                    for c in range(NCH):
                        s = slice(c * CH, (c + 1) * CH)
                        t = self.take_temp(act)
                        v = self.temp[t]
                        m = act.do(lambda e: e.activation(v[:], src[:, tap + c * CH:tap + (c + 1) * CH], ACT.Copy,
                                                          scale=self.columns("convb_dw_w_2", 2 * tap + 1)))
                        pool.wait(m, *last)
                        m = pool.do(lambda e: e.tensor_tensor(dst[:, s], dst[:, s], v[:], ALU.add))
                        self.temp_free[t] = [m]
                        dw_m[1].append(m)
                beside.append(one)

        def after_unit(unit):
            if unit == 3:
                vector_taps()
                other_taps()
                softplus()
            if 4 <= unit < 8:
                j = unit - 4
                dst = self.xc[j]
                dve.wait(*cx_m)
                m = dve.do(lambda e: e.tensor_scalar(dst[:], self.cx[:, 0:TM], self.columns("rg_conv_w_2", j),
                                                     self.columns("rg_conv_b_2", j), ALU.mult, ALU.add))
                for tap in range(1, RG_K):
                    dve.wait(m)
                    m = dve.do(lambda e, tap=tap: e.scalar_tensor_tensor(
                        dst[:], self.cx[:, tap:tap + TM], self.columns("rg_conv_w_2", 4 * tap + j), dst[:], ALU.mult, ALU.add))
                cx_free[:] = [m]
                cx_m.clear()
                xc_m[j] = [m]
            if unit >= 8:
                i = unit - 8 if unit < 10 else unit - 10
                dram = self.d_pool[i] if unit < 10 else self.d_gelu[i]
                pool.wait(*work_m)
                m = self.dma(pool, s_stage[0], dram, self.work[:])
                (pool_m if unit < 10 else gelu_m).append(m)
                self.work_free = [m]
                work_m.clear()
            for steps, n in ((background, 4), (beside, 3)):
                for _ in range(min(n, len(steps))):
                    steps.pop(0)()

        def extra_at(first):
            def extra(i, W_hi, W_lo):
                pe.wait(*meta_ready)
                b = self.take_bank()
                for k in range(KT):
                    mark = self.passes(self.psum[:, b, 0:META], W_hi[:, k, :], W_lo[:, k, :], self.U_meta_hi[:, k, :],
                                       self.U_meta_lo[:, k, :], k == 0, k == KT - 1)
                evac(first + i, -1, b, mark)
                after_unit(first + i)
                return mark
            return extra

        self.up_group(4, chunk_ready, evac, before_mixers_chunk, chunk_major=True, extra=extra_at(0))
        for unit in range(4, 14):
            self.up_group(1, chunk_ready, lambda i, c, b, mark, unit=unit: evac(unit, c, b, mark), extra=extra_at(unit))
        u_done = (pe.stage, pe.count)
        while background or beside:
            for steps in (background, beside):
                if steps:
                    steps.pop(0)()
        dw_ready = dw_m[0] + dw_m[1]
        Yslot = lambda k, c: (self.U_hi[:, c, k, :], self.U_lo[:, c, k, :])
        unit_small = self.take_unit()
        unit_rg = self.take_unit()

        y_ready = {}
        gated_free = [*dw_ready, *gated_m[0], *gated_m[1]]
        L = TM

        pool_in = []
        for i, (tile, free) in enumerate(((self.cx[:, 0:TM], cx_free), (self.work[:], self.work_free))):
            pool.wait(*free, *pool_m)
            pool_in.append((tile, self.dma(pool, s_stage[2 + i], tile, self.d_pool[i])))

        pooled = {}

        def pooling(i):
            nonlocal gated_free
            x_t, loaded = pool_in[i]
            s_a, s_b = self.gated[0], self.gated[1]
            dve.wait(loaded, *gated_free)
            m = dve.do(lambda e: e.tensor_tensor(s_a[:, 1:L], x_t[:, 1:L], x_t[:, 0:L - 1], ALU.add))
            dve.wait(m)
            if i == 0:
                m = dve.do(lambda e: e.tensor_tensor(s_b[64:P, 3:L], s_a[64:P, 3:L], s_a[64:P, 1:L - 2], ALU.add))
                parts = ((0, s_a, 2), (64, s_b, 4))
            else:
                m = dve.do(lambda e: e.tensor_tensor(s_b[:, 3:L], s_a[:, 3:L], s_a[:, 1:L - 2], ALU.add))
                dve.wait(m)
                m = dve.do(lambda e: e.tensor_tensor(s_a[:, 7:L], s_b[:, 7:L], s_b[:, 3:L - 4], ALU.add))
                dve.wait(m)
                m = dve.do(lambda e: e.tensor_tensor(s_b[64:P, 15:L], s_a[64:P, 15:L], s_a[64:P, 7:L - 8], ALU.add))
                parts = ((0, s_a, 8), (64, s_b, 16))
            dve.wait(m)
            for p0, src, w in parts:
                m = dve.do(lambda e, p0=p0, src=src, w=w: e.scalar_tensor_tensor(
                    src[p0:p0 + 64, META:TM], src[p0:p0 + 64, META:TM], 1.0 / w, x_t[p0:p0 + 64, META:TM],
                    ALU.mult, ALU.subtract))
            dve.wait(m)
            m = dve.do(lambda e: e.tensor_copy(s_a[64:P, META:TM], s_b[64:P, META:TM]))
            if i == 0:
                cx_free[:] = [m]
            else:
                self.work_free = [m]
            for c in range(NCH):
                hi, lo = Yslot(i, c)
                gated_free = pooled[(i, c)] = self.split(s_a[:, META + c * CH:META + (c + 1) * CH], hi, lo, [m], [u_done])

        def group_products(i):
            for c in range(NCH):
                hi, lo = Yslot(i, c)
                b = self.take_bank()
                pe.wait(*pooled[(i, c)])
                mark = self.passes(self.psum[:, b, :], unit_small.hi[:, i * P:(i + 1) * P],
                                   unit_small.lo[:, i * P:(i + 1) * P], hi, lo, True, True)
                t = self.take_temp(act)
                act.wait(mark)
                mv = act.do(lambda e, t=t, b=b, i=i: e.activation(self.temp[t][:], self.psum[:, b, :], ACT.Copy,
                                                                  scale=self.columns("pool_scale_2", i)))
                self.bank_free[b] = [mv]
                got2 = self.split(self.temp[t][:], hi, lo, [mv, mark])
                self.temp_free[t] = got2
                y_ready[(i, c)] = got2
        pe.wait(*dw_ready)
        token_major = []
        for pair in range(TPC):
            b = self.take_bank()
            for i in range(2):
                for k in range(2):
                    s = slice((2 * pair + i) * P, (2 * pair + i + 1) * P)
                    m = pe.do(lambda e: e.transpose(self.psum[:, b, (2 * i + k) * P:(2 * i + k + 1) * P],
                                                    self.dw[k][:, s], self.ident[:]))
            tiles = [self.psum[:, b, 2 * i * P:(2 * i + 2) * P] for i in range(2)]
            token_major.append((b, tiles, [self.moments(x, P, 2 * P, [m]) for x in tiles]))
        back = []
        for pair, (b, tiles, moments) in enumerate(token_major):
            norms = [self.scale_and_bias(*x) for x in moments]
            t = self.take_temp(act)
            v = self.temp[t]
            for i, (x, (sc, bi, got)) in enumerate(zip(tiles, norms)):
                act.wait(*norms[1][2])
                m = act.do(lambda e: e.activation(v[:, 2 * i * P:(2 * i + 2) * P], x, ACT.Identity, bias=bi, scale=sc))
            self.bank_free[b] = [m]
            if pair % 2 == 0:
                back.append([self.take_bank(), self.take_bank()])
            pe.wait(m)
            for i in range(2):
                for k in range(2):
                    at = (2 * (pair % 2) + i) * P
                    m = pe.do(lambda e: e.transpose(self.psum[:, back[-1][k], at:at + P],
                                                    v[:, (2 * i + k) * P:(2 * i + k + 1) * P], self.ident[:]))
            self.temp_free[t] = [m]
        turned = m
        pooling(0)
        pooling(1)
        group_products(0)
        z = []
        for c in range(NCH):
            for k in range(2):
                t = self.take_temp(act)
                v = self.temp[t]
                act.wait(turned)
                m = act.do(lambda e: e.activation(v[:], self.psum[:, back[c][k], :], ACT.Silu,
                                                  bias=self.columns("convb_ln_b_2", k),
                                                  scale=self.columns("convb_ln_g_2", k)))
                self.bank_free[back[c][k]] = [m]
                hi, lo = Yslot(2 + k, c)
                got = self.split(v[:], hi, lo, [m], [u_done])
                self.temp_free[t] = got
                z += got
        group_products(1)
        pe.wait(*z)
        for c in range(NCH):
            outs = []
            for j in range(2):
                b = self.take_bank()
                for k in range(2):
                    s = slice(256 + k * 256 + j * P, 256 + k * 256 + (j + 1) * P)
                    hi, lo = Yslot(2 + k, c)
                    mark = self.passes(self.psum[:, b, :], unit_small.hi[:, s], unit_small.lo[:, s], hi, lo, k == 0, k == 1)
                outs.append(b)
            for j, b in enumerate(outs):
                hi, lo = Yslot(2 + j, c)
                got = self.split(self.psum[:, b, :], hi, lo, [mark])
                self.bank_free[b] = got
                y_ready[(2 + j, c)] = got
        self.release(unit_small, mark)
        work = [(self.gated[0][:, 0:TM], self.gated[1][:, 0:TM], self.cx[:, 0:TM]),
                (self.work[:], self.dw[0][:], self.dw[1][:])]
        work_free = [[gated_free, cx_free], [self.work_free, turned]]
        parts = ((-1, 0, META), (0, META, CH), (1, META + CH, CH))
        rg_state = {}
        ends = []

        def rg_gates(j):
            xc = self.xc[j]
            w_r, w_i, _ = work[j % 2]
            free = work_free[j % 2]
            slot = lambda c: Yslot(4 + j, c) if c >= 0 else (self.U_meta_hi[:, 4 + j, :], self.U_meta_lo[:, 4 + j, :])
            ready = [self.split(xc[:, at:at + n], *slot(c), xc_m[j], [u_done]) for c, at, n in parts]
            sig = []
            for which, dst, bias in ((0, w_r, "rg_b_a_2"), (1, w_i, "rg_b_x_2")):
                for (c, at, n), got in zip(parts, ready):
                    hi, lo = slot(c)
                    pe.wait(*got)
                    b = self.take_bank()
                    s = slice(which * 512 + j * P, which * 512 + (j + 1) * P)
                    mark = self.passes(self.psum[:, b, 0:n], unit_rg.hi[:, s], unit_rg.lo[:, s], hi, lo, True, True)
                    act.wait(mark, *free)
                    m = act.do(lambda e: e.activation(dst[:, at:at + n], self.psum[:, b, 0:n], ACT.Sigmoid,
                                                      bias=self.columns(bias, j)))
                    self.bank_free[b] = [m]
                    sig.append(m)
            dve.wait(*sig)
            m_ix = dve.do(lambda e: e.tensor_tensor(xc[:], w_i, xc[:], ALU.mult))
            rg_state[j] = (mark, m_ix, sig)
            if j == 3:
                self.release(unit_rg, mark)

        def rg_scan(j):
            read, m_ix, sig = rg_state[j]
            xc = self.xc[j]
            w_r, w_t, w_a = work[j % 2]
            act.wait(*sig, m_ix, *rates, *work_free[j % 2])
            m_a = act.do(lambda e: e.activation(w_a, w_r, ACT.Exp, scale=sp[5][:, j:j + 1]))
            m_t = act.do(lambda e: e.activation(w_t, w_r, ACT.Tanh, scale=sp[6][:, j:j + 1]))
            dve.wait(m_a, m_t)
            m = chain(lambda e: e.tensor_tensor(w_r, w_a, w_a, ALU.mult))
            m = chain(lambda e: e.scalar_tensor_tensor(w_r, w_r, 1.0, w_t, ALU.add, ALU.mult))
            pool.wait(m, *gelu_m)
            gelu = self.dma(pool, s_stage[1], w_t, self.d_gelu[j])
            act.wait(m)
            m = act.do(lambda e: e.activation(w_r, w_r, ACT.Sqrt))
            dve.wait(m, m_ix)
            m = chain(lambda e: e.tensor_tensor(xc[:], xc[:], w_r, ALU.mult))
            m = chain(lambda e: e.tensor_tensor_scan(w_r, w_a, xc[:], 0.0, ALU.mult, ALU.add))
            dve.wait(gelu)
            m = dve.do(lambda e: e.tensor_tensor(w_t, w_r, w_t, ALU.mult))
            for c in range(NCH):
                hi, lo = Yslot(4 + j, c)
                at = META + c * CH
                y_ready[(4 + j, c)] = self.split(w_t[:, at:at + CH], hi, lo, [m, read])
            work_free[j % 2] = [y_ready[(4 + j, c)] for c in range(NCH)]
            ends[:] = [m, read, *work_free[0], *work_free[1]]

        turns = {0: [(rg_gates, 0), (rg_gates, 1)], 1: [(rg_scan, 0)], 2: [(rg_gates, 2)], 3: [(rg_scan, 1)],
                 4: [(rg_gates, 3)], 5: [(rg_scan, 2)], 6: [(rg_scan, 3)]}

        def rg_step(tt):
            for step, j in turns[tt]:
                step(j)
            self.a_read = list(ends)
        return y_ready, rg_step

    def finish(self):
        rows = [self.load("final_g", self.row_g[:], self.a["final_norm_g_2"].partition_broadcast(P), *self.rows_used,
                          self.a_read)]
        out = self.out[0].rearrange("(t p) d -> p t d", p=P)
        stores = []

        def after_tile(tt):
            h = self.H[:, tt, :]
            m = self.normalize(h, h, P, self.h_ready[tt], rms=True)
            self.dve.wait(m, *rows)
            m = self.dve.do(lambda e: e.tensor_tensor(h, h, self.row_g[:], ALU.mult))
            self.pool.wait(m)
            stores.append(self.dma(self.pool, [self.semaphore(f"s_out{tt}"), 0], out[:, tt, :], h))
        return after_tile, stores

    def build(self):
        a = self.a
        modulation = lambda layer, which: (lambda k: self.mod[:, layer, 24 * which + 8 + k:24 * which + 9 + k],
                                           lambda k: self.mod[:, layer, 24 * which + k:24 * which + k + 1])
        gain = lambda name: (lambda k: self.columns(name, k), lambda k: self.eps[:, 2:3])
        self.allocate()
        self.weights_begin(self.plan_units())
        xh, xhc = self.start()
        self.project_attention(xh, xhc)
        self.gate_row(0, 0)
        conv_done, o_marks = self.attention()
        o_ready = self.attention_out(conv_done, o_marks)
        for q in (self.pe, self.act, self.dve, self.pool):
            q.begin("mix_out")
        self.a_read = [m for ready in o_ready for m in ready]
        after, make, ready, _ = self.boundary((a["ln_g"][0, 0], a["ln_b"][0, 0]), False, *modulation(0, 1), from_u=True)
        self.down_block(self.u_lhs(4), lambda j, tt: o_ready[(tt // TPC) * HEADS + j], 1.0, after)
        self.a_read = []
        self.gate_used = self.gate_used_now()
        late = {}

        def then_fourier(tt):
            if tt == 0:
                self.ada_fill(0)
                late["b"] = self.boundary((a["ln_g"][0, 1], a["ln_b"][0, 1]), False, None, None, fourier=True)
            late["b"][0](tt)

        self.mlp("mlp0", ready, make, self.ada_fill, then_fourier, ALPHA, gate=(0, 1), tile_first=True)
        self.gate_used = self.gate_used_now()
        y_ready = self.fourier(late["b"][3])
        self.down_block(self.u_lhs(0), lambda j, tt: y_ready[j], ALPHA)
        after, make, ready, _ = self.boundary((a["ln_g"][1, 0], a["ln_b"][1, 0]), False, *modulation(1, 1), from_u=True)
        self.down_block(self.u_lhs(4), lambda j, tt: y_ready[4 + j], 1.0, after)
        self.gate_used = self.gate_used_now()

        def then_mixers(tt):
            if tt == 0:
                late["b"] = self.boundary((a["ln_g"][1, 1], a["ln_b"][1, 1]), True, *gain("mix_norm_g_2"))
            late["b"][0](tt)
        self.mlp("mlp1", ready, make, None, then_mixers, ALPHA, gate=(1, 1))
        _, make, ready, _ = late["b"]
        y_ready, rg_step = self.mixers(ready, make)
        self.down_block(self.u_lhs(0), lambda j, tt: y_ready[(j, tt // TPC)], 1.0, beside=rg_step)
        after, make, ready, _ = self.boundary(None, True, *gain("mlp_norm_g_2"), from_u=True)
        self.down_block(self.u_lhs(4), lambda j, tt: y_ready[(4 + j, tt // TPC)], 1.0, after)
        after_last, stores = self.finish()
        self.mlp("mlp2", ready, make, None, after_last)
        self.pool.wait(*stores)
        self.sp.wait(*stores)

    def run(self):
        nc = self.nc
        block = self.stack.enter_context(nc.Block())

        @block.sync
        def _(e):
            self.sp.run(e)

        @block.scalar
        def _(e):
            self.act.run(e)

        @block.vector
        def _(e):
            self.dve.run(e)

        @block.gpsimd
        def _(e):
            self.pool.run(e)

        @block.tensor
        def _(e):
            self.pe.run(e)


def build_program(nc, arrays, out):
    program = Program(nc, arrays, out)
    with program.stack:
        program.build()
        program.run()


def rope_tables():
    d = np.arange(P) % QK
    inv = (np.float32(10000.0) ** (-np.arange(16, dtype=np.float32) / np.float32(16))).astype(np.float32)
    tok = np.arange(T)
    pos = np.where((d < 32)[:, None], tok[None, :] // 64, tok[None, :] % 64).astype(np.float32)
    ang = (pos * inv[d % 16][:, None]).astype(np.float32).astype(np.float64)
    sign = np.where(d % 32 < 16, -1.0, 1.0)[:, None]
    return np.cos(ang).astype(np.float32), (np.sin(ang) * sign).astype(np.float32)


def dft_tables():
    out = np.zeros((6, P, UNIT), np.float32)
    n = np.arange(P)[:, None]
    for t in range(4):
        ang = 2 * np.pi * (((n + P * t) * (2 * np.arange(CH) + 1)[None, :]) % T) / T
        out[t] = np.concatenate([np.cos(ang), -np.sin(ang)], 1)
    for c, off in ((4, 2), (5, 0)):
        parts = []
        for t in range(2):
            ang = 2 * np.pi * (((n + P * t) * (4 * np.arange(CH // 2) + off)[None, :]) % T) / T
            parts += [np.cos(ang), -np.sin(ang)]
        out[c] = np.concatenate(parts, 1)
    ang = 2 * np.pi * ((n * np.arange(P)[None, :]) % P) / P
    chan = np.concatenate([np.cos(ang), np.sin(ang)], 1) / math.sqrt(T * P)
    return out, chan.astype(np.float32)


_WHOLE = ["x", "ctx", "ada_w", "ln_g", "ln_b", "mlp_w1", "mlp_w2", "w_in", "lambda_qk", "w_out_mix", "w_out_fourier",
          "meta_tokens_2", "w_in_2", "pool_w_2", "convb_pw_w_2", "rg_w_a_2", "rg_w_x_2", "w_out_2", "w_up_2",
          "w_down_2", "final_norm_g_2"]


def kernel(**inputs):
    import numpy as _np
    import concourse.bacc as _bacc
    from concourse import mybir as _mybir
    from concourse.bass_utils import run_bass_kernel_spmd as _run

    nc = _bacc.Bacc("TRN2", target_bir_lowering=False, num_devices=1)
    host = {name: _np.ascontiguousarray(inputs[name]) for name in _WHOLE}
    host["vectors"] = _np.concatenate([_np.ascontiguousarray(inputs[name]).reshape(rows, P) for name, rows in VECTORS])
    host["rope_cos"], host["rope_sin"] = rope_tables()
    host["dft"], host["dft_chan"] = dft_tables()
    arrays, aps = {}, {}
    for name, a in host.items():
        arrays[f"in_{name}_dram"] = a
        aps[name] = nc.dram_tensor(f"in_{name}_dram", a.shape, _mybir.dt.from_np(a.dtype), kind="ExternalInput").ap()
    out = nc.dram_tensor("out_0_dram", (1, T, D), _mybir.dt.float32, kind="ExternalOutput").ap()
    build_program(nc, aps, out)
    r = _run(nc, [arrays], core_ids=[0])
    return r.results[0]["out_0_dram"]
```
